# Optimizing a Trainium2 kernel written in Bass

```python
import math
import jax
import jax.numpy as jnp
from jax import lax
import numpy as np

D_MODEL = 2048
BATCH = 1
SEQ = 128
DEPTH = 1
DEC_BATCH = 1
DEC_SEQ = 256
PAST_LEN = 128

GRID_W = 64
EPS = 1e-6
CHUNK = 64
SHORT_W = 3
N_BRANCH = 3
HY_WIDTH = 1024
HY_ORDER = 2
HY_EMB = 33
HY_BANDS = (HY_EMB - 1) // 2
HY_FFN = 64
HY_DECAY_TARGET = 1e-2
HY_FAST_PCT = 0.3
HY_SLOW_PCT = 1.5
GLA_HEADS = 4
GLA_DK = 128
GLA_DV = 256
GLA_RANK = 16
GLA_NORMALIZER = 16.0
GLA_QK = GLA_HEADS * GLA_DK
GLA_VW = GLA_HEADS * GLA_DV
ML_HEADS = 4
ML_DH = 256
ML_W = ML_HEADS * ML_DH
BRANCH_W = HY_WIDTH
PEER_HEADS = 8
PEER_NKEYS = 128
PEER_EXPERTS = PEER_NKEYS * PEER_NKEYS
PEER_DKEY = 256
PEER_TOPK = 16
PEER_BLOCK = 128
IN_SPLITS = (HY_WIDTH, HY_WIDTH, HY_WIDTH,
             GLA_QK, GLA_QK, GLA_VW, GLA_VW, GLA_RANK, GLA_RANK,
             ML_W, ML_W, ML_W, ML_W, 2 * ML_HEADS, 2 * ML_HEADS,
             D_MODEL, D_MODEL, D_MODEL)
IN_COLS = sum(IN_SPLITS)

kernel_name = 'hybrid_flow_trunk_step'

def _f32(a):
    return a.astype(jnp.float32)

def rmsnorm(x, g):
    xf = _f32(x)
    y = xf * lax.rsqrt(jnp.mean(xf * xf, axis=-1, keepdims=True) + EPS)
    return (y * _f32(g)).astype(x.dtype)

def split_cols(z):
    parts, start = [], 0
    for width in IN_SPLITS:
        parts.append(z[..., start:start + width])
        start += width
    return parts

def short_conv(x, w, grid):
    b, l, ch = x.shape
    xr = x.reshape(b * (l // GRID_W), GRID_W, ch) if grid else x
    xp = jnp.pad(xr, ((0, 0), (1, 1), (0, 0)))
    y = xp[:, :-2] * w[0] + xp[:, 1:-1] * w[1] + xp[:, 2:] * w[2]
    return y.reshape(b, l, ch)

def to_heads(a, n_heads):
    b, l, _ = a.shape
    return a.reshape(b, l, n_heads, -1).transpose(0, 2, 1, 3)

def from_heads_norm(o, g):
    o = o * lax.rsqrt(jnp.mean(o * o, axis=-1, keepdims=True) + EPS) * _f32(g)
    b, h, l, d = o.shape
    return o.transpose(0, 2, 1, 3).reshape(b, l, h * d)

def to_chunks(a):
    b, h, l = a.shape[:3]
    a = a.reshape((b, h, l // CHUNK, CHUNK) + a.shape[3:])
    return jnp.moveaxis(a, 2, 0)

def from_chunks(a):
    a = jnp.moveaxis(a, 0, 2)
    return a.reshape(a.shape[:2] + (-1,) + a.shape[4:])

def flip_t(a):
    return jnp.flip(a, axis=2)

def hyena_filter_spectrum(length, w1, b1, w2, b2, w3, freq):
    t = jnp.arange(length, dtype=jnp.float32)
    t_norm = t / (length - 1)
    bands = jnp.linspace(1e-4, HY_BANDS - 1, HY_BANDS, dtype=jnp.float32)
    ang = (2.0 * math.pi / length) * t[:, None] * bands[None, :]
    z = jnp.concatenate([t_norm[:, None], jnp.cos(ang), -jnp.sin(ang)], axis=-1)
    hid = jnp.sin(_f32(freq[0]) * (z @ _f32(w1) + _f32(b1)))
    hid = jnp.sin(_f32(freq[1]) * (hid @ _f32(w2) + _f32(b2)))
    filt = (hid @ _f32(w3)).reshape(length, HY_ORDER, 2, HY_WIDTH)
    max_decay = math.log(HY_DECAY_TARGET) / HY_FAST_PCT
    min_decay = math.log(HY_DECAY_TARGET) / HY_SLOW_PCT
    deltas = jnp.abs(jnp.linspace(min_decay, max_decay, HY_WIDTH, dtype=jnp.float32))
    filt = filt * jnp.exp(-t_norm[:, None] * deltas[None, :])[:, None, None, :]
    fwd, bwd = filt[:, :, 0], filt[:, :, 1]
    circ = jnp.concatenate([fwd, jnp.zeros((1, HY_ORDER, HY_WIDTH), jnp.float32), bwd[:0:-1]], axis=0)
    return jnp.fft.rfft(circ, axis=0)

def long_conv(u, spec, bias):
    l = u.shape[1]
    uf = jnp.fft.rfft(u, n=2 * l, axis=1)
    y = jnp.fft.irfft(uf * spec[None], n=2 * l, axis=1)[:, :l]
    return y + u * bias

def hyena_operator(x1, x2, v, spec, bias):
    z = _f32(x1) * long_conv(_f32(v), spec[:, 0], _f32(bias[0]))
    return _f32(x2) * long_conv(z, spec[:, 1], _f32(bias[1]))

def gla_scan(q, k, v, lg, s0):
    tri = jnp.tril(jnp.ones((CHUNK, CHUNK), bool))

    def step(s, inp):
        qc, kc, vc, gc = inp
        bc = jnp.cumsum(gc, axis=2)
        inter = jnp.einsum('bhtd,bhdv->bhtv', qc * jnp.exp(bc), s)
        decay = jnp.exp(jnp.where(tri[:, :, None], bc[:, :, :, None, :] - bc[:, :, None, :, :], -jnp.inf))
        att = jnp.einsum('bhtd,bhsd,bhtsd->bhts', qc, kc, decay)
        o = inter + jnp.einsum('bhts,bhsv->bhtv', att, vc)
        b_end = bc[:, :, -1]
        s_new = jnp.exp(b_end)[..., None] * s + jnp.einsum(
            'bhsd,bhsv->bhdv', kc * jnp.exp(b_end[:, :, None] - bc), vc)
        return s_new, o

    s_fin, o = lax.scan(step, s0, (to_chunks(q), to_chunks(k), to_chunks(v), to_chunks(lg)))
    return from_chunks(o), s_fin

def mlstm_scan(q, k, v, li, lf, state0):
    tri = jnp.tril(jnp.ones((CHUNK, CHUNK), bool))

    def step(carry, inp):
        cm, nv, m = carry
        qc, kc, vc, ic, fc = inp
        b = jnp.cumsum(fc, axis=-1)
        dmat = jnp.where(tri, b[..., :, None] - b[..., None, :] + ic[..., None, :], -jnp.inf)
        m_t = jnp.maximum(b + m[..., None], jnp.max(dmat, axis=-1))
        w_inter = jnp.exp(b + m[..., None] - m_t)
        sc = jnp.einsum('bhtd,bhsd->bhts', qc, kc) * jnp.exp(dmat - m_t[..., None])
        num = w_inter[..., None] * jnp.einsum('bhtd,bhdv->bhtv', qc, cm) + jnp.einsum('bhts,bhsv->bhtv', sc, vc)
        den = w_inter * jnp.einsum('bhtd,bhd->bht', qc, nv) + jnp.sum(sc, axis=-1)
        hc = num / jnp.maximum(jnp.abs(den), jnp.exp(-m_t))[..., None]
        g = b[..., -1:] - b + ic
        m_new = jnp.maximum(b[..., -1] + m, jnp.max(g, axis=-1))
        w_c = jnp.exp(b[..., -1] + m - m_new)
        w_k = jnp.exp(g - m_new[..., None])
        c_new = w_c[..., None, None] * cm + jnp.einsum('bhs,bhsd,bhsv->bhdv', w_k, kc, vc)
        n_new = w_c[..., None] * nv + jnp.einsum('bhs,bhsd->bhd', w_k, kc)
        return (c_new, n_new, m_new), hc

    carry, h = lax.scan(step, state0, (to_chunks(q), to_chunks(k), to_chunks(v), to_chunks(li), to_chunks(lf)))
    return from_chunks(h), carry

def token_mixers(h, w_in, b_in, hy_conv, hy_spec, hy_bias, gla_a2_w, gla_a2_b, gla_norm_g,
                 ml_conv, ml_gate_b, ml_norm_g, w_branch, w_out, gla_init, ml_init, grid):
    b, l, _ = h.shape
    dt = h.dtype
    (hx1, hx2, hv, gq, gk, gv, gr, glr_f, glr_b, mq, mk, mv, mo, mi, mf, ga, gb, gc) = split_cols(h @ w_in + b_in)
    y_hy = hyena_operator(short_conv(hx1, hy_conv[0], grid), short_conv(hx2, hy_conv[1], grid),
                          short_conv(hv, hy_conv[2], grid), hy_spec, hy_bias).astype(dt)
    q = to_heads(_f32(gq), GLA_HEADS) * GLA_DK ** -0.5
    k = to_heads(_f32(gk), GLA_HEADS)
    v = to_heads(_f32(gv), GLA_HEADS)
    lg_f = to_heads(jax.nn.log_sigmoid(_f32(glr_f @ gla_a2_w[0] + gla_a2_b[0])) / GLA_NORMALIZER, GLA_HEADS)
    lg_b = to_heads(jax.nn.log_sigmoid(_f32(glr_b @ gla_a2_w[1] + gla_a2_b[1])) / GLA_NORMALIZER, GLA_HEADS)
    o_f, s_f = gla_scan(q, k, v, lg_f, gla_init[0])
    o_b, s_b = gla_scan(flip_t(q), flip_t(k), flip_t(v), flip_t(lg_b), gla_init[1])
    y_gla = from_heads_norm(o_f + flip_t(o_b), gla_norm_g).astype(dt) * jax.nn.silu(gr)
    q = to_heads(_f32(short_conv(mq, ml_conv[0], grid)), ML_HEADS)
    k = to_heads(_f32(short_conv(mk, ml_conv[1], grid)), ML_HEADS) * ML_DH ** -0.5
    v = to_heads(_f32(mv), ML_HEADS)
    li = (_f32(mi).reshape(b, l, 2, ML_HEADS) + _f32(ml_gate_b[:, 0])).transpose(2, 0, 3, 1)
    lf = jax.nn.log_sigmoid(_f32(mf).reshape(b, l, 2, ML_HEADS) + _f32(ml_gate_b[:, 1])).transpose(2, 0, 3, 1)
    h_f, st_f = mlstm_scan(q, k, v, li[0], lf[0], ml_init[0])
    h_b, st_b = mlstm_scan(flip_t(q), flip_t(k), flip_t(v), flip_t(li[1]), flip_t(lf[1]), ml_init[1])
    y_ml = from_heads_norm(h_f + flip_t(h_b), ml_norm_g).astype(dt) * jax.nn.sigmoid(mo)
    merged = (jax.nn.sigmoid(ga) * (y_hy @ w_branch[0])
              + jax.nn.sigmoid(gb) * (y_gla @ w_branch[1])
              + jax.nn.sigmoid(gc) * (y_ml @ w_branch[2]))
    return merged @ w_out, (s_f, s_b), (st_f, st_b)

def peer(h, wq, keys, u_tab, v_tab):
    b, l, d = h.shape

    def block(x):
        q = _f32(x @ wq).reshape(PEER_BLOCK, PEER_HEADS, 2, PEER_DKEY // 2)
        s = jnp.einsum('thpd,hpkd->thpk', q, _f32(keys))
        sv, si = lax.top_k(s, PEER_TOPK)
        cand = (sv[:, :, 0, :, None] + sv[:, :, 1, None, :]).reshape(PEER_BLOCK, PEER_HEADS, PEER_TOPK * PEER_TOPK)
        best, bi = lax.top_k(cand, PEER_TOPK)
        i1 = jnp.take_along_axis(si[:, :, 0], bi // PEER_TOPK, axis=-1)
        i2 = jnp.take_along_axis(si[:, :, 1], bi % PEER_TOPK, axis=-1)
        idx = i1 * PEER_NKEYS + i2
        g = jax.nn.softmax(best, axis=-1).astype(x.dtype)
        act = jnp.einsum('td,thkd->thk', x, u_tab[idx])
        return jnp.einsum('thk,thkd->td', g * jax.nn.gelu(act), v_tab[idx])

    return lax.map(block, h.reshape(-1, PEER_BLOCK, d)).reshape(b, l, d)

def setup_inputs(seed: int = 0) -> dict:
    key = jax.random.key(seed)
    ks = list(jax.random.split(key, 48))

    def nrm(i, shape, scale):
        return scale * jax.random.normal(ks[i], shape, jnp.float32)

    ml_gate_b = jnp.concatenate([
        nrm(30, (DEPTH, 2, 1, ML_HEADS), 0.1),
        jnp.linspace(3.0, 6.0, ML_HEADS, dtype=jnp.float32) + nrm(31, (DEPTH, 2, 1, ML_HEADS), 0.1)], axis=2)
    return {
        'x_prompt': nrm(0, (BATCH, SEQ, D_MODEL), 1.0),
        'x_sample': nrm(1, (DEC_BATCH, DEC_SEQ, D_MODEL), 1.0),
        'c': nrm(2, (DEC_BATCH, D_MODEL), 1.0),
        'state_gla': nrm(3, (DEC_BATCH, DEPTH, 2, GLA_HEADS, GLA_DK, GLA_DV), 0.3),
        'state_mlstm_C': nrm(4, (DEC_BATCH, DEPTH, 2, ML_HEADS, ML_DH, ML_DH), 0.3),
        'state_mlstm_n': jnp.abs(nrm(5, (DEC_BATCH, DEPTH, 2, ML_HEADS, ML_DH), 0.5)),
        'state_mlstm_m': nrm(6, (DEC_BATCH, DEPTH, 2, ML_HEADS), 0.5),
        'c_ctx': nrm(7, (D_MODEL,), 1.0),
        'mod_w': nrm(8, (DEPTH, D_MODEL, 6 * D_MODEL), 0.5 * D_MODEL ** -0.5),
        'mod_b': nrm(9, (DEPTH, 6 * D_MODEL), 0.01),
        'norm1_g': 1.0 + nrm(10, (DEPTH, D_MODEL), 0.02),
        'norm2_g': 1.0 + nrm(11, (DEPTH, D_MODEL), 0.02),
        'final_g': 1.0 + nrm(12, (D_MODEL,), 0.02),
        'w_in': nrm(13, (DEPTH, D_MODEL, IN_COLS), D_MODEL ** -0.5),
        'b_in': nrm(14, (DEPTH, IN_COLS), 0.01),
        'hy_conv': nrm(15, (DEPTH, 3, SHORT_W, HY_WIDTH), SHORT_W ** -0.5),
        'hy_w1': nrm(16, (DEPTH, HY_EMB, HY_FFN), HY_EMB ** -0.5),
        'hy_b1': nrm(17, (DEPTH, HY_FFN), 0.1),
        'hy_w2': nrm(18, (DEPTH, HY_FFN, HY_FFN), HY_FFN ** -0.5),
        'hy_b2': nrm(19, (DEPTH, HY_FFN), 0.1),
        'hy_w3': nrm(20, (DEPTH, HY_FFN, HY_ORDER * 2 * HY_WIDTH), 0.05 * HY_FFN ** -0.5),
        'hy_freq': 1.0 + nrm(21, (DEPTH, 2, HY_FFN), 0.02),
        'hy_bias': nrm(22, (DEPTH, HY_ORDER, HY_WIDTH), 0.1),
        'gla_a2_w': nrm(23, (DEPTH, 2, GLA_RANK, GLA_QK), GLA_RANK ** -0.5),
        'gla_a2_b': nrm(24, (DEPTH, 2, GLA_QK), 0.1),
        'gla_norm_g': 1.0 + nrm(25, (DEPTH, GLA_DV), 0.02),
        'ml_conv': nrm(26, (DEPTH, 2, SHORT_W, ML_W), SHORT_W ** -0.5),
        'ml_gate_b': ml_gate_b,
        'ml_norm_g': 1.0 + nrm(27, (DEPTH, ML_DH), 0.02),
        'w_branch': nrm(28, (DEPTH, N_BRANCH, BRANCH_W, D_MODEL), BRANCH_W ** -0.5),
        'w_out': nrm(29, (DEPTH, D_MODEL, D_MODEL), D_MODEL ** -0.5),
        'peer_wq': nrm(32, (DEPTH, D_MODEL, PEER_HEADS * PEER_DKEY), D_MODEL ** -0.5),
        'peer_keys': nrm(33, (DEPTH, PEER_HEADS, 2, PEER_NKEYS, PEER_DKEY // 2), (PEER_DKEY // 2) ** -0.5),
        'peer_u': nrm(34, (DEPTH, PEER_EXPERTS, D_MODEL), D_MODEL ** -0.5),
        'peer_v': nrm(35, (DEPTH, PEER_EXPERTS, D_MODEL), PEER_HEADS ** -0.5),
    }

def reference(x_prompt, x_sample, c, state_gla, state_mlstm_C, state_mlstm_n, state_mlstm_m, c_ctx,
              mod_w, mod_b, norm1_g, norm2_g, final_g, w_in, b_in, hy_conv, hy_w1, hy_b1, hy_w2, hy_b2,
              hy_w3, hy_freq, hy_bias, gla_a2_w, gla_a2_b, gla_norm_g, ml_conv, ml_gate_b, ml_norm_g,
              w_branch, w_out, peer_wq, peer_keys, peer_u, peer_v):

    def run_layer(x, mod, l, gla_init, ml_init, grid):
        sh1, sc1, gt1, sh2, sc2, gt2 = jnp.split(mod[:, None, :], 6, axis=-1)
        h = rmsnorm(x, norm1_g[l]) * (1 + sc1) + sh1
        spec = hyena_filter_spectrum(x.shape[1], hy_w1[l], hy_b1[l], hy_w2[l], hy_b2[l], hy_w3[l], hy_freq[l])
        mix, gla_fin, ml_fin = token_mixers(h, w_in[l], b_in[l], hy_conv[l], spec, hy_bias[l], gla_a2_w[l],
                                            gla_a2_b[l], gla_norm_g[l], ml_conv[l], ml_gate_b[l], ml_norm_g[l],
                                            w_branch[l], w_out[l], gla_init, ml_init, grid)
        x = x + gt1 * mix
        h = rmsnorm(x, norm2_g[l]) * (1 + sc2) + sh2
        x = x + gt2 * peer(h, peer_wq[l], peer_keys[l], peer_u[l], peer_v[l])
        return x, gla_fin, ml_fin

    bp = x_prompt.shape[0]
    z_gla = jnp.zeros((bp, GLA_HEADS, GLA_DK, GLA_DV), jnp.float32)
    z_ml = (jnp.zeros((bp, ML_HEADS, ML_DH, ML_DH), jnp.float32),
            jnp.zeros((bp, ML_HEADS, ML_DH), jnp.float32),
            jnp.zeros((bp, ML_HEADS), jnp.float32))
    xp = x_prompt
    new_gla, new_c, new_n, new_m = [], [], [], []
    for l in range(DEPTH):
        mod_ctx = jax.nn.silu(c_ctx)[None] @ mod_w[l] + mod_b[l]
        xp, gla_fin, ml_fin = run_layer(xp, mod_ctx, l, (z_gla, z_gla), (z_ml, z_ml), False)
        new_gla.append(jnp.stack(gla_fin, axis=1))
        new_c.append(jnp.stack([ml_fin[0][0], ml_fin[1][0]], axis=1))
        new_n.append(jnp.stack([ml_fin[0][1], ml_fin[1][1]], axis=1))
        new_m.append(jnp.stack([ml_fin[0][2], ml_fin[1][2]], axis=1))
    new_state_gla = jnp.stack(new_gla, axis=1)
    new_state_mlstm_C = jnp.stack(new_c, axis=1)
    new_state_mlstm_n = jnp.stack(new_n, axis=1)
    new_state_mlstm_m = jnp.stack(new_m, axis=1)

    xs = x_sample
    for l in range(DEPTH):
        mod = jax.nn.silu(c) @ mod_w[l] + mod_b[l]
        gla_init = (_f32(state_gla[:, l, 0]), _f32(state_gla[:, l, 1]))
        ml_init = tuple((_f32(state_mlstm_C[:, l, dr]), _f32(state_mlstm_n[:, l, dr]), _f32(state_mlstm_m[:, l, dr]))
                        for dr in range(2))
        xs, _, _ = run_layer(xs, mod, l, gla_init, ml_init, True)

    y_prompt = rmsnorm(xp, final_g)
    y_sample = rmsnorm(xs, final_g)
    return (y_prompt, y_sample, new_state_gla, new_state_mlstm_C, new_state_mlstm_n, new_state_mlstm_m)


_drawn_inputs = setup_inputs


def setup_inputs(seed=0):
    import zlib

    import numpy as np

    out = dict(_drawn_inputs(seed))
    spreads = {}
    factors = {'state_gla': 64.0,
     'state_mlstm_C': 22.792,
     'state_mlstm_n': 37.816,
     'state_mlstm_m': 41.592,
     'norm2_g': 53.136,
     'final_g': 24.801,
     'hy_conv': 5.121,
     'hy_w1': 5.408,
     'hy_b1': 8.0,
     'hy_w2': 5.802,
     'hy_b2': 8.0,
     'hy_w3': 5.823,
     'hy_freq': 8.0,
     'hy_bias': 8.0,
     'gla_norm_g': 200.0,
     'ml_norm_g': 200.0}
    for name, (base, spread) in spreads.items():
        noise = np.random.default_rng([zlib.crc32(name.encode()), seed]).standard_normal(out[name].shape)
        drawn = base * np.exp(spread * noise) if base else spread * noise
        out[name] = jnp.asarray(drawn.astype(out[name].dtype))
    for name, factor in factors.items():
        out[name] = (out[name] * factor).astype(out[name].dtype)
    return out
```

```python
from contextlib import ExitStack
import math

import numpy as np

import concourse.bass as bass
from concourse import mybir

ALU = mybir.AluOpType
ACT = mybir.ActivationFunctionType
AX_X = mybir.AxisListType.X
F32 = mybir.dt.float32
U32 = mybir.dt.uint32

P = 128
D = 2048
KD = D // P
PROMPT, SAMPLE = 128, 256
TOK = PROMPT + SAMPLE
TT = TOK // P
CHUNK = 64
NC = TOK // CHUNK
GROUPS = ((0, 2), (2, 4))
EPS = 1e-6
W = 1024
WT = W // P
HEADS = 4
DK, DV = 128, 256
SUB = 16
NSUB = CHUNK // SUB
MAX_EXP = 50.0
NEG = -1.0e30
COL_HY, COL_GLA, COL_LR, COL_ML, COL_IF, COL_GATE = 0, 3072, 6144, 6176, 10272, 10288
PEER_H, NKEYS, TOPK = 8, 128, 16
MAGIC = 12582912.0
TWO_PI_HI = 6.28125
TWO_PI_LO = 2.0 * math.pi - TWO_PI_HI
PI_IN = 3.1415925

C_ID = 0
C_TRI = 128
C_GMASK = C_TRI + 2 * P
C_NEG = C_GMASK + 2 * CHUNK
C_SEL = C_NEG + 2 * CHUNK
C_IOTA = C_SEL + 4 * P
C_ONE = C_IOTA + TOPK
C_END = C_ONE + 1
V_HY, V_GLA, V_ML, V_GATE = 0, 24, 48, 80
V_HYCONV, V_MLCONV = 128, 128 + 72
V_N1, V_N2, V_GLAN, V_MLN = 256, 272, 288, 290


def shape_constants():
    c = np.zeros((P, C_END), np.float32)
    c[:, C_ID:C_ID + P] = np.eye(P)
    t = np.arange(P)
    same = (t[:, None] // CHUNK) == (t[None, :] // CHUNK)
    c[:, C_TRI:C_TRI + P] = (same & (t[:, None] <= t[None, :])) / 16.0
    c[:, C_TRI + P:C_TRI + 2 * P] = (same & (t[:, None] >= t[None, :])) / 16.0
    s = np.arange(CHUNK)
    fwd = s[:, None] <= s[None, :]
    bwd = s[:, None] >= s[None, :]
    for n, m in enumerate((fwd, bwd)):
        c[:CHUNK, C_GMASK + n * CHUNK:C_GMASK + (n + 1) * CHUNK] = m
        c[:CHUNK, C_NEG + n * CHUNK:C_NEG + (n + 1) * CHUNK] = np.where(m, 0.0, NEG)
    for h in range(HEADS):
        c[h, C_SEL + h * P:C_SEL + (h + 1) * P] = 1.0
    c[:, C_IOTA:C_IOTA + TOPK] = np.arange(TOPK)
    c[:, C_ONE] = 1.0
    out = {"cst": c}
    for name, n in (("p", PROMPT), ("s", SAMPLE)):
        k = np.arange(n)
        ang = np.pi * ((2 * k[None, :] + 1) * k[:, None] % (4 * n)) / (2 * n)
        mats = np.stack([np.cos(ang), np.sin(ang), np.cos(ang).T / n, np.sin(ang).T / n])
        out["dft_" + name] = np.ascontiguousarray(
            mats.reshape(4, n // P, P, n).transpose(2, 0, 1, 3)).astype(np.float32)
        t = np.arange(n, dtype=np.float32)
        tn = t / np.float32(n - 1)
        bands = np.linspace(1e-4, 15, 16, dtype=np.float32)
        an = (np.float32(2.0 * math.pi / n) * t[:, None] * bands[None, :]).astype(np.float32)
        z = np.concatenate([tn[:, None], np.cos(an), -np.sin(an)], -1)
        out["feat_" + name] = np.ascontiguousarray(z.T).astype(np.float32)
        lo, hi = math.log(1e-2) / 1.5, math.log(1e-2) / 0.3
        deltas = np.abs(np.linspace(lo, hi, W, dtype=np.float32))
        win = np.exp(-tn[:, None] * deltas[None, :]).astype(np.float32)
        out["win_" + name] = np.ascontiguousarray(win.reshape(n // P, P, W).transpose(1, 0, 2))
    return out


class Steps:

    def __init__(self, eng, sem):
        self.eng, self.sem, self.n, self.base = eng, sem, 0, 0

    def __call__(self, ins, wait=True):
        self.n += 1
        ins.then_inc(self.sem, 1)
        if wait:
            self.eng.wait_ge(self.sem, self.base + self.n)

    def enter(self, turn, per):
        self.before, self.base, self.n = self.n, turn * per + self.n, 0
        self.per = per

    def leave(self, turns):
        assert self.n == self.per, (self.n, self.per)
        self.base, self.n = 0, self.before + turns * self.per


class Core:
    pass


def build(nc, io, upto=99):
    k = Core()
    k.nc, k.io = nc, io
    with ExitStack() as top:
        k.banks = [top.enter_context(nc.psum_tensor(f"bank{i}", [P, 512], F32)) for i in range(8)]

        handles = []

        def sem(name):
            handles.append(nc.alloc_semaphore(name=name))
            return handles[-1]

        def clear_semaphores():
            with nc.Block() as block:
                @block.gpsimd
                def _(pool):
                    for s in handles:
                        pool.sem_clear(s)
            for s in handles:
                nc.release_semaphore(s)
            handles.clear()

        def sb(ctx, name, shape, dt=F32):
            return ctx.enter_context(nc.sbuf_tensor(name, shape, dt))

        k.sem, k.sb = sem, sb
        k.cst = sb(top, "cst", [P, C_END])
        k.vcol = sb(top, "vcol", [P, 3 * P])
        k.h2cols = sb(top, "h2cols", [P, 2, KD, 2])
        k.gt_dram = nc.dram_tensor("gt_rows", (2, 2, D), F32, kind="Internal").ap()
        k.x1_dram = nc.dram_tensor("x1_rows", (TT, P, D), F32, kind="Internal").ap()
        with ExitStack() as mix:
            k.hT = sb(mix, "hT", [P, KD, TOK])
            k.h1cols = sb(mix, "h1cols", [P, 2, KD, 2])
            with ExitStack() as ctx:
                stage_modulation(k, ctx)
            with ExitStack() as ctx:
                stage_norm(k, ctx, 1)
            if upto < 2: return
            k.yT = [sb(mix, "yT_hyena", [P, WT, TOK])]
            with ExitStack() as ctx:
                k.uTM = sb(ctx, "hyena_rows", [P, 3, TT, W])
                with ExitStack() as in1:
                    zT = sb(in1, "z_hyena", [P, 24, TOK])
                    with ExitStack() as in2:
                        stage_project(k, in2, "hy", COL_HY, V_HY, zT, 24)
                    with ExitStack() as in2:
                        stage_hyena_rows(k, in2, zT)
                if upto < 3: return
                k.dft = {"p": sb(ctx, "dft_prompt", [P, 4, 1, PROMPT]),
                         "s": sb(ctx, "dft_sample", [P, 4, 2, SAMPLE])}
                k.spec = sb(ctx, "filter_spectra", [P, 3, 2, 2, W])
                with ExitStack() as in1:
                    stage_filters(k, in1)
                with ExitStack() as in1:
                    stage_hyena(k, in1)
            if upto < 4: return
            k.yT.append(sb(mix, "yT_gla", [P, WT, TOK]))
            with ExitStack() as ctx:
                zT = sb(ctx, "z_gla", [P, 24, TOK])
                k.lrT = sb(ctx, "low_rank", [17, 2, TOK])
                with ExitStack() as in1:
                    stage_project(k, in1, "gla", COL_GLA, V_GLA, zT, 24)
                with ExitStack() as in1:
                    stage_gla(k, in1, zT)
            if upto < 5: return
            k.yT.append(sb(mix, "yT_mlstm", [P, WT, TOK]))
            with ExitStack() as ctx:
                zT = sb(ctx, "z_mlstm", [P, 32, TOK])
                with ExitStack() as in1:
                    stage_project(k, in1, "ml", COL_ML, V_ML, zT, 32)
                with ExitStack() as in1:
                    stage_mlstm(k, in1, zT)
            if upto < 6: return
            clear_semaphores()
            k.mergedT = sb(mix, "mergedT", [P, KD, TOK])
            with ExitStack() as ctx:
                stage_merge(k, ctx)
            with ExitStack() as ctx:
                stage_out(k, ctx)
        if upto < 7: return
        with ExitStack() as tail:
            k.h1cols = k.h2cols
            k.index = sb(tail, "expert_index", [P, TT * PEER_H, TOPK], U32)
            k.gate = sb(tail, "expert_gate", [P, TT * PEER_H, TOPK])
            k.h2 = sb(tail, "h2_rows", [P, TT, D])
            with ExitStack() as ctx:
                k.hT = sb(ctx, "h2T", [P, KD, TOK])
                with ExitStack() as in1:
                    stage_norm(k, in1, 2)
                if upto < 8: return
                k.scores = sb(ctx, "key_scores", [P, TT, 2 * PEER_H, NKEYS])
                with ExitStack() as in1:
                    stage_queries(k, in1)
                with ExitStack() as in1:
                    stage_topk(k, in1)
            if upto < 9: return
            k.acc = sb(tail, "expert_sum", [P, TT, D])
            with ExitStack() as ctx:
                stage_experts(k, ctx)
            with ExitStack() as ctx:
                stage_final(k, ctx)


def stage_modulation(k, ctx):
    nc, io, sem = k.nc, k.io, k.sem
    SLOTS, COLS = 3, 512
    TURNS = 6 * D // COLS // SLOTS
    ring = [k.sb(ctx, f"mod_w{s}", [P, KD, COLS]) for s in range(SLOTS)]
    rows = k.sb(ctx, "mod_rows", [2, 6 * D])
    bias = k.sb(ctx, "mod_bias", [2, 6 * D // 2])
    vrow = k.sb(ctx, "vector_rows", [P, 3, P])
    cT = k.sb(ctx, "cT", [P, KD, 2])
    const_in, vec_in, c_in, bias_in = sem("const_in"), sem("vec_in"), sem("c_in"), sem("mod_bias_in")
    slot_in = [sem(f"mod_w_in{s}") for s in range(SLOTS)]
    silu_done, part_done, part_out = sem("silu_done"), sem("mod_part_done"), sem("mod_part_out")
    zeroed, vec_turned, vec_out = sem("vec_zeroed"), sem("vec_turned"), sem("vec_out")
    mod_turned, gt_stored = sem("mod_turned"), sem("gt_stored")
    w = io["mod_w"][0].rearrange("(k p) n -> p k n", p=P)
    b_in = io["b_in"][0]

    with nc.Block() as block:
        @block.sync
        def _(sp):
            sp.dma_start(cT[:, :, 0], io["c_ctx"].rearrange("(k p) -> p k", p=P),
                         allow_slow_non_contiguous=True).then_inc(c_in, 16)
            sp.dma_start(cT[:, :, 1], io["c"][0].rearrange("(k p) -> p k", p=P),
                         allow_slow_non_contiguous=True).then_inc(c_in, 16)
            for s in range(SLOTS):
                sp.dma_start(ring[s][:, :, :], w[:, :, s * COLS:(s + 1) * COLS]).then_inc(slot_in[s], 16)
            with sp.Fori(1, TURNS) as i:
                for s in range(SLOTS):
                    sp.wait_ge(part_done, i * SLOTS + (s + 1 - SLOTS))
                    sp.dma_start(ring[s][:, :, :], w[:, :, bass.ds(i * (SLOTS * COLS) + s * COLS, COLS)]
                                 ).then_inc(slot_in[s], 16)

        @block.scalar
        def _(act):
            half = 3 * D
            act.dma_start(k.cst[:, :], io["cst"]).then_inc(const_in, 16)
            act.dma_start(bias[:, :], io["mod_b"][:, 0:half].broadcast_to([2, half])).then_inc(bias_in, 16)
            act.wait_ge(zeroed, 1)
            act.dma_start(vrow[0:48, 0, :], b_in[0:COL_LR].rearrange("(r c) -> r c", c=P)).then_inc(vec_in, 16)
            act.dma_start(vrow[48:80, 0, :], b_in[COL_ML:COL_IF].rearrange("(r c) -> r c", c=P)).then_inc(vec_in, 16)
            act.dma_start(vrow[80:128, 0, :], b_in[COL_GATE:].rearrange("(r c) -> r c", c=P)).then_inc(vec_in, 16)
            act.dma_start(vrow[0:72, 1, :], io["hy_conv"][0].rearrange("a b (r c) -> (a b r) c", c=P)).then_inc(vec_in, 16)
            act.dma_start(vrow[72:120, 1, :], io["ml_conv"][0].rearrange("a b (r c) -> (a b r) c", c=P)).then_inc(vec_in, 16)
            act.dma_start(vrow[0:16, 2, :], io["norm1_g"][0].rearrange("(r c) -> r c", c=P)).then_inc(vec_in, 16)
            act.dma_start(vrow[16:32, 2, :], io["norm2_g"][0].rearrange("(r c) -> r c", c=P)).then_inc(vec_in, 16)
            act.dma_start(vrow[32:34, 2, :], io["gla_norm_g"][0].rearrange("(r c) -> r c", c=P)).then_inc(vec_in, 16)
            act.dma_start(vrow[34:36, 2, :], io["ml_norm_g"][0].rearrange("(r c) -> r c", c=P)).then_inc(vec_in, 16)
            act.wait_ge(c_in, 32)
            act.activation(cT[:, :, :], cT[:, :, :], ACT.Silu).then_inc(silu_done, 1)
            act.wait_ge(part_out, SLOTS + TURNS * SLOTS // 2)
            act.dma_start(bias[:, :], io["mod_b"][:, half:].broadcast_to([2, half])).then_inc(bias_in, 16)
            act.wait_ge(part_out, SLOTS + TURNS * SLOTS)
            act.dma_start(k.gt_dram[0], rows[:, 2 * D:3 * D]).then_inc(gt_stored, 16)
            act.dma_start(k.gt_dram[1], rows[:, 5 * D:6 * D]).then_inc(gt_stored, 16)
            act.wait_ge(gt_stored, 32)

        @block.tensor
        def _(pe):
            pe.wait_ge(const_in, 16)
            pe.wait_ge(vec_in, 9 * 16)
            ident = k.cst[:, C_ID:C_ID + P]
            for n in range(3):
                last = pe.transpose(k.banks[7][:, n * P:(n + 1) * P], vrow[:, n, :], ident)
            last.then_inc(vec_turned, 1)
            pe.wait_ge(silu_done, 1)
            with pe.Fori(0, TURNS) as i:
                for s in range(SLOTS):
                    pe.wait_ge(slot_in[s], i * 16 + 16)
                    pe.wait_ge(part_out, i * SLOTS + (s + 1))
                    for kk in range(KD):
                        last = pe.matmul(k.banks[s][0:2, :], cT[:, kk, :], ring[s][:, kk, :],
                                         start=(kk == 0), stop=(kk == KD - 1))
                    last.then_inc(part_done, 1)
            pe.wait_ge(part_out, SLOTS + TURNS * SLOTS)
            for n, part in enumerate((0, 1, 3, 4)):
                for t in range(KD):
                    at = part * D + t * P
                    last = pe.transpose(k.banks[6][:, (n * KD + t) * 2:(n * KD + t) * 2 + 2],
                                        rows[:, at:at + P], k.cst[0:2, C_ID:C_ID + 2])
            last.then_inc(mod_turned, 1)

        @block.vector
        def _(dve):
            dve.memset(vrow[:, :, :], 0.0).then_inc(zeroed, 1)
            dve.sem_inc(part_out, SLOTS)
            dve.wait_ge(vec_turned, 1)
            dve.tensor_copy(k.vcol[:, :], k.banks[7][:, 0:3 * P]).then_inc(vec_out, 1)
            for half in range(2):
                dve.wait_ge(bias_in, 16 * (half + 1))
                n = TURNS // 2
                with dve.Fori(0, n) as i:
                    for s in range(SLOTS):
                        dve.wait_ge(part_done, i * SLOTS + (half * n * SLOTS + s + 1))
                        dve.tensor_tensor(
                            rows[:, bass.ds(i * (SLOTS * COLS) + (half * n * SLOTS + s) * COLS, COLS)],
                            k.banks[s][0:2, :], bias[:, bass.ds(i * (SLOTS * COLS) + s * COLS, COLS)],
                            ALU.add).then_inc(part_out, 1)
            dve.wait_ge(vec_out, 1)
            dve.wait_ge(mod_turned, 1)
            cols = k.banks[6][:, 0:4 * KD * 2].rearrange("p (n t g) -> p n t g", n=4, t=KD)
            for n, (dst, v) in enumerate(((k.h1cols, V_N1), (k.h2cols, V_N2))):
                gain = k.vcol[:, v:v + KD].unsqueeze(2).broadcast_to([P, KD, 2])
                dve.scalar_tensor_tensor(out=dst[:, 0, :, :], in0=cols[:, 2 * n + 1], scalar=1.0, in1=gain,
                                         op0=ALU.add, op1=ALU.mult).then_inc(vec_out, 1)
                dve.tensor_copy(dst[:, 1, :, :], cols[:, 2 * n]).then_inc(vec_out, 1)


def stage_norm(k, ctx, which):
    nc, io, sem = k.nc, k.io, k.sem
    x = k.sb(ctx, f"norm{which}_x", [P, TT, D])
    junk = k.sb(ctx, f"norm{which}_squares", [P, D])
    ss = k.sb(ctx, f"norm{which}_sums", [P, TT])
    x_in, squared, root, scaled = (sem(f"norm{which}_{n}") for n in ("x_in", "squared", "root", "scaled"))
    turned, written, rms = sem(f"norm{which}_turned"), sem(f"norm{which}_written"), sem(f"norm{which}_rms")

    with nc.Block() as block:
        @block.sync
        def _(sp):
            if which == 1:
                sp.dma_start(x[:, 0, :], io["x_prompt"][0]).then_inc(x_in, 16)
                sp.dma_start(x[:, 1:3, :], io["x_sample"][0].rearrange("(t p) d -> p t d", p=P)).then_inc(x_in, 16)
            else:
                sp.dma_start(x[:, :, :], k.x1_dram.rearrange("t p d -> p t d")).then_inc(x_in, 32)

        @block.scalar
        def _(act):
            act.wait_ge(x_in, 32)
            for t in range(TT):
                act.activation(junk[:, :], x[:, t, :], ACT.Square, accum_out=ss[:, t:t + 1]).then_inc(squared, 1)
                act.wait_ge(squared, t + 1)
            act.wait_ge(rms, 1)
            act.activation(ss[:, :], ss[:, :], ACT.Sqrt).then_inc(root, 1)
            act.wait_ge(rms, 2)
            for t in range(TT):
                act.activation(x[:, t, :], x[:, t, :], ACT.Copy, scale=ss[:, t:t + 1]).then_inc(scaled, 1)

        @block.tensor
        def _(pe):
            for t in range(KD):
                for r in range(TT):
                    pe.wait_ge(scaled, r + 1)
                    if t >= 4:
                        pe.wait_ge(written, 2 * (t - 3))
                    last = pe.transpose(k.banks[t % 4][:, r * P:(r + 1) * P], x[:, r, t * P:(t + 1) * P],
                                        k.cst[:, C_ID:C_ID + P])
                last.then_inc(turned, 1)

        @block.vector
        def _(dve):
            dve.wait_ge(squared, TT)
            dve.tensor_scalar(ss[:, :], ss[:, :], 1.0 / D, EPS, ALU.mult, ALU.add).then_inc(rms, 1)
            dve.wait_ge(root, 1)
            dve.reciprocal(ss[:, :], ss[:, :]).then_inc(rms, 1)
            for t in range(KD):
                dve.wait_ge(turned, t + 1)
                for g, (a, b) in enumerate(((0, PROMPT), (PROMPT, TOK))):
                    dve.tensor_scalar(k.hT[:, t, a:b], k.banks[t % 4][:, a:b], k.h1cols[:, 0, t, g:g + 1],
                                      k.h1cols[:, 1, t, g:g + 1], ALU.mult, ALU.add).then_inc(written, 1)


def stage_project(k, ctx, name, col0, v0, zT, tiles):
    nc, io, sem = k.nc, k.io, k.sem
    SLOTS, COLS, BANKS = 4, 256, 4
    TURNS = tiles * P // COLS // SLOTS
    PER = SLOTS * COLS // P
    ring = [k.sb(ctx, f"{name}_w{s}", [P, KD, COLS]) for s in range(SLOTS)]
    slot_in = [sem(f"{name}_w_in{s}") for s in range(SLOTS)]
    tile_done, tile_out = sem(f"{name}_tile_done"), sem(f"{name}_tile_out")
    w = io["w_in"][0].rearrange("(k p) n -> p k n", p=P)

    with nc.Block() as block:
        @block.sync
        def _(sp):
            for s in range(SLOTS):
                at = col0 + s * COLS
                sp.dma_start(ring[s][:, :, :], w[:, :, at:at + COLS]).then_inc(slot_in[s], 16)
            with sp.Fori(1, TURNS) as i:
                for s in range(SLOTS):
                    sp.wait_ge(tile_done, i * PER + (2 * (s + 1) - PER))
                    sp.dma_start(ring[s][:, :, :], w[:, :, bass.ds(i * (SLOTS * COLS) + (col0 + s * COLS), COLS)]
                                 ).then_inc(slot_in[s], 16)

        @block.tensor
        def _(pe):
            with pe.Fori(0, TURNS) as i:
                for j in range(PER):
                    s, half = j // 2, j % 2
                    if half == 0:
                        pe.wait_ge(slot_in[s], i * 16 + 16)
                    pe.wait_ge(tile_out, i * PER + (j + 1))
                    for kk in range(KD):
                        last = pe.matmul(k.banks[j % BANKS][:, 0:TOK], ring[s][:, kk, half * P:(half + 1) * P],
                                         k.hT[:, kk, :], start=(kk == 0), stop=(kk == KD - 1))
                    last.then_inc(tile_done, 1)

        @block.scalar
        def _(act):
            act.sem_inc(tile_out, BANKS)
            with act.Fori(0, TURNS) as i:
                for j in range(PER):
                    act.wait_ge(tile_done, i * PER + (j + 1))
                    act.activation(zT[:, bass.ds(i * PER + j, 1), :], k.banks[j % BANKS][:, 0:TOK].unsqueeze(1),
                                   ACT.Identity, bias=k.vcol[:, bass.ds(i * PER + (v0 + j), 1)]
                                   ).then_inc(tile_out, 1)


def short_conv(dve, go, out, z, wcol):
    go(dve.tensor_scalar(out, z, wcol(1), None, ALU.mult))
    for tap in (0, 2):
        for a, b, n in ((0, PROMPT, PROMPT), (PROMPT, TOK, CHUNK)):
            o = out[:, a:b].rearrange("p (r c) -> p r c", c=n)
            i = z[:, a:b].rearrange("p (r c) -> p r c", c=n)
            o, i = (o[:, :, 1:], i[:, :, :-1]) if tap == 0 else (o[:, :, :-1], i[:, :, 1:])
            last = dve.scalar_tensor_tensor(out=o, in0=i, scalar=wcol(tap), in1=o, op0=ALU.mult, op1=ALU.add)
            if tap == 0 or a == 0:
                go(last)
    return last


def stage_hyena_rows(k, ctx, zT):
    nc, sem = k.nc, k.sem
    conv = [k.sb(ctx, f"hy_conv{s}", [P, TOK]) for s in range(2)]
    conv_done, conv_turned, rows_out = sem("hy_conv_done"), sem("hy_conv_turned"), sem("hy_rows_out")
    with nc.Block() as block:
        @block.vector
        def _(dve):
            go = Steps(dve, sem("hy_conv_step"))
            for part in range(3):
                with dve.Fori(0, WT // 2) as i:
                    go.enter(i, 8)
                    for s in range(2):
                        dve.wait_ge(conv_turned, i * 2 + (part * WT + s + 1))
                        def wcol(tap, s=s):
                            return k.vcol[:, bass.ds(i * 2 + (V_HYCONV + (part * 3 + tap) * WT + s), 1)]
                        z = zT[:, bass.ds(i * 2 + (part * WT + s), 1), :].rearrange("p a t -> p (a t)")
                        short_conv(dve, go, conv[s][:, :], z, wcol).then_inc(conv_done, 1)
                    go.leave(WT // 2)

        @block.tensor
        def _(pe):
            pe.sem_inc(conv_turned, 2)
            with pe.Fori(0, 3 * WT // 2) as i:
                for s in range(2):
                    pe.wait_ge(conv_done, i * 2 + (s + 1))
                    pe.wait_ge(rows_out, i * 2 + (s + 1))
                    for r in range(TT):
                        last = pe.transpose(k.banks[s][:, r * P:(r + 1) * P], conv[s][:, r * P:(r + 1) * P],
                                            k.cst[:, C_ID:C_ID + P])
                    last.then_inc(conv_turned, 1)

        @block.scalar
        def _(act):
            act.sem_inc(rows_out, 2)
            for part in range(3):
                with act.Fori(0, WT // 2) as i:
                    for s in range(2):
                        act.wait_ge(conv_turned, i * 2 + (part * WT + s + 3))
                        act.copy(k.uTM[:, part, :, bass.ds(i * (2 * P) + s * P, P)],
                                 k.banks[s][:, 0:TOK].rearrange("p (r c) -> p r c", c=P)).then_inc(rows_out, 1)


def stage_filters(k, ctx):
    nc, io, sem = k.nc, k.io, k.sem
    w1 = k.sb(ctx, "ffn_w1", [33, 64])
    w2 = k.sb(ctx, "ffn_w2", [64, 64])
    w3 = k.sb(ctx, "ffn_w3", [64, 4 * W])
    feat = k.sb(ctx, "features", [33, TOK])
    cols = k.sb(ctx, "ffn_cols", [64, 4])
    win = k.sb(ctx, "window", [P, TT, W])
    bias = k.sb(ctx, "lag0_bias", [1, 2, W])
    hid = [k.sb(ctx, f"hidden{n}", [64, TOK]) for n in range(2)]
    turns = k.sb(ctx, "turns", [64, TOK])
    fw, bw = k.sb(ctx, "filter_fwd", [P, W]), k.sb(ctx, "filter_bwd", [P, W])
    both = k.sb(ctx, "filter_sum_diff", [P, 2, 2, W])
    ffn_in, filt_in = sem("ffn_in"), sem("filter_in")
    hid_mm, arg_ready, hid_ready = sem("hidden_mm"), sem("sin_argument"), sem("hidden_ready")
    filt_mm, filt_read, filt_ready = sem("filter_mm"), sem("filter_read"), sem("filter_ready")
    spec_mm, spec_out = sem("spectrum_mm"), sem("spectrum_out")
    combos = [(name, o) for name in "ps" for o in range(2)]
    first, count = {"p": 0, "s": 1}, {"p": 1, "s": 2}

    with nc.Block() as block:
        @block.sync
        def _(sp):
            sp.dma_start(w1[:, :], io["hy_w1"][0]).then_inc(ffn_in, 16)
            sp.dma_start(w2[:, :], io["hy_w2"][0]).then_inc(ffn_in, 16)
            sp.dma_start(feat[:, 0:PROMPT], io["feat_p"]).then_inc(ffn_in, 16)
            sp.dma_start(feat[:, PROMPT:], io["feat_s"]).then_inc(ffn_in, 16)
            sp.dma_start(cols[:, 0:1], io["hy_b1"][0].unsqueeze(1)).then_inc(ffn_in, 16)
            sp.dma_start(cols[:, 1:2], io["hy_b2"][0].unsqueeze(1)).then_inc(ffn_in, 16)
            sp.dma_start(cols[:, 2:3], io["hy_freq"][0, 0].unsqueeze(1)).then_inc(ffn_in, 16)
            sp.dma_start(cols[:, 3:4], io["hy_freq"][0, 1].unsqueeze(1)).then_inc(ffn_in, 16)
            sp.dma_start(w3[:, :], io["hy_w3"][0]).then_inc(filt_in, 16)
            sp.dma_start(win[:, 0:1, :], io["win_p"]).then_inc(filt_in, 16)
            sp.dma_start(win[:, 1:3, :], io["win_s"]).then_inc(filt_in, 16)
            sp.dma_start(bias[:, :, :], io["hy_bias"]).then_inc(filt_in, 16)
            sp.dma_start(k.dft["p"][:, :, :, :], io["dft_p"]).then_inc(filt_in, 16)
            sp.dma_start(k.dft["s"][:, :, :, :], io["dft_s"]).then_inc(filt_in, 16)

        @block.tensor
        def _(pe):
            pe.wait_ge(ffn_in, 8 * 16)
            pe.matmul(k.banks[0][0:64, 0:TOK], w1[:, :], feat[:, :], start=True, stop=True).then_inc(hid_mm, 1)
            pe.wait_ge(hid_ready, 1)
            pe.matmul(k.banks[0][0:64, 0:TOK], w2[:, :], hid[0][:, :], start=True, stop=True).then_inc(hid_mm, 1)
            pe.wait_ge(hid_ready, 2)
            pe.wait_ge(filt_in, 6 * 16)
            tile, spec = 0, 0
            for n, (name, o) in enumerate(combos):
                for t in range(count[name]):
                    if tile:
                        pe.wait_ge(filt_read, tile)
                    at = (first[name] + t) * P
                    for b in range(4):
                        last = pe.matmul(k.banks[b][:, :], hid[1][:, at:at + P],
                                         w3[:, o * 2 * W + b * 512:o * 2 * W + (b + 1) * 512],
                                         start=True, stop=True)
                    last.then_inc(filt_mm, 1)
                    tile += 1
                pe.wait_ge(filt_ready, n + 1)
                dft = k.dft[name]
                for m in range(count[name]):
                    for part in range(2):
                        for half in range(2):
                            if spec >= 4:
                                pe.wait_ge(spec_out, spec - 3)
                            for t in range(count[name]):
                                last = pe.matmul(k.banks[4 + spec % 4][:, :], dft[:, part, t, m * P:(m + 1) * P],
                                                 both[:, t, part, half * 512:(half + 1) * 512],
                                                 start=(t == 0), stop=(t == count[name] - 1))
                            last.then_inc(spec_mm, 1)
                            spec += 1

        @block.scalar
        def _(act):
            for n in range(2):
                act.wait_ge(arg_ready, n + 1)
                act.activation(hid[n][:, :], hid[n][:, :], ACT.Sin).then_inc(hid_ready, 1)
            spec = 0
            for name, o in combos:
                for m in range(count[name]):
                    for part in range(2):
                        for half in range(2):
                            act.wait_ge(spec_mm, spec + 1)
                            act.copy(k.spec[:, first[name] + m, o, part, half * 512:(half + 1) * 512],
                                     k.banks[4 + spec % 4][:, :]).then_inc(spec_out, 1)
                            spec += 1

        @block.vector
        def _(dve):
            go = Steps(dve, sem("filter_step"))
            dve.wait_ge(ffn_in, 8 * 16)
            for n in range(2):
                dve.wait_ge(hid_mm, n + 1)
                go(dve.tensor_scalar(hid[n][:, :], k.banks[0][0:64, 0:TOK], cols[:, n:n + 1], cols[:, 2 + n:3 + n],
                                     ALU.add, ALU.mult))
                go(dve.tensor_scalar(turns[:, :], hid[n][:, :], 1.0 / (2.0 * math.pi), MAGIC, ALU.mult, ALU.add))
                go(dve.tensor_scalar(turns[:, :], turns[:, :], MAGIC, None, ALU.subtract))
                go(dve.scalar_tensor_tensor(out=hid[n][:, :], in0=turns[:, :], scalar=-TWO_PI_HI, in1=hid[n][:, :],
                                            op0=ALU.mult, op1=ALU.add))
                go(dve.scalar_tensor_tensor(out=hid[n][:, :], in0=turns[:, :], scalar=-TWO_PI_LO, in1=hid[n][:, :],
                                            op0=ALU.mult, op1=ALU.add))
                dve.tensor_scalar(hid[n][:, :], hid[n][:, :], PI_IN, -PI_IN, ALU.min, ALU.max).then_inc(arg_ready, 1)
            dve.wait_ge(filt_in, 6 * 16)
            tile, spec = 0, 0
            for n, (name, o) in enumerate(combos):
                if spec:
                    dve.wait_ge(spec_mm, spec)
                for t in range(count[name]):
                    dve.wait_ge(filt_mm, tile + 1)
                    for b in range(4):
                        dst = (fw, bw)[b // 2][:, b % 2 * 512:(b % 2 + 1) * 512]
                        last = dve.tensor_tensor(dst, k.banks[b][:, :],
                                                 win[:, first[name] + t, b % 2 * 512:(b % 2 + 1) * 512], ALU.mult)
                        if b < 3:
                            go(last, wait=False)
                    last.then_inc(filt_read, 1)
                    tile += 1
                    dve.wait_ge(filt_read, tile)
                    if t == 0:
                        go(dve.tensor_tensor(fw[0:1, :], fw[0:1, :], bias[:, o, :], ALU.add))
                        go(dve.memset(bw[0:1, :], 0.0))
                    go(dve.tensor_tensor(both[:, t, 0, :], fw[:, :], bw[:, :], ALU.add))
                    last = dve.tensor_tensor(both[:, t, 1, :], fw[:, :], bw[:, :], ALU.subtract)
                    if t == count[name] - 1:
                        last.then_inc(filt_ready, 1)
                        dve.wait_ge(filt_ready, n + 1)
                    else:
                        go(last)
                spec += 4 * count[name]


def stage_hyena(k, ctx):
    nc, sem = k.nc, k.sem
    uf = k.sb(ctx, "u_spectrum", [P, TT, 2, W])
    yf = k.sb(ctx, "y_spectrum", [P, TT, 2, W])
    tmp = k.sb(ctx, "product", [P, W])
    u_mm, u_out, y_ready = sem("u_mm"), sem("u_out"), sem("y_spectrum_ready")
    y_mm, rows_ready = sem("y_mm"), sem("hy_rows_ready")
    y_turned, y_stored = sem("hy_y_turned"), sem("hy_y_stored")
    units = [(g, o) for o in range(2) for g in "ps"]
    tiles = {"p": (0,), "s": (1, 2)}
    first = {"p": 0, "s": 1}
    H = lambda half: slice(half * 512, (half + 1) * 512)
    rows = k.uTM[:, 2]

    with nc.Block() as block:
        @block.tensor
        def _(pe):
            u = y = 0
            for o in range(2):
                for g in "ps":
                    if o:
                        pe.wait_ge(rows_ready, 2 * (first[g] + len(tiles[g])))
                    for m in tiles[g]:
                        for part in range(2):
                            for half in range(2):
                                if u >= 4:
                                    pe.wait_ge(u_out, u - 3)
                                for t in tiles[g]:
                                    mt = (m - first[g]) * P
                                    last = pe.matmul(k.banks[u % 4][:, :],
                                                     k.dft[g][:, part, t - first[g], mt:mt + P],
                                                     rows[:, t, H(half)], start=(t == tiles[g][0]),
                                                     stop=(t == tiles[g][-1]))
                                last.then_inc(u_mm, 1)
                                u += 1
                for g in "ps":
                    pe.wait_ge(y_ready, TT * o + first[g] + len(tiles[g]))
                    for t in tiles[g]:
                        for half in range(2):
                            if y >= 4:
                                pe.wait_ge(rows_ready, y - 3)
                            for part in range(2):
                                for m in tiles[g]:
                                    tt = (t - first[g]) * P
                                    last = pe.matmul(k.banks[4 + y % 4][:, :],
                                                     k.dft[g][:, 2 + part, m - first[g], tt:tt + P],
                                                     yf[:, m, part, H(half)],
                                                     start=(part == 0 and m == tiles[g][0]),
                                                     stop=(part == 1 and m == tiles[g][-1]))
                            last.then_inc(y_mm, 1)
                            y += 1
            pe.wait_ge(rows_ready, 4 * TT)
            for c in range(WT):
                if c >= 4:
                    pe.wait_ge(y_stored, c - 3)
                for t in range(TT):
                    last = pe.transpose(k.banks[c % 4][:, t * P:(t + 1) * P], rows[:, t, c * P:(c + 1) * P],
                                        k.cst[:, C_ID:C_ID + P])
                last.then_inc(y_turned, 1)

        @block.scalar
        def _(act):
            u = 0
            for o in range(2):
                for m in range(TT):
                    if o:
                        act.wait_ge(y_ready, m + 1)
                    for part in range(2):
                        for half in range(2):
                            act.wait_ge(u_mm, u + 1)
                            act.copy(uf[:, m, part, H(half)], k.banks[u % 4][:, :]).then_inc(u_out, 1)
                            u += 1
            for c in range(WT):
                act.wait_ge(y_turned, c + 1)
                act.copy(k.yT[0][:, c, :], k.banks[c % 4][:, 0:TOK]).then_inc(y_stored, 1)

        @block.vector
        def _(dve):
            go = Steps(dve, sem("hyena_step"))
            y = 0
            for o in range(2):
                for m in range(TT):
                    dve.wait_ge(u_out, 4 * (TT * o + m + 1))
                    if o:
                        dve.wait_ge(y_mm, 2 * TT)
                    ur, us = uf[:, m, 0, :], uf[:, m, 1, :]
                    hr, hs = k.spec[:, m, o, 0, :], k.spec[:, m, o, 1, :]
                    go(dve.tensor_tensor(yf[:, m, 0, :], ur, hr, ALU.mult), wait=False)
                    go(dve.tensor_tensor(tmp[:, :], us, hs, ALU.mult))
                    go(dve.tensor_tensor(yf[:, m, 0, :], yf[:, m, 0, :], tmp[:, :], ALU.subtract))
                    go(dve.tensor_tensor(yf[:, m, 1, :], ur, hs, ALU.mult), wait=False)
                    go(dve.tensor_tensor(tmp[:, :], us, hr, ALU.mult))
                    dve.tensor_tensor(yf[:, m, 1, :], yf[:, m, 1, :], tmp[:, :], ALU.add).then_inc(y_ready, 1)
                    dve.wait_ge(y_ready, TT * o + m + 1)
                for t in range(TT):
                    for half in range(2):
                        dve.wait_ge(y_mm, y + 1)
                        dve.tensor_tensor(rows[:, t, H(half)], k.banks[4 + y % 4][:, :], k.uTM[:, o, t, H(half)],
                                          ALU.mult).then_inc(rows_ready, 1)
                        y += 1


def chunk_of(group, turn, backward):
    first, count = group
    return turn * -1 + (first + count - 1) if backward else turn + first


def stage_gla(k, ctx, zT):
    nc, io, sem = k.nc, k.io, k.sem
    vTM = k.sb(ctx, "gla_v", [CHUNK, NC, W])
    oTM = k.sb(ctx, "gla_o", [P, NC, W])
    b = k.sb(ctx, "gla_cumulated", [P, 2, HEADS, TOK])
    state = k.sb(ctx, "gla_state", [P, 2, HEADS, DV])
    with ExitStack() as pre:
        gla_prepare(k, pre, zT, vTM, oTM, b, state)
    with ExitStack() as scan:
        gla_scan(k, scan, zT, vTM, oTM, b, state)
    with ExitStack() as post:
        stage_heads_out(k, post, "gla", oTM, zT[:, 16:24, :], ACT.Silu, V_GLAN, k.yT[1])


def rows_of_v(pe, act, k, zT, tile0, vTM, turned, out, banks):
    for n in range(NC * 2):
        if n >= len(banks):
            pe.wait_ge(out, n + 1 - len(banks))
        c, g = n // 2, n % 2
        for t in range(4):
            last = pe.transpose(banks[n % len(banks)][0:CHUNK, t * P:(t + 1) * P],
                                zT[:, tile0 + 4 * g + t, c * CHUNK:(c + 1) * CHUNK], k.cst[:, C_ID:C_ID + P])
        last.then_inc(turned, 1)


def gla_prepare(k, ctx, zT, vTM, oTM, b, state):
    nc, io, sem = k.nc, k.io, k.sem
    wlr = k.sb(ctx, "lr_w", [P, KD, 32])
    blr = k.sb(ctx, "lr_bias", [16, 2])
    a2 = k.sb(ctx, "gla_a2", [17, 2, HEADS * DK])
    lg = k.sb(ctx, "log_gate", [P, TT, 2, HEADS * DK])
    mag = oTM[:, 0:3, :].rearrange("p c (d n) -> p c d n", d=2)
    lr_in, v_turned, v_out = sem("lr_in"), sem("gla_v_turned"), sem("gla_v_out")
    lr_mm, lr_ready, x_mm, x_read = sem("lr_mm"), sem("lr_ready"), sem("gate_mm"), sem("gate_read")
    soft, lg_ready, sum_mm, sum_out = sem("softplus_done"), sem("log_gate_ready"), sem("cumsum_mm"), sem("cumsum_out")

    with nc.Block() as block:
        @block.sync
        def _(sp):
            sp.dma_start(wlr[:, :, :], io["w_in"][0].rearrange("(k p) n -> p k n", p=P)[:, :, COL_LR:COL_ML]
                         ).then_inc(lr_in, 16)
            sp.dma_start(blr[:, :], io["b_in"][0, COL_LR:COL_ML].rearrange("(d r) -> r d", d=2),
                         allow_slow_non_contiguous=True).then_inc(lr_in, 16)
            sp.dma_start(a2[0:16, :, :], io["gla_a2_w"][0].rearrange("d r n -> r d n")).then_inc(lr_in, 16)
            sp.dma_start(a2[16:17, :, :], io["gla_a2_b"]).then_inc(lr_in, 16)
            sp.dma_start(state[:, :, :, :], io["state_gla"][0, 0].rearrange("d h p v -> p d h v")).then_inc(lr_in, 16)
            sp.wait_ge(lr_in, 5 * 16)

        @block.tensor
        def _(pe):
            rows_of_v(pe, None, k, zT, 8, vTM, v_turned, v_out, k.banks[4:8])
            pe.wait_ge(lr_in, 5 * 16)
            for d in range(2):
                for kk in range(KD):
                    last = pe.matmul(k.banks[d][0:16, 0:TOK], wlr[:, kk, 16 * d:16 * d + 16], k.hT[:, kk, :],
                                     start=(kk == 0), stop=(kk == KD - 1))
                last.then_inc(lr_mm, 1)
            pe.wait_ge(lr_ready, 2)
            for n in range(2 * TT):
                t, d = n // 2, n % 2
                if n >= 4:
                    pe.wait_ge(x_read, n - 3)
                pe.matmul(k.banks[n % 4][:, :], k.lrT[:, d, t * P:(t + 1) * P], a2[:, d, :],
                          start=True, stop=True).then_inc(x_mm, 1)
            pe.wait_ge(lg_ready, 1)
            pe.wait_ge(v_out, NC * 2)
            for n in range(2 * HEADS):
                d, h = n // HEADS, n % HEADS
                if n >= 4:
                    pe.wait_ge(sum_out, n - 3)
                for t in range(TT):
                    last = pe.matmul(k.banks[4 + n % 4][:, t * P:(t + 1) * P], lg[:, t, d, h * DK:(h + 1) * DK],
                                     k.cst[:, C_TRI + d * P:C_TRI + (d + 1) * P], start=True, stop=True)
                last.then_inc(sum_mm, 1)

        @block.scalar
        def _(act):
            for n in range(NC * 2):
                act.wait_ge(v_turned, n + 1)
                act.copy(vTM[:, n // 2, n % 2 * 512:(n % 2 + 1) * 512], k.banks[4 + n % 4][0:CHUNK, :]).then_inc(v_out, 1)
            act.wait_ge(x_read, 2 * TT)
            act.activation(mag, mag, ACT.Exp, scale=-1.0).then_inc(soft, 1)
            act.wait_ge(soft, 1)
            act.activation(mag, mag, ACT.Ln, bias=1.0).then_inc(soft, 1)
            for n in range(2 * HEADS):
                act.wait_ge(sum_mm, n + 1)
                act.copy(b[:, n // HEADS, n % HEADS, :], k.banks[4 + n % 4][:, 0:TOK]).then_inc(sum_out, 1)

        @block.vector
        def _(dve):
            go = Steps(dve, sem("gla_prepare_step"))
            dve.memset(k.lrT[:, :, :], 1.0).then_inc(lr_ready, 1)
            dve.wait_ge(lr_ready, 1)
            dve.wait_ge(lr_in, 5 * 16)
            for d in range(2):
                dve.wait_ge(lr_mm, d + 1)
                last = dve.tensor_scalar(k.lrT[0:16, d, :], k.banks[d][0:16, 0:TOK], blr[:, d:d + 1], None, ALU.add)
            last.then_inc(lr_ready, 1)
            for n in range(2 * TT):
                dve.wait_ge(x_mm, n + 1)
                go(dve.tensor_scalar(lg[:, n // 2, n % 2, :], k.banks[n % 4][:, :], 0.0, None, ALU.min))
                dve.scalar_tensor_tensor(out=mag[:, n // 2, n % 2, :], in0=lg[:, n // 2, n % 2, :], scalar=-2.0,
                                         in1=k.banks[n % 4][:, :], op0=ALU.mult, op1=ALU.add).then_inc(x_read, 1)
            dve.wait_ge(x_read, 2 * TT)
            dve.wait_ge(soft, 2)
            dve.tensor_tensor(lg[:, :, :, :], lg[:, :, :, :], mag, ALU.subtract).then_inc(lg_ready, 1)


def gla_scan(k, ctx, zT, vTM, oTM, b, state):
    nc, io, sem = k.nc, k.io, k.sem
    sub_k = [k.sb(ctx, f"gla_sub_k{d}", [P, NSUB, HEADS, CHUNK]) for d in range(2)]
    e3 = [k.sb(ctx, f"gla_e3{d}", [P, 3, HEADS, CHUNK]) for d in range(2)]
    att = [k.sb(ctx, f"gla_att{d}", [CHUNK, HEADS, CHUNK]) for d in range(2)]
    k_rows = [k.sb(ctx, f"gla_k_rows{d}", [CHUNK, HEADS * DK]) for d in range(2)]
    end = [k.sb(ctx, f"gla_end{d}", [P, HEADS]) for d in range(2)]
    v_now = [k.sb(ctx, f"gla_v_now{d}", [CHUNK, W]) for d in range(2)]
    v_ready = sem("gla_v_ready")
    diff_ready, exp_done, prep_done = sem("gla_diff_ready"), sem("gla_exp_done"), sem("gla_prep_done")
    att_mm, att_ready, k_turned, k_out = sem("gla_att_mm"), sem("gla_att_ready"), sem("gla_k_turned"), sem("gla_k_out")
    o_mm, o_read, state_mm, state_ready = sem("gla_o_mm"), sem("gla_o_read"), sem("gla_state_mm"), sem("gla_state_ready")
    state_stored = sem("gla_state_stored")
    runs = ((GROUPS[1], 0, 0), (GROUPS[0], 2 * GROUPS[1][1], 2 * GROUPS[1][1] + 2))
    qs = DK ** -0.5

    def toks(group, i, d):
        return bass.ds(chunk_of(group, i, d) * CHUNK, CHUNK)

    with nc.Block() as block:
        @block.vector
        def _(dve):
            go = Steps(dve, sem("gla_step"))
            go(dve.memset(oTM[0:CHUNK, :, :], 0.0))
            dve.sem_inc(state_ready, 2)
            for group, q0, s0 in runs:
                if q0:
                    dve.wait_ge(state_mm, q0)
                    dve.wait_ge(state_ready, q0 + 2)
                    dve.memset(state[:, :, :, :], 0.0).then_inc(state_ready, 2)
                    dve.wait_ge(state_ready, q0 + 4)
                with dve.Fori(0, group[1]) as i:
                    go.enter(i, 2 * (3 + 4 + 3))
                    for d in range(2):
                        q = i * 2 + (q0 + d)
                        bc = b[:, d, :, toks(group, i, d)]
                        qc, kc = zT[:, 0:4, toks(group, i, d)], zT[:, 4:8, toks(group, i, d)]
                        sub = bc.rearrange("p h (i s) -> p i h s", s=SUB)
                        ref = sub[:, :, :, SUB // 2:SUB // 2 + 1].broadcast_to([P, NSUB, HEADS, CHUNK])
                        dif = sub_k[d]
                        go(dve.tensor_tensor(dif[:, :, :, :], ref, bc.unsqueeze(1).broadcast_to([P, NSUB, HEADS, CHUNK]),
                                             ALU.subtract))
                        go(dve.tensor_scalar(dif[:, :, :, :], dif[:, :, :, :], MAX_EXP, None, ALU.min), wait=False)
                        own = bc.rearrange("p h (i s) -> p h i s", s=SUB)
                        go(dve.tensor_tensor(e3[d][:, 0].rearrange("p h (i s) -> p h i s", s=SUB), own,
                                             own[:, :, :, SUB // 2:SUB // 2 + 1].broadcast_to([P, HEADS, NSUB, SUB]),
                                             ALU.subtract), wait=False)
                        last = bc[:, :, 0:1] if d else bc[:, :, CHUNK - 1:CHUNK]
                        dve.tensor_tensor(e3[d][:, 1], last.broadcast_to([P, HEADS, CHUNK]), bc, ALU.subtract
                                          ).then_inc(diff_ready, 1)
                    for d in range(2):
                        q = i * 2 + (q0 + d)
                        qc, kc = zT[:, 0:4, toks(group, i, d)], zT[:, 4:8, toks(group, i, d)]
                        dve.wait_ge(exp_done, q * 3 + 3)
                        at = 0 if d else CHUNK - 1
                        go(dve.tensor_copy(end[d][:, :].unsqueeze(2), e3[d][:, 2, :, at:at + 1]))
                        go(dve.tensor_tensor(sub_k[d][:, :, :, :], sub_k[d][:, :, :, :],
                                             kc.unsqueeze(1).broadcast_to([P, NSUB, HEADS, CHUNK]), ALU.mult), wait=False)
                        go(dve.scalar_tensor_tensor(out=e3[d][:, 0], in0=e3[d][:, 0], scalar=qs, in1=qc,
                                                    op0=ALU.mult, op1=ALU.mult), wait=False)
                        go(dve.tensor_tensor(e3[d][:, 1], e3[d][:, 1], kc, ALU.mult), wait=False)
                        dve.scalar_tensor_tensor(out=e3[d][:, 2], in0=e3[d][:, 2], scalar=qs, in1=qc,
                                                 op0=ALU.mult, op1=ALU.mult).then_inc(prep_done, 1)
                    for d in range(2):
                        q = i * 2 + (q0 + d)
                        dve.wait_ge(att_mm, q + 1)
                        mask = k.cst[0:CHUNK, C_GMASK + d * CHUNK:C_GMASK + (d + 1) * CHUNK]
                        dve.tensor_tensor(att[d][:, :, :], k.banks[d][0:CHUNK, 0:HEADS * CHUNK].rearrange(
                            "p (h t) -> p h t", h=HEADS), mask.unsqueeze(1).broadcast_to([CHUNK, HEADS, CHUNK]),
                            ALU.mult).then_inc(att_ready, 1)
                    for d in range(2):
                        q = i * 2 + (q0 + d)
                        dve.wait_ge(o_mm, q + 1)
                        for half in range(2):
                            o = oTM[0:CHUNK, bass.ds(chunk_of(group, i, d), 1), half * 512:(half + 1) * 512]
                            add = dve.tensor_tensor(o, k.banks[4 + half][0:CHUNK, :].unsqueeze(1), o, ALU.add)
                        add.then_inc(o_read, 1)
                        dve.wait_ge(state_mm, q + 1)
                        for h in range(HEADS):
                            part = dve.scalar_tensor_tensor(
                                out=state[:, d, h, :], in0=state[:, d, h, :], scalar=end[d][:, h:h + 1],
                                in1=k.banks[6 + h // 2][:, h % 2 * DV:(h % 2 + 1) * DV], op0=ALU.mult, op1=ALU.add)
                            if h < HEADS - 1:
                                go(part, wait=False)
                        part.then_inc(state_ready, 1)
                    go.leave(group[1])

        @block.scalar
        def _(act):
            for group, q0, s0 in runs:
                with act.Fori(0, group[1]) as i:
                    for d in range(2):
                        q = i * 2 + (q0 + d)
                        act.wait_ge(diff_ready, q + 1)
                        act.activation(sub_k[d][:, :, :, :], sub_k[d][:, :, :, :], ACT.Exp).then_inc(exp_done, 1)
                        act.activation(e3[d][:, 0:2], e3[d][:, 0:2], ACT.Exp).then_inc(exp_done, 1)
                        act.activation(e3[d][:, 2], b[:, d, :, toks(group, i, d)], ACT.Exp).then_inc(exp_done, 1)
                    for d in range(2):
                        act.wait_ge(k_turned, i * 2 + (q0 + d + 1))
                        act.copy(k_rows[d][:, :], k.banks[2 + d][0:CHUNK, :]).then_inc(k_out, 1)
                    for d in range(2):
                        act.wait_ge(state_ready, i * 2 + (s0 + d + 1))
                        act.copy(v_now[d][:, :].unsqueeze(1), vTM[:, bass.ds(chunk_of(group, i, d), 1), :]
                                 ).then_inc(v_ready, 1)

        @block.tensor
        def _(pe):
            for group, q0, s0 in runs:
                with pe.Fori(0, group[1]) as i:
                    for d in range(2):
                        q = i * 2 + (q0 + d)
                        pe.wait_ge(prep_done, q + 1)
                        for h in range(HEADS):
                            for s in range(NSUB):
                                at = h * CHUNK + s * SUB
                                mm = pe.matmul(k.banks[d][0:CHUNK, at:at + SUB], sub_k[d][:, s, h, :],
                                               e3[d][:, 0, h, s * SUB:(s + 1) * SUB], start=True, stop=True)
                        mm.then_inc(att_mm, 1)
                        for h in range(HEADS):
                            mm = pe.transpose(k.banks[2 + d][0:CHUNK, h * DK:(h + 1) * DK], e3[d][:, 1, h, :],
                                              k.cst[:, C_ID:C_ID + P])
                        mm.then_inc(k_turned, 1)
                    for d in range(2):
                        q = i * 2 + (q0 + d)
                        v = lambda h: v_now[d][:, h * DV:(h + 1) * DV]
                        pe.wait_ge(att_ready, q + 1)
                        pe.wait_ge(v_ready, q + 1)
                        pe.wait_ge(o_read, q)
                        pe.wait_ge(state_ready, i * 2 + (s0 + d + 1))
                        for h in range(HEADS):
                            out = k.banks[4 + h // 2][0:CHUNK, h % 2 * DV:(h % 2 + 1) * DV]
                            pe.matmul(out, e3[d][:, 2, h, :], state[:, d, h, :], start=True, stop=False)
                            mm = pe.matmul(out, att[d][:, h, :], v(h), start=False, stop=True)
                        mm.then_inc(o_mm, 1)
                        pe.wait_ge(k_out, q + 1)
                        pe.wait_ge(state_ready, i * 2 + (s0 + d + 2))
                        for h in range(HEADS):
                            mm = pe.matmul(k.banks[6 + h // 2][:, h % 2 * DV:(h % 2 + 1) * DV],
                                           k_rows[d][:, h * DK:(h + 1) * DK], v(h), start=True, stop=True)
                        mm.then_inc(state_mm, 1)

        @block.sync
        def _(sp):
            sp.wait_ge(state_ready, 2 * NC + 4)
            sp.dma_start(io["new_state_gla"][0, 0].rearrange("d h p v -> p d h v"), state[:, :, :, :]
                         ).then_inc(state_stored, 16)
            sp.wait_ge(state_stored, 16)


def stage_heads_out(k, ctx, name, oTM, gateT, func, gain, yT):
    nc, sem = k.nc, k.sem
    sq = k.sb(ctx, name + "_squares", [CHUNK, W])
    ss = k.sb(ctx, name + "_head_sums", [CHUNK, NC, HEADS])
    sums_ready, root_done, scaled = sem(name + "_sums_ready"), sem(name + "_root_done"), sem(name + "_scaled")
    gate_done, turned, written = sem(name + "_gate_done"), sem(name + "_turned"), sem(name + "_written")
    with nc.Block() as block:
        @block.scalar
        def _(act):
            act.activation(gateT, gateT, func).then_inc(gate_done, 1)
            act.wait_ge(sums_ready, 1)
            act.activation(ss[:, :, :], ss[:, :, :], ACT.Sqrt).then_inc(root_done, 1)

        @block.vector
        def _(dve):
            go = Steps(dve, sem(name + "_head_step"))
            for c in range(NC):
                o = oTM[0:CHUNK, c, :]
                go(dve.tensor_tensor(sq[:, :], o, o, ALU.mult))
                go(dve.tensor_reduce(ss[:, c, :], sq[:, :].rearrange("p (h v) -> p h v", h=HEADS), AX_X, ALU.add))
            dve.tensor_scalar(ss[:, :, :], ss[:, :, :], 1.0 / DV, EPS, ALU.mult, ALU.add).then_inc(sums_ready, 1)
            dve.wait_ge(root_done, 1)
            go(dve.reciprocal(ss[:, :, :], ss[:, :, :]))
            for c in range(NC):
                o = oTM[0:CHUNK, c, :].rearrange("p (h v) -> p h v", h=HEADS)
                dve.tensor_tensor(o, o, ss[:, c, :].unsqueeze(2).broadcast_to([CHUNK, HEADS, DV]), ALU.mult
                                  ).then_inc(scaled, 1)
            dve.wait_ge(gate_done, 1)
            for t in range(WT):
                dve.wait_ge(turned, t + 1)
                g = gain + t % 2
                dve.scalar_tensor_tensor(out=yT[:, t, :], in0=k.banks[t % 4][:, 0:TOK], scalar=k.vcol[:, g:g + 1],
                                         in1=gateT[:, t, :], op0=ALU.mult, op1=ALU.mult).then_inc(written, 1)

        @block.tensor
        def _(pe):
            pe.wait_ge(scaled, NC)
            for t in range(WT):
                if t >= 4:
                    pe.wait_ge(written, t - 3)
                for c in range(NC):
                    mm = pe.transpose(k.banks[t % 4][:, c * CHUNK:(c + 1) * CHUNK],
                                      oTM[0:CHUNK, c, t * P:(t + 1) * P], k.cst[0:CHUNK, C_ID:C_ID + CHUNK])
                mm.then_inc(turned, 1)


def stage_mlstm(k, ctx, zT):
    nc, io = k.nc, k.io
    rows = k.sb(ctx, "ml_rows", [HEADS, 2, 2, TOK])
    cols = k.sb(ctx, "ml_cols", [CHUNK, 3, 2, NC, HEADS])
    keep = k.sb(ctx, "ml_keep", [P, 2, NC, HEADS])
    state = k.sb(ctx, "ml_state", [P, 2, 2 * HEADS, DV])
    norm = k.sb(ctx, "ml_norm", [P, 2, 2 * HEADS])
    with ExitStack() as pre:
        mlstm_prepare(k, pre, zT, rows, cols, keep, state, norm)
    with ExitStack() as scan:
        oTM = k.sb(scan, "ml_o", [CHUNK, NC, W])
        with ExitStack() as inner:
            mlstm_scan(k, inner, zT, oTM, rows, cols, keep, state, norm)
        with ExitStack() as post:
            stage_heads_out(k, post, "ml", oTM, zT[:, 24:32, :], ACT.Sigmoid, V_MLN, k.yT[2])


def mlstm_prepare(k, ctx, zT, rows, cols, keep, state, norm):
    nc, io, sem = k.nc, k.io, k.sem
    wg = k.sb(ctx, "ml_gate_w", [P, KD, 16])
    bg = k.sb(ctx, "ml_gate_bias", [HEADS, 2, 2, 2])
    gates = k.sb(ctx, "ml_gates", [HEADS, 2, 2, TOK])
    mag = k.sb(ctx, "ml_gate_mag", [HEADS, 2, TOK])
    zero = k.sb(ctx, "ml_zero", [HEADS, CHUNK])
    b = k.sb(ctx, "ml_b", [HEADS, 2, TOK])
    top = k.sb(ctx, "ml_running_max", [HEADS, 2, TOK])
    quant = k.sb(ctx, "ml_quantities", [HEADS, 3, 2, TOK])
    enter = k.sb(ctx, "ml_m_enter", [HEADS, 2, NC])
    leave = k.sb(ctx, "ml_m_leave", [HEADS, 2, NC])
    decay = k.sb(ctx, "ml_decay", [HEADS, 2, NC])
    m0 = k.sb(ctx, "ml_m_start", [HEADS, 2])
    conv = k.sb(ctx, "ml_conv", [P, TOK])
    g_in, state_in, m_stored = sem("ml_gate_in"), sem("ml_state_in"), sem("ml_m_stored")
    g_mm, g_read, soft, m_ready = sem("ml_gate_mm"), sem("ml_gate_read"), sem("ml_softplus"), sem("ml_m_ready")
    exps_ready, exps_done, turned = sem("ml_exps_ready"), sem("ml_exps_done"), sem("ml_cols_turned")
    cols_out = sem("ml_cols_out")

    with nc.Block() as block:
        @block.sync
        def _(sp):
            sp.dma_start(wg[:, :, :], io["w_in"][0].rearrange("(k p) n -> p k n", p=P)[:, :, COL_IF:COL_GATE]
                         ).then_inc(g_in, 16)
            for x in range(2):
                at = COL_IF + x * 2 * HEADS
                sp.dma_start(bg[:, 0, x, :], io["b_in"][0, at:at + 2 * HEADS].rearrange("(d h) -> h d", h=HEADS),
                             allow_slow_non_contiguous=True).then_inc(g_in, 16)
                sp.dma_start(bg[:, 1, x, :], io["ml_gate_b"][0, :, x, :].rearrange("d h -> h d"),
                             allow_slow_non_contiguous=True).then_inc(g_in, 16)
            sp.dma_start(m0[:, :], io["state_mlstm_m"][0, 0].rearrange("d h -> h d"),
                         allow_slow_non_contiguous=True).then_inc(g_in, 16)
            for d in range(2):
                sp.dma_start(state[:, d, :, :], io["state_mlstm_C"][0, 0, d].rearrange("h (j p) v -> p (h j) v", p=P)
                             ).then_inc(state_in, 16)
                sp.dma_start(norm[:, d, :], io["state_mlstm_n"][0, 0, d].rearrange("h (j p) -> p (h j)", p=P),
                             allow_slow_non_contiguous=True).then_inc(state_in, 16)
            sp.wait_ge(state_in, 4 * 16)
            sp.wait_ge(m_ready, 1)
            for d in range(2):
                sp.dma_start(io["new_state_mlstm_m"][0, 0, d].unsqueeze(1), leave[:, d, 1 - d:2 - d],
                             allow_slow_non_contiguous=True).then_inc(m_stored, 16)
            sp.wait_ge(m_stored, 32)

        @block.tensor
        def _(pe):
            pe.wait_ge(g_in, 6 * 16)
            for n in range(4):
                for kk in range(KD):
                    mm = pe.matmul(k.banks[n][0:HEADS, 0:TOK], wg[:, kk, n * HEADS:(n + 1) * HEADS], k.hT[:, kk, :],
                                   start=(kk == 0), stop=(kk == KD - 1))
                mm.then_inc(g_mm, 1)
            pe.wait_ge(exps_done, 3)
            pe.wait_ge(g_read, 4)
            for n in range(3 * 2 * NC):
                q, d, c = n // (2 * NC), n // NC % 2, n % NC
                pe.transpose(k.banks[4][0:CHUNK, n * HEADS:(n + 1) * HEADS],
                             quant[:, q, d, c * CHUNK:(c + 1) * CHUNK], k.cst[0:HEADS, C_ID:C_ID + HEADS])
            for h in range(HEADS):
                mm = pe.matmul(k.banks[5][:, h * 2 * NC:(h + 1) * 2 * NC], k.cst[0:HEADS, C_SEL + h * P:C_SEL + (h + 1) * P],
                               decay[:, :, :].rearrange("h d c -> h (d c)"), start=True, stop=True)
            mm.then_inc(turned, 1)

        @block.scalar
        def _(act):
            act.wait_ge(g_read, 5)
            act.activation(mag[:, :, :], mag[:, :, :], ACT.Exp, scale=-1.0).then_inc(soft, 1)
            act.wait_ge(soft, 1)
            act.activation(mag[:, :, :], mag[:, :, :], ACT.Ln, bias=1.0).then_inc(soft, 1)
            act.wait_ge(exps_ready, 1)
            act.activation(rows[:, 1], rows[:, 1], ACT.Exp).then_inc(exps_done, 1)
            act.activation(quant[:, 1:3], quant[:, 1:3], ACT.Exp).then_inc(exps_done, 1)
            act.activation(decay[:, :, :], decay[:, :, :], ACT.Exp).then_inc(exps_done, 1)

        @block.vector
        def _(dve):
            go = Steps(dve, sem("ml_prepare_step"))
            go(dve.memset(zero[:, :], 0.0))
            dve.wait_ge(g_in, 6 * 16)
            go(dve.tensor_tensor(bg[:, 0], bg[:, 0], bg[:, 1], ALU.add))
            for n in range(4):
                dve.wait_ge(g_mm, n + 1)
                dve.tensor_scalar(gates[:, n // 2, n % 2, :], k.banks[n][0:HEADS, 0:TOK],
                                  bg[:, 0, n // 2, n % 2:n % 2 + 1], None, ALU.add).then_inc(g_read, 1)
            dve.wait_ge(g_read, 4)
            go(dve.tensor_scalar(mag[:, :, :], gates[:, 1], 0.0, None, ALU.min))
            dve.scalar_tensor_tensor(out=mag[:, :, :], in0=mag[:, :, :], scalar=-2.0, in1=gates[:, 1],
                                     op0=ALU.mult, op1=ALU.add).then_inc(g_read, 1)
            dve.wait_ge(g_read, 5)
            go(dve.tensor_scalar(gates[:, 1], gates[:, 1], 0.0, None, ALU.min))
            dve.wait_ge(soft, 2)
            go(dve.tensor_tensor(gates[:, 1], gates[:, 1], mag[:, :, :], ALU.subtract))
            cut = lambda t, d, c: t[:, d, c * CHUNK:(c + 1) * CHUNK][:, ::-1 if d else 1]
            a = quant[:, 0]
            for d in range(2):
                for c in range(NC):
                    go(dve.tensor_tensor_scan(cut(b, d, c), cut(gates[:, 1], d, c), zero[:, :], 0.0,
                                              ALU.add, ALU.add), wait=False)
            go(dve.memset(enter[:, :, :], 0.0))
            go(dve.tensor_tensor(a, gates[:, 0], b[:, :, :], ALU.subtract))
            for d in range(2):
                for c in range(NC):
                    go(dve.tensor_tensor_scan(cut(top, d, c), cut(a, d, c), cut(a, d, c), -3.0e38,
                                              ALU.max, ALU.max), wait=False)
            go(dve.tensor_copy(enter[:, 0, 2:3], m0[:, 0:1]), wait=False)
            go(dve.tensor_copy(enter[:, 1, NC - 1:NC], m0[:, 1:2]))
            mu = rows[:, 0]
            for group in GROUPS:
                for i in range(group[1]):
                    for d in range(2):
                        c = chunk_of(group, i, d)
                        end = c * CHUNK if d else (c + 1) * CHUNK - 1
                        go(dve.tensor_scalar(mu[:, d, c * CHUNK:(c + 1) * CHUNK], top[:, d, c * CHUNK:(c + 1) * CHUNK],
                                             enter[:, d, c:c + 1], None, ALU.max))
                        go(dve.tensor_tensor(leave[:, d, c:c + 1], b[:, d, end:end + 1], mu[:, d, end:end + 1], ALU.add))
                        if i + 1 < group[1]:
                            to = chunk_of(group, i + 1, d)
                            go(dve.tensor_copy(enter[:, d, to:to + 1], leave[:, d, c:c + 1]))
            per = lambda t: t.rearrange("h (c s) -> h c s", s=CHUNK)
            for d in range(2):
                at = 0 if d else CHUNK - 1
                end = per(mu[:, d])[:, :, at:at + 1]
                m = enter[:, d, :].unsqueeze(2)
                go(dve.tensor_tensor(per(rows[:, 1, d]), m.broadcast_to([HEADS, NC, CHUNK]), per(mu[:, d]),
                                     ALU.subtract), wait=False)
                go(dve.scalar_tensor_tensor(out=quant[:, 1, d], in0=b[:, d, :], scalar=-1.0, in1=mu[:, d],
                                            op0=ALU.mult, op1=ALU.subtract), wait=False)
                go(dve.tensor_tensor(per(quant[:, 2, d]), per(a[:, d]), end.broadcast_to([HEADS, NC, CHUNK]),
                                     ALU.subtract), wait=False)
                go(dve.tensor_tensor(decay[:, d, :].unsqueeze(2), m, end, ALU.subtract))
            go(dve.tensor_scalar(mu, mu, -1.0, None, ALU.mult))
            dve.memset(zero[:, :], 0.0).then_inc(exps_ready, 1)
            dve.sem_inc(m_ready, 1)
            dve.wait_ge(turned, 1)
            go(dve.tensor_copy(cols[:, :, :, :, :].rearrange("p q d c h -> p (q d c h)"),
                               k.banks[4][0:CHUNK, 0:3 * 2 * NC * HEADS]), wait=False)
            go(dve.tensor_copy(keep[:, :, :, :].rearrange("p d c h -> p (d c) h"),
                               k.banks[5][:, 0:2 * NC * HEADS].rearrange("p (h n) -> p n h", h=HEADS)), wait=False)
            for part in range(2):
                with dve.Fori(0, WT) as i:
                    go.enter(i, 6)
                    z = zT[:, bass.ds(i + part * WT, 1), :].rearrange("p a t -> p (a t)")
                    last = short_conv(dve, go, conv[:, :], z, lambda tap: k.vcol[
                        :, bass.ds(i + (V_MLCONV + (part * 3 + tap) * WT), 1)])
                    go(last)
                    go(dve.tensor_scalar(z, conv[:, :], 0.0625 if part else 1.0, None, ALU.mult))
                    go.leave(WT)


def mlstm_scan(k, ctx, zT, oTM, rows, cols, keep, state, norm):
    nc, io, sem = k.nc, k.io, k.sem
    two = range(2)
    now = [k.sb(ctx, f"ml_qkv_now{d}", [P, 3 * WT, CHUNK]) for d in two]
    row_now = [k.sb(ctx, f"ml_rows_now{d}", [HEADS, 2, CHUNK]) for d in two]
    q_decayed = [k.sb(ctx, f"ml_q_decayed{d}", [P, 2 * HEADS, CHUNK]) for d in two]
    k_rows = [k.sb(ctx, f"ml_k_rows{d}", [CHUNK, W]) for d in two]
    v_rows = [k.sb(ctx, f"ml_v_rows{d}", [CHUNK, W]) for d in two]
    weight = [k.sb(ctx, f"ml_weight{d}", [CHUNK, HEADS, CHUNK]) for d in two]
    den = [k.sb(ctx, f"ml_den{d}", [CHUNK, 2, HEADS]) for d in two]
    hid = k.sb(ctx, "ml_hidden", [CHUNK, W])
    now_ready, weight_done, v_out = sem("ml_now_ready"), sem("ml_weight_done"), sem("ml_v_out")
    qk_mm, spread_mm, k_turned, v_turned = sem("ml_qk_mm"), sem("ml_spread_mm"), sem("ml_k_turned"), sem("ml_v_turned")
    q_ready, att_ready, k_ready = sem("ml_q_ready"), sem("ml_att_ready"), sem("ml_k_ready")
    o_mm, o_read, state_mm, half_read = sem("ml_o_mm"), sem("ml_o_read"), sem("ml_state_mm"), sem("ml_half_read")
    state_ready, state_stored = sem("ml_state_ready"), sem("ml_state_stored")
    runs = ((GROUPS[1], 0, 0), (GROUPS[0], 2 * GROUPS[1][1], 2 * GROUPS[1][1] + 2))

    with nc.Block() as block:
        @block.scalar
        def _(act):
            for group, q0, s0 in runs:
                with act.Fori(0, group[1]) as i:
                    for d in two:
                        act.wait_ge(state_ready, i * 2 + (s0 + d + 1))
                        at = bass.ds(chunk_of(group, i, d) * CHUNK, CHUNK)
                        act.copy(now[d][:, :, :], zT[:, 0:3 * WT, at]).then_inc(now_ready, 1)
                        act.copy(row_now[d][:, :, :], rows[:, :, d, at]).then_inc(now_ready, 1)
                    for d in two:
                        c = chunk_of(group, i, d)
                        act.wait_ge(qk_mm, i * 2 + (q0 + d + 1))
                        for h in range(HEADS):
                            e = k.banks[0][0:CHUNK, (HEADS + h) * CHUNK:(HEADS + h + 1) * CHUNK]
                            act.activation(weight[d][:, h, :], e, ACT.Exp, bias=cols[:, 0, d, bass.ds(c, 1), h]
                                           ).then_inc(weight_done, 1)
                        for half in two:
                            act.wait_ge(v_turned, i * 4 + (2 * (q0 + d) + half + 1))
                            act.copy(v_rows[d][:, half * 512:(half + 1) * 512], k.banks[7 - 3 * half][0:CHUNK, :]
                                     ).then_inc(v_out, 1)

        @block.tensor
        def _(pe):
            ident = k.cst[:, C_ID:C_ID + P]
            for group, q0, s0 in runs:
                with pe.Fori(0, group[1]) as i:
                    pe.wait_ge(state_ready, i * 2 + (s0 + 2))
                    for d in two:
                        q = i * 2 + (q0 + d)
                        pe.wait_ge(now_ready, q * 2 + 2)
                        pe.wait_ge(att_ready, q)
                        for h in range(HEADS):
                            for j in two:
                                pe.matmul(k.banks[0][0:CHUNK, h * CHUNK:(h + 1) * CHUNK], now[d][:, WT + 2 * h + j, :],
                                          now[d][:, 2 * h + j, :], start=(j == 0), stop=(j == 1))
                        e = k.banks[0][0:CHUNK, HEADS * CHUNK:2 * HEADS * CHUNK]
                        mask = k.cst[0:CHUNK, C_NEG + d * CHUNK:C_NEG + (d + 1) * CHUNK]
                        pe.matmul(e.rearrange("p (h t) -> p h t", h=HEADS), k.cst[0:CHUNK, C_ID:C_ID + CHUNK],
                                  mask.unsqueeze(1).broadcast_to([CHUNK, HEADS, CHUNK]), start=True, stop=False)
                        for h in range(HEADS):
                            sel = C_SEL + h * P
                            mm = pe.matmul(e[:, h * CHUNK:(h + 1) * CHUNK], k.cst[0:HEADS, sel:sel + CHUNK],
                                           row_now[d][:, 0, :], start=False, stop=(h == HEADS - 1))
                        mm.then_inc(qk_mm, 1)
                        pe.wait_ge(q_ready, q)
                        pe.wait_ge(k_ready, q)
                        pe.wait_ge(v_out, q * 2)
                        for h in range(HEADS):
                            mm = pe.matmul(k.banks[1][:, h * CHUNK:(h + 1) * CHUNK],
                                           k.cst[0:HEADS, C_SEL + h * P:C_SEL + (h + 1) * P], row_now[d][:, 1, :],
                                           start=True, stop=True)
                        mm.then_inc(spread_mm, 1)
                        for t in range(WT):
                            mm = pe.transpose(k.banks[5 + t // 4][0:CHUNK, t % 4 * P:(t % 4 + 1) * P],
                                              now[d][:, WT + t, :], ident)
                        mm.then_inc(k_turned, 1)
                        for half in two:
                            for t in range(4):
                                mm = pe.transpose(k.banks[7 - 3 * half][0:CHUNK, t * P:(t + 1) * P],
                                                  now[d][:, 2 * WT + 4 * half + t, :], ident)
                            mm.then_inc(v_turned, 1)
                    for d in two:
                        q = i * 2 + (q0 + d)
                        pe.wait_ge(att_ready, q + 1)
                        pe.wait_ge(q_ready, q + 1)
                        pe.wait_ge(v_out, i * 4 + (2 * q0 + 4))
                        pe.wait_ge(o_read, q)
                        for h in range(HEADS):
                            out = k.banks[2 + h // 2][0:CHUNK, h % 2 * DV:(h % 2 + 1) * DV]
                            for j in two:
                                pe.matmul(out, q_decayed[d][:, 2 * h + j, :], state[:, d, 2 * h + j, :],
                                          start=(j == 0), stop=False)
                            pe.matmul(out, weight[d][:, h, :], v_rows[d][:, h * DV:(h + 1) * DV], start=False, stop=True)
                        for h in range(HEADS):
                            out = k.banks[4][0:CHUNK, h:h + 1]
                            for j in two:
                                pe.matmul(out, q_decayed[d][:, 2 * h + j, :], norm[:, d, 2 * h + j:2 * h + j + 1],
                                          start=(j == 0), stop=False)
                            mm = pe.matmul(out, weight[d][:, h, :], k.cst[0:CHUNK, C_ONE:C_ONE + 1], start=False, stop=True)
                        mm.then_inc(o_mm, 1)
                        pe.wait_ge(k_ready, i * 2 + (q0 + 2))
                        pe.wait_ge(state_ready, i * 2 + (s0 + d + 2))
                        for h in range(HEADS):
                            if h == 2:
                                pe.wait_ge(half_read, q + 1)
                            for j in two:
                                pe.matmul(k.banks[5 + h % 2][:, j * DV:(j + 1) * DV],
                                          k_rows[d][:, (2 * h + j) * P:(2 * h + j + 1) * P],
                                          v_rows[d][:, h * DV:(h + 1) * DV], start=True, stop=True)
                                mm = pe.matmul(k.banks[1][:, 256 + 2 * h + j:257 + 2 * h + j],
                                               k_rows[d][:, (2 * h + j) * P:(2 * h + j + 1) * P],
                                               k.cst[0:CHUNK, C_ONE:C_ONE + 1], start=True, stop=True)
                            if h % 2:
                                mm.then_inc(state_mm, 1)

        @block.vector
        def _(dve):
            go = Steps(dve, sem("ml_scan_step"))
            go(dve.memset(oTM[0:CHUNK, :, :], 0.0))
            dve.sem_inc(state_ready, 2)
            for group, q0, s0 in runs:
                if q0:
                    dve.wait_ge(state_ready, q0 + 2)
                    go(dve.memset(norm[:, :, :], 0.0))
                    dve.memset(state[:, :, :, :], 0.0).then_inc(state_ready, 2)
                    dve.wait_ge(state_ready, q0 + 4)
                with dve.Fori(0, group[1]) as i:
                    go.enter(i, 2 * (1 + 4 + 2 + 7 + 1))
                    for d in two:
                        q = i * 2 + (q0 + d)
                        c = chunk_of(group, i, d)
                        dve.wait_ge(spread_mm, q + 1)
                        spread = k.banks[1][:, 0:HEADS * CHUNK].rearrange("p (h t) -> p h t", h=HEADS)
                        dve.tensor_tensor(q_decayed[d][:, :, :].rearrange("p (h j) t -> p h j t", j=2),
                                          spread.unsqueeze(2).broadcast_to([P, HEADS, 2, CHUNK]),
                                          now[d][:, 0:WT, :].rearrange("p (h j) t -> p h j t", j=2),
                                          ALU.mult).then_inc(q_ready, 1)
                        dve.wait_ge(k_turned, q + 1)
                        for half in two:
                            wk = cols[:, 2, d, bass.ds(c, 1), 2 * half:2 * half + 2].rearrange("p a h -> p (a h)")
                            last = dve.tensor_tensor(
                                k_rows[d][:, half * 512:(half + 1) * 512].rearrange("p (h v) -> p h v", h=2),
                                k.banks[5 + half][0:CHUNK, :].rearrange("p (h v) -> p h v", h=2),
                                wk.unsqueeze(2).broadcast_to([CHUNK, 2, DV]), ALU.mult)
                            if half == 0:
                                go(last, wait=False)
                        last.then_inc(k_ready, 1)
                        dve.wait_ge(weight_done, q * 4 + 4)
                        dve.tensor_tensor(weight[d][:, :, :], k.banks[0][0:CHUNK, 0:HEADS * CHUNK].rearrange(
                            "p (h t) -> p h t", h=HEADS), weight[d][:, :, :], ALU.mult).then_inc(att_ready, 1)
                    for d in two:
                        q = i * 2 + (q0 + d)
                        c = chunk_of(group, i, d)
                        dve.wait_ge(o_mm, q + 1)
                        low, up = den[d][:, 0, :], den[d][:, 1, :]
                        em = cols[:, 1, d, bass.ds(c, 1), :].rearrange("p a h -> p (a h)")
                        go(dve.tensor_copy(low, k.banks[4][0:CHUNK, 0:HEADS]))
                        go(dve.scalar_tensor_tensor(out=up, in0=low, scalar=-1.0, in1=low, op0=ALU.mult, op1=ALU.max))
                        go(dve.tensor_tensor(up, up, em, ALU.max))
                        go(dve.reciprocal(low, up))
                        for half in two:
                            last = dve.tensor_tensor(
                                hid[:, half * 512:(half + 1) * 512].rearrange("p (h v) -> p h v", h=2),
                                k.banks[2 + half][0:CHUNK, :].rearrange("p (h v) -> p h v", h=2),
                                low[:, 2 * half:2 * half + 2].unsqueeze(2).broadcast_to([CHUNK, 2, DV]), ALU.mult)
                            if half == 0:
                                go(last, wait=False)
                        last.then_inc(o_read, 1)
                        dve.wait_ge(o_read, q + 1)
                        o = oTM[0:CHUNK, bass.ds(c, 1), :]
                        go(dve.tensor_tensor(o, o, hid[:, :].unsqueeze(1), ALU.add))
                        for h in range(HEADS):
                            if h % 2 == 0:
                                dve.wait_ge(state_mm, q * 2 + (h // 2 + 1))
                            for j in two:
                                part = dve.scalar_tensor_tensor(
                                    out=state[:, d, 2 * h + j, :], in0=state[:, d, 2 * h + j, :],
                                    scalar=keep[:, d, bass.ds(c, 1), h], in1=k.banks[5 + h % 2][:, j * DV:(j + 1) * DV],
                                    op0=ALU.mult, op1=ALU.add)
                                if (h, j) == (1, 1):
                                    part.then_inc(half_read, 1)
                                else:
                                    go(part, wait=False)
                        n8 = norm[:, d, :].rearrange("p (h j) -> p h j", j=2)
                        kp = keep[:, d, bass.ds(c, 1), :].rearrange("p a h -> p (a h)")
                        go(dve.tensor_tensor(n8, n8, kp.unsqueeze(2).broadcast_to([P, HEADS, 2]), ALU.mult))
                        dve.tensor_tensor(norm[:, d, :], k.banks[1][:, 256:264], norm[:, d, :], ALU.add
                                          ).then_inc(state_ready, 1)
                    go.leave(group[1])

        @block.sync
        def _(sp):
            sp.wait_ge(state_ready, 2 * NC + 4)
            for d in two:
                sp.dma_start(io["new_state_mlstm_C"][0, 0, d].rearrange("h (j p) v -> p (h j) v", p=P),
                             state[:, d, :, :]).then_inc(state_stored, 16)
                sp.dma_start(io["new_state_mlstm_n"][0, 0, d].rearrange("h (j p) -> p (h j)", p=P), norm[:, d, :],
                             allow_slow_non_contiguous=True).then_inc(state_stored, 16)
            sp.wait_ge(state_stored, 64)


def stage_merge(k, ctx):
    nc, io, sem = k.nc, k.io, k.sem
    SLOTS = 2
    wg = [k.sb(ctx, f"merge_gate_w{s}", [P, 3, KD, P]) for s in range(SLOTS)]
    wb = [k.sb(ctx, f"merge_branch_w{s}", [P, 3, WT, P]) for s in range(SLOTS)]
    sig = k.sb(ctx, "merge_sigmoid", [P, 3, TOK])
    tmp = k.sb(ctx, "merge_product", [P, TOK])
    slot_in = [sem(f"merge_w_in{s}") for s in range(SLOTS)]
    g_mm, b_mm, sig_done, prod_done = sem("merge_gate_mm"), sem("merge_branch_mm"), sem("merge_sig_done"), sem("merge_prod_done")
    gate_w = io["w_in"][0][:, COL_GATE:].rearrange("(k p) (b n) -> p b k n", p=P, b=3)
    branch_w = io["w_branch"][0].rearrange("b (k p) n -> p b k n", p=P)

    with nc.Block() as block:
        @block.sync
        def _(sp):
            def load(s, at):
                for b in range(3):
                    sp.dma_start(wg[s][:, b], gate_w[:, b, :, at]).then_inc(slot_in[s], 16)
                    sp.dma_start(wb[s][:, b], branch_w[:, b, :, at]).then_inc(slot_in[s], 16)
            for s in range(SLOTS):
                load(s, slice(s * P, (s + 1) * P))
            with sp.Fori(1, KD // SLOTS) as i:
                for s in range(SLOTS):
                    sp.wait_ge(b_mm, i * (3 * SLOTS) + 3 * (s + 1 - SLOTS))
                    load(s, bass.ds(i * (SLOTS * P) + s * P, P))

        @block.tensor
        def _(pe):
            with pe.Fori(0, KD // SLOTS) as i:
                for s in range(SLOTS):
                    pe.wait_ge(slot_in[s], i * 96 + 96)
                    for b in range(3):
                        done = i * (3 * SLOTS) + (3 * s + b + 1)
                        pe.wait_ge(sig_done, done)
                        for kk in range(KD):
                            mm = pe.matmul(k.banks[b][:, 0:TOK], wg[s][:, b, kk, :], k.hT[:, kk, :],
                                           start=(kk == 0), stop=(kk == KD - 1))
                        mm.then_inc(g_mm, 1)
                        pe.wait_ge(prod_done, done)
                        for kk in range(WT):
                            mm = pe.matmul(k.banks[3 + b][:, 0:TOK], wb[s][:, b, kk, :], k.yT[b][:, kk, :],
                                           start=(kk == 0), stop=(kk == WT - 1))
                        mm.then_inc(b_mm, 1)

        @block.scalar
        def _(act):
            act.sem_inc(sig_done, 3)
            with act.Fori(0, KD // SLOTS) as i:
                for s in range(SLOTS):
                    for b in range(3):
                        done = i * (3 * SLOTS) + (3 * s + b + 1)
                        act.wait_ge(g_mm, done)
                        act.wait_ge(prod_done, done)
                        act.activation(sig[:, b, :], k.banks[b][:, 0:TOK], ACT.Sigmoid,
                                       bias=k.vcol[:, bass.ds(i * SLOTS + (V_GATE + b * KD + s), 1)]
                                       ).then_inc(sig_done, 1)

        @block.vector
        def _(dve):
            go = Steps(dve, sem("merge_step"))
            dve.sem_inc(prod_done, 3)
            with dve.Fori(0, KD // SLOTS) as i:
                go.enter(i, 2 * SLOTS)
                for s in range(SLOTS):
                    out = k.mergedT[:, bass.ds(i * SLOTS + s, 1), :]
                    for b in range(3):
                        done = i * (3 * SLOTS) + (3 * s + b + 1)
                        dve.wait_ge(b_mm, done)
                        dve.wait_ge(sig_done, done + 3)
                        to = out if b == 0 else tmp[:, :].unsqueeze(1)
                        dve.tensor_tensor(to, k.banks[3 + b][:, 0:TOK].unsqueeze(1), sig[:, b:b + 1, :], ALU.mult
                                          ).then_inc(prod_done, 1)
                        dve.wait_ge(prod_done, done + 3)
                        if b:
                            go(dve.tensor_tensor(out, out, tmp[:, :].unsqueeze(1), ALU.add))
                go.leave(KD // SLOTS)


def stage_out(k, ctx):
    nc, io, sem = k.nc, k.io, k.sem
    COLS = 512
    N = D // COLS
    ring = [k.sb(ctx, f"out_w{s}", [P, KD, COLS]) for s in range(2)]
    x = k.sb(ctx, "out_x", [P, TT, D])
    gt = k.sb(ctx, "out_gt", [P, 2, D])
    tmp = k.sb(ctx, "out_product", [P, COLS])
    slot_in = [sem(f"out_w_in{s}") for s in range(2)]
    x_in, mm_done, added, stored = sem("out_x_in"), sem("out_mm"), sem("out_added"), sem("x1_stored")
    w = io["w_out"][0].rearrange("(k p) n -> p k n", p=P)
    with nc.Block() as block:
        @block.sync
        def _(sp):
            for n in range(N):
                if n >= 2:
                    sp.wait_ge(mm_done, TT * (n - 1))
                sp.dma_start(ring[n % 2][:, :, :], w[:, :, n * COLS:(n + 1) * COLS]).then_inc(slot_in[n % 2], 16)
                if n == 0:
                    sp.dma_start(x[:, 0, :], io["x_prompt"][0]).then_inc(x_in, 16)
                    sp.dma_start(x[:, 1:3, :], io["x_sample"][0].rearrange("(t p) d -> p t d", p=P)).then_inc(x_in, 16)
                    for g in range(2):
                        sp.dma_start(gt[:, g, :], k.gt_dram[0, g:g + 1].broadcast_to([P, D])).then_inc(x_in, 16)
            sp.wait_ge(added, TT * N)
            sp.dma_start(k.x1_dram.rearrange("t p d -> p t d"), x[:, :, :]).then_inc(stored, 16)
            sp.wait_ge(stored, 16)

        @block.tensor
        def _(pe):
            for n in range(N):
                pe.wait_ge(slot_in[n % 2], 16 * (n // 2 + 1))
                for t in range(TT):
                    u = TT * n + t
                    if u >= 8:
                        pe.wait_ge(added, u - 7)
                    for kk in range(KD):
                        mm = pe.matmul(k.banks[u % 8][:, :], k.mergedT[:, kk, t * P:(t + 1) * P], ring[n % 2][:, kk, :],
                                       start=(kk == 0), stop=(kk == KD - 1))
                    mm.then_inc(mm_done, 1)

        @block.vector
        def _(dve):
            go = Steps(dve, sem("out_step"))
            dve.wait_ge(x_in, 64)
            for n in range(N):
                for t in range(TT):
                    u = TT * n + t
                    dve.wait_ge(mm_done, u + 1)
                    cols = slice(n * COLS, (n + 1) * COLS)
                    go(dve.tensor_tensor(tmp[:, :], k.banks[u % 8][:, :], gt[:, min(t, 1), cols], ALU.mult))
                    dve.tensor_tensor(x[:, t, cols], x[:, t, cols], tmp[:, :], ALU.add).then_inc(added, 1)
                    dve.wait_ge(added, u + 1)


def stage_queries(k, ctx):
    nc, io, sem = k.nc, k.io, k.sem
    SLOTS, COLS = 4, 256
    TURNS = D // COLS // SLOTS
    PER = SLOTS * COLS // P
    ring = [k.sb(ctx, f"wq{s}", [P, KD, COLS]) for s in range(SLOTS)]
    keys = k.sb(ctx, "keys", [NKEYS, 2 * PEER_H, P])
    keysT = k.sb(ctx, "keysT", [P, 2 * PEER_H, NKEYS])
    qT = [k.sb(ctx, f"queryT{s}", [P, TOK]) for s in range(2)]
    slot_in = [sem(f"wq_in{s}") for s in range(SLOTS)]
    keys_in, keys_turned, keys_out = sem("keys_in"), sem("keys_turned"), sem("keys_out")
    q_mm, q_out, s_mm, s_out = sem("query_mm"), sem("query_out"), sem("score_mm"), sem("score_out")
    h_turned, h_out = sem("h2_turned"), sem("h2_out")
    w = io["peer_wq"][0].rearrange("(k p) n -> p k n", p=P)
    with nc.Block() as block:
        @block.sync
        def _(sp):
            for t in range(2 * PEER_H):
                sp.dma_start(keys[:, t, :], io["peer_keys"][0, t // 2, t % 2]).then_inc(keys_in, 16)
            for s in range(SLOTS):
                sp.dma_start(ring[s][:, :, :], w[:, :, s * COLS:(s + 1) * COLS]).then_inc(slot_in[s], 16)
            with sp.Fori(1, TURNS) as i:
                for s in range(SLOTS):
                    sp.wait_ge(q_mm, i * PER + (2 * (s + 1) - PER))
                    sp.dma_start(ring[s][:, :, :], w[:, :, bass.ds(i * (SLOTS * COLS) + s * COLS, COLS)]
                                 ).then_inc(slot_in[s], 16)

        @block.tensor
        def _(pe):
            ident = k.cst[:, C_ID:C_ID + P]
            for r in range(TT):
                for g in range(4):
                    n = r * 4 + g
                    if n >= 4:
                        pe.wait_ge(h_out, n - 3)
                    for t in range(4):
                        mm = pe.transpose(k.banks[4 + n % 4][:, t * P:(t + 1) * P],
                                          k.hT[:, 4 * g + t, r * P:(r + 1) * P], ident)
                    mm.then_inc(h_turned, 1)
            pe.wait_ge(keys_in, 16 * 2 * PEER_H)
            for n in range(4):
                for t in range(4):
                    mm = pe.transpose(k.banks[n][:, t * P:(t + 1) * P], keys[:, 4 * n + t, :], ident)
                mm.then_inc(keys_turned, 1)
            pe.wait_ge(keys_out, 4)
            pe.wait_ge(h_out, 12)

            def scores(i, j):
                pe.wait_ge(q_out, i * PER + (j + 1))
                pe.wait_ge(s_out, i * PER + (j + 1))
                for r in range(TT):
                    mm = pe.matmul(k.banks[2 + j % 2][:, r * P:(r + 1) * P], qT[j % 2][:, r * P:(r + 1) * P],
                                   keysT[:, bass.ds(i * PER + j, 1), :].rearrange("p a n -> p (a n)"),
                                   start=True, stop=True)
                mm.then_inc(s_mm, 1)
            with pe.Fori(0, TURNS) as i:
                for j in range(PER):
                    s, half = j // 2, j % 2
                    if half == 0:
                        pe.wait_ge(slot_in[s], i * 16 + 16)
                    for kk in range(KD):
                        mm = pe.matmul(k.banks[j % 2][:, 0:TOK], ring[s][:, kk, half * P:(half + 1) * P],
                                       k.hT[:, kk, :], start=(kk == 0), stop=(kk == KD - 1))
                    mm.then_inc(q_mm, 1)
                    if j:
                        scores(i, j - 1)
                scores(i, PER - 1)

        @block.scalar
        def _(act):
            for n in range(12):
                act.wait_ge(h_turned, n + 1)
                act.copy(k.h2[:, n // 4, n % 4 * 512:(n % 4 + 1) * 512], k.banks[4 + n % 4][:, :]).then_inc(h_out, 1)
            for n in range(4):
                act.wait_ge(keys_turned, n + 1)
                act.copy(keysT[:, 4 * n:4 * n + 4, :], k.banks[n][:, :].rearrange("p (t n) -> p t n", t=4)
                         ).then_inc(keys_out, 1)
            with act.Fori(0, TURNS) as i:
                for j in range(PER):
                    act.wait_ge(q_mm, i * PER + (j + 1))
                    act.wait_ge(s_mm, i * PER + j)
                    act.copy(qT[j % 2][:, :], k.banks[j % 2][:, 0:TOK]).then_inc(q_out, 1)

        @block.vector
        def _(dve):
            dve.sem_inc(s_mm, 1)
            dve.sem_inc(s_out, 2)
            with dve.Fori(0, TURNS) as i:
                for j in range(PER):
                    dve.wait_ge(s_mm, i * PER + (j + 2))
                    dve.tensor_copy(k.scores[:, :, bass.ds(i * PER + j, 1), :],
                                    k.banks[2 + j % 2][:, 0:TOK].rearrange("p (r a n) -> p r a n", r=TT, a=1)
                                    ).then_inc(s_out, 1)


def top16(dve, go, waited, values, index, src, rest):
    dve.sem_inc(waited, 1)
    go(dve.max(values[:, 0:8], src))
    dve.sem_inc(waited, 1)
    go(dve.max_index(index[:, 0:8], values[:, 0:8], src), wait=False)
    go(dve.match_replace(rest, values[:, 0:8], src, NEG))
    dve.sem_inc(waited, 1)
    go(dve.max(values[:, 8:16], rest))
    dve.sem_inc(waited, 1)
    go(dve.max_index(index[:, 8:16], values[:, 8:16], rest))


def stage_topk(k, ctx):
    nc, sem = k.nc, k.sem
    now = k.sb(ctx, "scores_now", [P, 2, NKEYS])
    rest = k.sb(ctx, "scores_rest", [P, 256])
    val = k.sb(ctx, "key_values", [P, 2, TOPK])
    ind = k.sb(ctx, "key_index", [P, 2, TOPK], U32)
    indf = k.sb(ctx, "key_index_f", [P, 2, TOPK])
    cand = k.sb(ctx, "candidates", [P, TOPK, TOPK])
    best = k.sb(ctx, "best", [P, TOPK])
    bi = k.sb(ctx, "best_index", [P, TOPK], U32)
    part = k.sb(ctx, "best_parts", [P, 2, TOPK], U32)
    partf = k.sb(ctx, "best_parts_f", [P, 2, TOPK])
    eq = k.sb(ctx, "one_hot", [P, 2, TOPK, TOPK])
    sel = k.sb(ctx, "selected", [P, 2, TOPK])
    neg = k.sb(ctx, "neg_best", [P, 1])
    ex = k.sb(ctx, "best_exp", [P, TOPK])
    tot = k.sb(ctx, "best_sum", [P, 1])
    best_ready, exp_done = sem("best_ready"), sem("best_exp_done")
    N = TT * PEER_H
    scores = k.scores[:, :, :, :].rearrange("p t s n -> p (t s) n")
    with nc.Block() as block:
        @block.vector
        def _(dve):
            go, waited = Steps(dve, sem("topk_step")), sem("topk_waited")
            with dve.Fori(0, N) as i:
                go.enter(i, 1 + 3 * 5 + 11)
                go(dve.tensor_copy(now[:, :, :], scores[:, bass.ds(i * 2, 2), :]))
                for s in range(2):
                    top16(dve, go, waited, val[:, s, :], ind[:, s, :], now[:, s, :], rest[:, s * P:(s + 1) * P])
                go(dve.tensor_tensor(cand[:, :, :], val[:, 0, :].unsqueeze(2).broadcast_to([P, TOPK, TOPK]),
                                     val[:, 1, :].unsqueeze(1).broadcast_to([P, TOPK, TOPK]), ALU.add))
                top16(dve, go, waited, best, bi, cand[:, :, :].rearrange("p a b -> p (a b)"), rest[:, :])
                dve.tensor_scalar(neg[:, :], best[:, 0:1], -1.0, None, ALU.mult).then_inc(best_ready, 1)
                go(dve.tensor_copy(indf[:, :, :], ind[:, :, :]), wait=False)
                go(dve.tensor_scalar(part[:, 0, :], bi[:, :], 4, None, ALU.logical_shift_right), wait=False)
                go(dve.tensor_scalar(part[:, 1, :], bi[:, :], 15, None, ALU.bitwise_and))
                go(dve.tensor_copy(partf[:, :, :], part[:, :, :]))
                iota = k.cst[:, C_IOTA:C_IOTA + TOPK].unsqueeze(1).unsqueeze(1).broadcast_to([P, 2, TOPK, TOPK])
                go(dve.tensor_tensor(eq[:, :, :, :], partf[:, :, :].unsqueeze(3).broadcast_to([P, 2, TOPK, TOPK]), iota,
                                     ALU.is_equal))
                go(dve.tensor_tensor(eq[:, :, :, :], eq[:, :, :, :],
                                     indf[:, :, :].unsqueeze(2).broadcast_to([P, 2, TOPK, TOPK]), ALU.mult))
                go(dve.tensor_reduce(sel[:, :, :], eq[:, :, :, :], AX_X, ALU.add))
                go(dve.scalar_tensor_tensor(out=k.index[:, bass.ds(i, 1), :], in0=sel[:, 0:1, :], scalar=float(NKEYS),
                                            in1=sel[:, 1:2, :], op0=ALU.mult, op1=ALU.add))
                dve.wait_ge(exp_done, i + 1)
                go(dve.reciprocal(tot[:, :], tot[:, :]))
                go(dve.tensor_scalar(k.gate[:, bass.ds(i, 1), :], ex[:, :].unsqueeze(1), tot[:, 0:1], None, ALU.mult))
                go.leave(N)

        @block.scalar
        def _(act):
            with act.Fori(0, N) as i:
                act.wait_ge(best_ready, i + 1)
                act.activation(ex[:, :], best[:, :], ACT.Exp, bias=neg[:, 0:1], accum_out=tot[:, 0:1]
                               ).then_inc(exp_done, 1)


def stage_experts(k, ctx):
    nc, io, sem = k.nc, k.io, k.sem
    R = 8
    u = [k.sb(ctx, f"u_rows{s}", [P, D]) for s in range(R)]
    v = [k.sb(ctx, f"v_rows{s}", [P, D]) for s in range(R)]
    idx = [k.sb(ctx, f"index_now{s}", [P, TOPK], U32) for s in range(2)]
    dots = k.sb(ctx, "dots", [P, TOPK])
    wgt = k.sb(ctx, "weights", [P, TOPK])
    u_in, v_in = [sem(f"u_in{s}") for s in range(R)], [sem(f"v_in{s}") for s in range(R)]
    idx_ready, dot_done, gelu_done, w_ready, acc_done = (
        sem("index_now_ready"), sem("dot_done"), sem("gelu_done"), sem("weights_ready"), sem("acc_done"))
    zeroed, slot_free = sem("acc_zeroed"), sem("gather_slot_free")
    u_tab, v_tab = io["peer_u"][0], io["peer_v"][0]
    N = TT * PEER_H

    with nc.Block() as block:
        @block.gpsimd
        def _(pool):
            with pool.Fori(0, N // 2) as i:
                for odd in range(2):
                    pool.wait_ge(w_ready, i * 2 + odd)
                    pool.tensor_copy(idx[odd][:, :].unsqueeze(1), k.index[:, bass.ds(i * 2 + odd, 1), :]
                                     ).then_inc(idx_ready, 1)
                    pool.wait_ge(idx_ready, i * 2 + (odd + 1))
                    for tab, ring, arrived, used in ((u_tab, u, u_in, dot_done), (v_tab, v, v_in, acc_done)):
                        for n in range(TOPK):
                            pool.wait_ge(used, i * (2 * TOPK) + (odd * TOPK + n + 1))
                            pool.sem_inc(slot_free, 1)
                            pool.indirect_dma_start(
                                out=ring[n % R][:, :], out_offset=None, in_=tab,
                                in_offset=bass.IndirectOffsetOnAxis(ap=idx[odd][:, n:n + 1], axis=0)
                                ).then_inc(arrived[n % R], 16)

        @block.vector
        def _(dve):
            dve.memset(k.acc[:, :, :], 0.0).then_inc(zeroed, 1)
            dve.wait_ge(zeroed, 1)
            dve.sem_inc(dot_done, R)
            dve.sem_inc(acc_done, R)
            with dve.Fori(0, TT) as t:
                with dve.Fori(0, PEER_H) as h:
                    i = t * PEER_H + h
                    row = k.h2[:, bass.ds(t, 1), :]
                    acc = k.acc[:, bass.ds(t, 1), :]
                    for n in range(TOPK):
                        dve.wait_ge(u_in[n % R], i * 32 + 16 * (n // R + 1))
                        dve.scalar_tensor_tensor(out=u[n % R][:, :].unsqueeze(1), in0=u[n % R][:, :].unsqueeze(1), scalar=1.0,
                                                 in1=row, op0=ALU.mult, op1=ALU.mult, accum_out=dots[:, n:n + 1]
                                                 ).then_inc(dot_done, 1)
                    dve.wait_ge(gelu_done, i + 1)
                    dve.tensor_tensor(wgt[:, :].unsqueeze(1), wgt[:, :].unsqueeze(1), k.gate[:, bass.ds(i, 1), :], ALU.mult
                                      ).then_inc(w_ready, 1)
                    dve.wait_ge(w_ready, i + 1)
                    for n in range(TOPK):
                        dve.wait_ge(v_in[n % R], i * 32 + 16 * (n // R + 1))
                        dve.wait_ge(acc_done, i * TOPK + (n + R))
                        dve.scalar_tensor_tensor(out=acc, in0=v[n % R][:, :].unsqueeze(1), scalar=wgt[:, n:n + 1],
                                                 in1=acc, op0=ALU.mult, op1=ALU.add).then_inc(acc_done, 1)

        @block.scalar
        def _(act):
            with act.Fori(0, N) as i:
                act.wait_ge(dot_done, i * TOPK + (TOPK + R))
                act.wait_ge(acc_done, i * TOPK + R)
                act.activation(wgt[:, :], dots[:, :], ACT.Gelu_apprx_tanh).then_inc(gelu_done, 1)


def stage_final(k, ctx):
    nc, io, sem = k.nc, k.io, k.sem
    x = k.sb(ctx, "final_x", [P, TT, D])
    gt = k.sb(ctx, "final_gt", [P, 2, D])
    gain = k.sb(ctx, "final_gain", [P, D])
    junk = k.sb(ctx, "final_squares", [P, D])
    ss = k.sb(ctx, "final_sums", [P, TT])
    x_in, added, squared, rms, root, done, stored = (
        sem("final_" + n) for n in ("x_in", "added", "squared", "rms", "root", "done", "stored"))
    with nc.Block() as block:
        @block.sync
        def _(sp):
            sp.dma_start(x[:, :, :], k.x1_dram.rearrange("t p d -> p t d")).then_inc(x_in, 16)
            for g in range(2):
                sp.dma_start(gt[:, g, :], k.gt_dram[1, g:g + 1].broadcast_to([P, D])).then_inc(x_in, 16)
            sp.dma_start(gain[:, :], io["final_g"].unsqueeze(0).broadcast_to([P, D])).then_inc(x_in, 16)
            sp.wait_ge(done, 1)
            sp.dma_start(io["y_prompt"][0], x[:, 0, :]).then_inc(stored, 16)
            sp.wait_ge(done, 3)
            sp.dma_start(io["y_sample"][0].rearrange("(t p) d -> p t d", p=P), x[:, 1:3, :]).then_inc(stored, 16)
            sp.wait_ge(stored, 32)

        @block.vector
        def _(dve):
            go = Steps(dve, sem("final_step"))
            dve.wait_ge(x_in, 64)
            for t in range(TT):
                go(dve.tensor_tensor(k.acc[:, t, :], k.acc[:, t, :], gt[:, min(t, 1), :], ALU.mult))
                dve.tensor_tensor(x[:, t, :], x[:, t, :], k.acc[:, t, :], ALU.add).then_inc(added, 1)
            dve.wait_ge(squared, TT)
            dve.tensor_scalar(ss[:, :], ss[:, :], 1.0 / D, EPS, ALU.mult, ALU.add).then_inc(rms, 1)
            dve.wait_ge(root, 1)
            go(dve.reciprocal(ss[:, :], ss[:, :]))
            for t in range(TT):
                dve.scalar_tensor_tensor(out=x[:, t, :], in0=x[:, t, :], scalar=ss[:, t:t + 1], in1=gain[:, :],
                                         op0=ALU.mult, op1=ALU.mult).then_inc(done, 1)

        @block.scalar
        def _(act):
            for t in range(TT):
                act.wait_ge(added, t + 1)
                act.activation(junk[:, :], x[:, t, :], ACT.Square, accum_out=ss[:, t:t + 1]).then_inc(squared, 1)
                act.wait_ge(squared, t + 1)
            act.wait_ge(rms, 1)
            act.activation(ss[:, :], ss[:, :], ACT.Sqrt).then_inc(root, 1)


_INS = ['x_prompt', 'x_sample', 'c', 'state_gla', 'state_mlstm_C', 'state_mlstm_n', 'state_mlstm_m', 'c_ctx',
        'mod_w', 'mod_b', 'norm1_g', 'norm2_g', 'final_g', 'w_in', 'b_in', 'hy_conv', 'hy_w1', 'hy_b1', 'hy_w2',
        'hy_b2', 'hy_w3', 'hy_freq', 'hy_bias', 'gla_a2_w', 'gla_a2_b', 'gla_norm_g', 'ml_conv', 'ml_gate_b',
        'ml_norm_g', 'w_branch', 'w_out', 'peer_wq', 'peer_keys', 'peer_u', 'peer_v']
_OUTS = {'y_prompt': (1, 128, 2048), 'y_sample': (1, 256, 2048), 'new_state_gla': (1, 1, 2, 4, 128, 256),
         'new_state_mlstm_C': (1, 1, 2, 4, 256, 256), 'new_state_mlstm_n': (1, 1, 2, 4, 256),
         'new_state_mlstm_m': (1, 1, 2, 4)}


def kernel(**inputs):
    import concourse.bacc as _bacc
    from concourse.bass_utils import run_bass_kernel_spmd as _run

    nc = _bacc.Bacc("TRN2", target_bir_lowering=False, num_devices=1)
    arrays, io = {}, {}
    for name, a in [(n, np.ascontiguousarray(inputs[n])) for n in _INS] + list(shape_constants().items()):
        arrays["in_" + name] = a
        io[name] = nc.dram_tensor("in_" + name, a.shape, mybir.dt.from_np(a.dtype), kind="ExternalInput").ap()
    for name, shape in _OUTS.items():
        io[name] = nc.dram_tensor("out_" + name, shape, F32, kind="ExternalOutput").ap()
    build(nc, io)
    r = _run(nc, [arrays], core_ids=[0])
    return tuple(r.results[0]["out_" + name] for name in _OUTS)
```

```python
from contextlib import ExitStack
import math

import numpy as np

import concourse.bass as bass
from concourse import mybir

ALU = mybir.AluOpType
ACT = mybir.ActivationFunctionType
AX_X = mybir.AxisListType.X
F32 = mybir.dt.float32
U32 = mybir.dt.uint32

P = 128
D = 2048
KD = D // P
PROMPT, SAMPLE = 128, 256
TOK = PROMPT + SAMPLE
TT = TOK // P
CHUNK = 64
NC = TOK // CHUNK
GROUPS = ((0, 2), (2, 4))
EPS = 1e-6
W = 1024
WT = W // P
HEADS = 4
DK, DV = 128, 256
SUB = 16
NSUB = CHUNK // SUB
MAX_EXP = 50.0
NEG = -1.0e30
COL_HY, COL_GLA, COL_LR, COL_ML, COL_IF, COL_GATE = 0, 3072, 6144, 6176, 10272, 10288
PEER_H, NKEYS, TOPK = 8, 128, 16
MAGIC = 12582912.0
TWO_PI_HI = 6.28125
TWO_PI_LO = 2.0 * math.pi - TWO_PI_HI
PI_IN = 3.1415925

C_ID = 0
C_TRI = 128
C_GMASK = C_TRI + 2 * P
C_NEG = C_GMASK + 2 * CHUNK
C_SEL = C_NEG + 2 * CHUNK
C_IOTA = C_SEL + 4 * P
C_ONE = C_IOTA + NKEYS
C_ZERO = C_ONE + 1
C_END = C_ZERO + 1
V_HY, V_GLA, V_ML, V_GATE = 0, 24, 48, 80
V_HYCONV, V_MLCONV = 128, 128 + 72
V_N1, V_N2, V_GLAN, V_MLN = 256, 272, 288, 290


def shape_constants():
    c = np.zeros((P, C_END), np.float32)
    c[:, C_ID:C_ID + P] = np.eye(P)
    t = np.arange(P)
    same = (t[:, None] // CHUNK) == (t[None, :] // CHUNK)
    c[:, C_TRI:C_TRI + P] = (same & (t[:, None] <= t[None, :])) / 16.0
    c[:, C_TRI + P:C_TRI + 2 * P] = (same & (t[:, None] >= t[None, :])) / 16.0
    s = np.arange(CHUNK)
    fwd = s[:, None] <= s[None, :]
    bwd = s[:, None] >= s[None, :]
    for n, m in enumerate((fwd, bwd)):
        c[:CHUNK, C_GMASK + n * CHUNK:C_GMASK + (n + 1) * CHUNK] = m
        c[:CHUNK, C_NEG + n * CHUNK:C_NEG + (n + 1) * CHUNK] = np.where(m, 0.0, NEG)
    for h in range(HEADS):
        c[h, C_SEL + h * P:C_SEL + (h + 1) * P] = 1.0
    c[:, C_IOTA:C_IOTA + NKEYS] = np.arange(NKEYS)
    c[:, C_ONE] = 1.0
    out = {"cst": c}
    for name, n in (("p", PROMPT), ("s", SAMPLE)):
        k = np.arange(n)
        ang = np.pi * ((2 * k[None, :] + 1) * k[:, None] % (4 * n)) / (2 * n)
        mats = np.stack([np.cos(ang), np.sin(ang), np.cos(ang).T / n, np.sin(ang).T / n])
        out["dft_" + name] = np.ascontiguousarray(
            mats.reshape(4, n // P, P, n).transpose(2, 0, 1, 3)).astype(np.float32)
        t = np.arange(n, dtype=np.float32)
        tn = t / np.float32(n - 1)
        bands = np.linspace(1e-4, 15, 16, dtype=np.float32)
        an = (np.float32(2.0 * math.pi / n) * t[:, None] * bands[None, :]).astype(np.float32)
        z = np.concatenate([tn[:, None], np.cos(an), -np.sin(an)], -1)
        out["feat_" + name] = np.ascontiguousarray(z.T).astype(np.float32)
        lo, hi = math.log(1e-2) / 1.5, math.log(1e-2) / 0.3
        deltas = np.abs(np.linspace(lo, hi, W, dtype=np.float32))
        win = np.exp(-tn[:, None] * deltas[None, :]).astype(np.float32)
        out["win_" + name] = np.ascontiguousarray(win.reshape(n // P, P, W).transpose(1, 0, 2))
    return out


class Steps:

    def __init__(self, eng, sem):
        self.eng, self.sem, self.n, self.base = eng, sem, 0, 0

    def __call__(self, ins, wait=True):
        self.n += 1
        ins.then_inc(self.sem, 1)
        if wait:
            self.eng.wait_ge(self.sem, self.base + self.n)

    def enter(self, turn, per):
        self.before, self.base, self.n = self.n, turn * per + self.n, 0
        self.per = per

    def leave(self, turns):
        assert self.n == self.per, (self.n, self.per)
        self.base, self.n = 0, self.before + turns * self.per


class Core:
    pass


def build(nc, io, upto=99):
    k = Core()
    k.nc, k.io = nc, io
    with ExitStack() as top:
        k.banks = [top.enter_context(nc.psum_tensor(f"bank{i}", [P, 512], F32)) for i in range(8)]

        handles = []

        def sem(name):
            handles.append(nc.alloc_semaphore(name=name))
            return handles[-1]

        def clear_semaphores():
            with nc.Block() as block:
                @block.gpsimd
                def _(pool):
                    for s in handles:
                        pool.sem_clear(s)
            for s in handles:
                nc.release_semaphore(s)
            handles.clear()

        def sb(ctx, name, shape, dt=F32):
            return ctx.enter_context(nc.sbuf_tensor(name, shape, dt))

        k.sem, k.sb = sem, sb
        k.cst = sb(top, "cst", [P, C_END])
        k.vcol = sb(top, "vcol", [P, 3 * P])
        k.h2cols = sb(top, "h2cols", [P, 2, KD, 2])
        k.gt_dram = nc.dram_tensor("gt_rows", (2, 2, D), F32, kind="Internal").ap()
        k.x1_dram = nc.dram_tensor("x1_rows", (TT, P, D), F32, kind="Internal").ap()
        k.sums_dram = nc.dram_tensor("sample_sum_columns", (2, 8, P, 2 * SAMPLE), F32, kind="Internal").ap()
        with ExitStack() as mix:
            k.hT = sb(mix, "hT", [P, KD, TOK])
            k.h1cols = sb(mix, "h1cols", [P, 2, KD, 2])
            with ExitStack() as ctx:
                stage_modulation(k, ctx)
            with ExitStack() as ctx:
                stage_norm(k, ctx, 1)
            if upto < 2: return
            k.yT = [sb(mix, "yT_hyena", [P, WT, TOK])]
            with ExitStack() as ctx:
                k.uTM = sb(ctx, "hyena_rows", [P, 3, TT, W])
                with ExitStack() as in1:
                    zT = sb(in1, "z_hyena", [P, 24, TOK])
                    with ExitStack() as in2:
                        stage_project(k, in2, "hy", COL_HY, V_HY, zT, 24)
                    with ExitStack() as in2:
                        stage_hyena_rows(k, in2, zT)
                if upto < 3: return
                k.dft = {"p": sb(ctx, "dft_prompt", [P, 4, 1, PROMPT]),
                         "s": sb(ctx, "dft_sample", [P, 4, 2, SAMPLE])}
                k.spec = sb(ctx, "filter_spectra", [P, 3, 2, 2, W])
                with ExitStack() as in1:
                    stage_filters(k, in1)
                with ExitStack() as in1:
                    stage_hyena(k, in1)
            if upto < 4: return
            k.yT.append(sb(mix, "yT_gla", [P, WT, TOK]))
            with ExitStack() as ctx:
                zT = sb(ctx, "z_gla", [P, 24, TOK])
                k.lrT = sb(ctx, "low_rank", [17, 2, TOK])
                with ExitStack() as in1:
                    stage_project(k, in1, "gla", COL_GLA, V_GLA, zT, 24)
                with ExitStack() as in1:
                    stage_gla(k, in1, zT)
            if upto < 5: return
            k.yT.append(sb(mix, "yT_mlstm", [P, WT, TOK]))
            with ExitStack() as ctx:
                zT = sb(ctx, "z_mlstm", [P, 32, TOK])
                with ExitStack() as in1:
                    stage_project(k, in1, "ml", COL_ML, V_ML, zT, 32)
                with ExitStack() as in1:
                    stage_mlstm(k, in1, zT)
            if upto < 6: return
            clear_semaphores()
            k.mergedT = sb(mix, "mergedT", [P, KD, TOK])
            with ExitStack() as ctx:
                stage_merge(k, ctx)
            with ExitStack() as ctx:
                stage_out(k, ctx)
        if upto < 7: return
        with ExitStack() as tail:
            k.h1cols = k.h2cols
            sample_heads = (TT - 1) * PEER_H
            k.index = sb(tail, "expert_index", [P, TT * PEER_H, TOPK], U32)
            k.gate = sb(tail, "expert_gate", [P, TT * PEER_H, TOPK])
            k.pairs = sb(tail, "expert_pairs", [P, 2, sample_heads, TOPK])
            k.weight = sb(tail, "expert_weight", [P, sample_heads, TOPK])
            k.h2_prompt = sb(tail, "h2_prompt_rows", [P, D])
            k.scores_prompt = sb(tail, "prompt_scores", [P, 2 * PEER_H, NKEYS])
            topk = TopK(k, tail)
            with ExitStack() as sample:
                k.h2_sample = sb(sample, "h2_sample_rows", [P, TT - 1, D])
                k.scores_sample = sb(sample, "sample_scores", [P, 2 * sample_heads, NKEYS])
                with ExitStack() as ctx:
                    k.hT = sb(ctx, "h2T", [P, KD, TOK])
                    with ExitStack() as in1:
                        stage_norm(k, in1, 2)
                    if upto < 8: return
                    with ExitStack() as in1:
                        stage_queries(k, in1)
                with ExitStack() as ctx:
                    stage_sample_dots(k, ctx, topk)
            if upto < 9: return
            k.acc = sb(tail, "prompt_expert_sum", [P, D])
            with ExitStack() as ctx:
                stage_experts(k, ctx, topk)
            with ExitStack() as ctx:
                stage_final(k, ctx)


def stage_modulation(k, ctx):
    nc, io, sem = k.nc, k.io, k.sem
    SLOTS, COLS = 3, 512
    TURNS = 6 * D // COLS // SLOTS
    ring = [k.sb(ctx, f"mod_w{s}", [P, KD, COLS]) for s in range(SLOTS)]
    rows = k.sb(ctx, "mod_rows", [2, 6 * D])
    bias = k.sb(ctx, "mod_bias", [2, 6 * D // 2])
    vrow = k.sb(ctx, "vector_rows", [P, 3, P])
    cT = k.sb(ctx, "cT", [P, KD, 2])
    const_in, vec_in, c_in, bias_in = sem("const_in"), sem("vec_in"), sem("c_in"), sem("mod_bias_in")
    slot_in = [sem(f"mod_w_in{s}") for s in range(SLOTS)]
    silu_done, part_done, part_out = sem("silu_done"), sem("mod_part_done"), sem("mod_part_out")
    zeroed, vec_turned, vec_out = sem("vec_zeroed"), sem("vec_turned"), sem("vec_out")
    mod_turned, gt_stored = sem("mod_turned"), sem("gt_stored")
    w = io["mod_w"][0].rearrange("(k p) n -> p k n", p=P)
    b_in = io["b_in"][0]

    with nc.Block() as block:
        @block.sync
        def _(sp):
            sp.dma_start(cT[:, :, 0], io["c_ctx"].rearrange("(k p) -> p k", p=P),
                         allow_slow_non_contiguous=True).then_inc(c_in, 16)
            sp.dma_start(cT[:, :, 1], io["c"][0].rearrange("(k p) -> p k", p=P),
                         allow_slow_non_contiguous=True).then_inc(c_in, 16)
            for s in range(SLOTS):
                sp.dma_start(ring[s][:, :, :], w[:, :, s * COLS:(s + 1) * COLS]).then_inc(slot_in[s], 16)
            with sp.Fori(1, TURNS) as i:
                for s in range(SLOTS):
                    sp.wait_ge(part_done, i * SLOTS + (s + 1 - SLOTS))
                    sp.dma_start(ring[s][:, :, :], w[:, :, bass.ds(i * (SLOTS * COLS) + s * COLS, COLS)]
                                 ).then_inc(slot_in[s], 16)

        @block.scalar
        def _(act):
            half = 3 * D
            act.dma_start(k.cst[:, :], io["cst"]).then_inc(const_in, 16)
            act.dma_start(bias[:, :], io["mod_b"][:, 0:half].broadcast_to([2, half])).then_inc(bias_in, 16)
            act.wait_ge(zeroed, 1)
            act.dma_start(vrow[0:48, 0, :], b_in[0:COL_LR].rearrange("(r c) -> r c", c=P)).then_inc(vec_in, 16)
            act.dma_start(vrow[48:80, 0, :], b_in[COL_ML:COL_IF].rearrange("(r c) -> r c", c=P)).then_inc(vec_in, 16)
            act.dma_start(vrow[80:128, 0, :], b_in[COL_GATE:].rearrange("(r c) -> r c", c=P)).then_inc(vec_in, 16)
            act.dma_start(vrow[0:72, 1, :], io["hy_conv"][0].rearrange("a b (r c) -> (a b r) c", c=P)).then_inc(vec_in, 16)
            act.dma_start(vrow[72:120, 1, :], io["ml_conv"][0].rearrange("a b (r c) -> (a b r) c", c=P)).then_inc(vec_in, 16)
            act.dma_start(vrow[0:16, 2, :], io["norm1_g"][0].rearrange("(r c) -> r c", c=P)).then_inc(vec_in, 16)
            act.dma_start(vrow[16:32, 2, :], io["norm2_g"][0].rearrange("(r c) -> r c", c=P)).then_inc(vec_in, 16)
            act.dma_start(vrow[32:34, 2, :], io["gla_norm_g"][0].rearrange("(r c) -> r c", c=P)).then_inc(vec_in, 16)
            act.dma_start(vrow[34:36, 2, :], io["ml_norm_g"][0].rearrange("(r c) -> r c", c=P)).then_inc(vec_in, 16)
            act.wait_ge(c_in, 32)
            act.activation(cT[:, :, :], cT[:, :, :], ACT.Silu).then_inc(silu_done, 1)
            act.wait_ge(part_out, SLOTS + TURNS * SLOTS // 2)
            act.dma_start(bias[:, :], io["mod_b"][:, half:].broadcast_to([2, half])).then_inc(bias_in, 16)
            act.wait_ge(part_out, SLOTS + TURNS * SLOTS)
            act.dma_start(k.gt_dram[0], rows[:, 2 * D:3 * D]).then_inc(gt_stored, 16)
            act.dma_start(k.gt_dram[1], rows[:, 5 * D:6 * D]).then_inc(gt_stored, 16)
            act.wait_ge(gt_stored, 32)

        @block.tensor
        def _(pe):
            pe.wait_ge(const_in, 16)
            pe.wait_ge(vec_in, 9 * 16)
            ident = k.cst[:, C_ID:C_ID + P]
            for n in range(3):
                last = pe.transpose(k.banks[7][:, n * P:(n + 1) * P], vrow[:, n, :], ident)
            last.then_inc(vec_turned, 1)
            pe.wait_ge(silu_done, 1)
            with pe.Fori(0, TURNS) as i:
                for s in range(SLOTS):
                    pe.wait_ge(slot_in[s], i * 16 + 16)
                    pe.wait_ge(part_out, i * SLOTS + (s + 1))
                    for kk in range(KD):
                        last = pe.matmul(k.banks[s][0:2, :], cT[:, kk, :], ring[s][:, kk, :],
                                         start=(kk == 0), stop=(kk == KD - 1))
                    last.then_inc(part_done, 1)
            pe.wait_ge(part_out, SLOTS + TURNS * SLOTS)
            for n, part in enumerate((0, 1, 3, 4)):
                for t in range(KD):
                    at = part * D + t * P
                    last = pe.transpose(k.banks[6][:, (n * KD + t) * 2:(n * KD + t) * 2 + 2],
                                        rows[:, at:at + P], k.cst[0:2, C_ID:C_ID + 2])
            last.then_inc(mod_turned, 1)

        @block.vector
        def _(dve):
            dve.memset(vrow[:, :, :], 0.0).then_inc(zeroed, 1)
            dve.sem_inc(part_out, SLOTS)
            dve.wait_ge(vec_turned, 1)
            dve.tensor_copy(k.vcol[:, :], k.banks[7][:, 0:3 * P]).then_inc(vec_out, 1)
            for half in range(2):
                dve.wait_ge(bias_in, 16 * (half + 1))
                n = TURNS // 2
                with dve.Fori(0, n) as i:
                    for s in range(SLOTS):
                        dve.wait_ge(part_done, i * SLOTS + (half * n * SLOTS + s + 1))
                        dve.tensor_tensor(
                            rows[:, bass.ds(i * (SLOTS * COLS) + (half * n * SLOTS + s) * COLS, COLS)],
                            k.banks[s][0:2, :], bias[:, bass.ds(i * (SLOTS * COLS) + s * COLS, COLS)],
                            ALU.add).then_inc(part_out, 1)
            dve.wait_ge(vec_out, 1)
            dve.wait_ge(mod_turned, 1)
            cols = k.banks[6][:, 0:4 * KD * 2].rearrange("p (n t g) -> p n t g", n=4, t=KD)
            for n, (dst, v) in enumerate(((k.h1cols, V_N1), (k.h2cols, V_N2))):
                gain = k.vcol[:, v:v + KD].unsqueeze(2).broadcast_to([P, KD, 2])
                dve.scalar_tensor_tensor(out=dst[:, 0, :, :], in0=cols[:, 2 * n + 1], scalar=1.0, in1=gain,
                                         op0=ALU.add, op1=ALU.mult).then_inc(vec_out, 1)
                dve.tensor_copy(dst[:, 1, :, :], cols[:, 2 * n]).then_inc(vec_out, 1)


def stage_norm(k, ctx, which):
    nc, io, sem = k.nc, k.io, k.sem
    x = k.sb(ctx, f"norm{which}_x", [P, TT, D])
    junk = k.sb(ctx, f"norm{which}_squares", [P, D])
    ss = k.sb(ctx, f"norm{which}_sums", [P, TT])
    x_in, squared, root, scaled = (sem(f"norm{which}_{n}") for n in ("x_in", "squared", "root", "scaled"))
    turned, written, rms = sem(f"norm{which}_turned"), sem(f"norm{which}_written"), sem(f"norm{which}_rms")

    with nc.Block() as block:
        @block.sync
        def _(sp):
            if which == 1:
                sp.dma_start(x[:, 0, :], io["x_prompt"][0]).then_inc(x_in, 16)
                sp.dma_start(x[:, 1:3, :], io["x_sample"][0].rearrange("(t p) d -> p t d", p=P)).then_inc(x_in, 16)
            else:
                sp.dma_start(x[:, :, :], k.x1_dram.rearrange("t p d -> p t d")).then_inc(x_in, 32)

        @block.scalar
        def _(act):
            act.wait_ge(x_in, 32)
            for t in range(TT):
                act.activation(junk[:, :], x[:, t, :], ACT.Square, accum_out=ss[:, t:t + 1]).then_inc(squared, 1)
                act.wait_ge(squared, t + 1)
            act.wait_ge(rms, 1)
            act.activation(ss[:, :], ss[:, :], ACT.Sqrt).then_inc(root, 1)
            act.wait_ge(rms, 2)
            for t in range(TT):
                act.activation(x[:, t, :], x[:, t, :], ACT.Copy, scale=ss[:, t:t + 1]).then_inc(scaled, 1)

        @block.tensor
        def _(pe):
            for t in range(KD):
                for r in range(TT):
                    pe.wait_ge(scaled, r + 1)
                    if t >= 4:
                        pe.wait_ge(written, 2 * (t - 3))
                    last = pe.transpose(k.banks[t % 4][:, r * P:(r + 1) * P], x[:, r, t * P:(t + 1) * P],
                                        k.cst[:, C_ID:C_ID + P])
                last.then_inc(turned, 1)

        @block.vector
        def _(dve):
            dve.wait_ge(squared, TT)
            dve.tensor_scalar(ss[:, :], ss[:, :], 1.0 / D, EPS, ALU.mult, ALU.add).then_inc(rms, 1)
            dve.wait_ge(root, 1)
            dve.reciprocal(ss[:, :], ss[:, :]).then_inc(rms, 1)
            for t in range(KD):
                dve.wait_ge(turned, t + 1)
                for g, (a, b) in enumerate(((0, PROMPT), (PROMPT, TOK))):
                    dve.tensor_scalar(k.hT[:, t, a:b], k.banks[t % 4][:, a:b], k.h1cols[:, 0, t, g:g + 1],
                                      k.h1cols[:, 1, t, g:g + 1], ALU.mult, ALU.add).then_inc(written, 1)


def stage_project(k, ctx, name, col0, v0, zT, tiles):
    nc, io, sem = k.nc, k.io, k.sem
    SLOTS, COLS, BANKS = 4, 256, 4
    TURNS = tiles * P // COLS // SLOTS
    PER = SLOTS * COLS // P
    ring = [k.sb(ctx, f"{name}_w{s}", [P, KD, COLS]) for s in range(SLOTS)]
    slot_in = [sem(f"{name}_w_in{s}") for s in range(SLOTS)]
    tile_done, tile_out = sem(f"{name}_tile_done"), sem(f"{name}_tile_out")
    w = io["w_in"][0].rearrange("(k p) n -> p k n", p=P)

    with nc.Block() as block:
        @block.sync
        def _(sp):
            for s in range(SLOTS):
                at = col0 + s * COLS
                sp.dma_start(ring[s][:, :, :], w[:, :, at:at + COLS]).then_inc(slot_in[s], 16)
            with sp.Fori(1, TURNS) as i:
                for s in range(SLOTS):
                    sp.wait_ge(tile_done, i * PER + (2 * (s + 1) - PER))
                    sp.dma_start(ring[s][:, :, :], w[:, :, bass.ds(i * (SLOTS * COLS) + (col0 + s * COLS), COLS)]
                                 ).then_inc(slot_in[s], 16)

        @block.tensor
        def _(pe):
            with pe.Fori(0, TURNS) as i:
                for j in range(PER):
                    s, half = j // 2, j % 2
                    if half == 0:
                        pe.wait_ge(slot_in[s], i * 16 + 16)
                    pe.wait_ge(tile_out, i * PER + (j + 1))
                    for kk in range(KD):
                        last = pe.matmul(k.banks[j % BANKS][:, 0:TOK], ring[s][:, kk, half * P:(half + 1) * P],
                                         k.hT[:, kk, :], start=(kk == 0), stop=(kk == KD - 1))
                    last.then_inc(tile_done, 1)

        @block.scalar
        def _(act):
            act.sem_inc(tile_out, BANKS)
            with act.Fori(0, TURNS) as i:
                for j in range(PER):
                    act.wait_ge(tile_done, i * PER + (j + 1))
                    act.activation(zT[:, bass.ds(i * PER + j, 1), :], k.banks[j % BANKS][:, 0:TOK].unsqueeze(1),
                                   ACT.Identity, bias=k.vcol[:, bass.ds(i * PER + (v0 + j), 1)]
                                   ).then_inc(tile_out, 1)


def short_conv(dve, go, out, z, wcol):
    go(dve.tensor_scalar(out, z, wcol(1), None, ALU.mult))
    for tap in (0, 2):
        for a, b, n in ((0, PROMPT, PROMPT), (PROMPT, TOK, CHUNK)):
            o = out[:, a:b].rearrange("p (r c) -> p r c", c=n)
            i = z[:, a:b].rearrange("p (r c) -> p r c", c=n)
            o, i = (o[:, :, 1:], i[:, :, :-1]) if tap == 0 else (o[:, :, :-1], i[:, :, 1:])
            last = dve.scalar_tensor_tensor(out=o, in0=i, scalar=wcol(tap), in1=o, op0=ALU.mult, op1=ALU.add)
            if tap == 0 or a == 0:
                go(last)
    return last


def stage_hyena_rows(k, ctx, zT):
    nc, sem = k.nc, k.sem
    conv = [k.sb(ctx, f"hy_conv{s}", [P, TOK]) for s in range(2)]
    conv_done, conv_turned, rows_out = sem("hy_conv_done"), sem("hy_conv_turned"), sem("hy_rows_out")
    with nc.Block() as block:
        @block.vector
        def _(dve):
            go = Steps(dve, sem("hy_conv_step"))
            for part in range(3):
                with dve.Fori(0, WT // 2) as i:
                    go.enter(i, 8)
                    for s in range(2):
                        dve.wait_ge(conv_turned, i * 2 + (part * WT + s + 1))
                        def wcol(tap, s=s):
                            return k.vcol[:, bass.ds(i * 2 + (V_HYCONV + (part * 3 + tap) * WT + s), 1)]
                        z = zT[:, bass.ds(i * 2 + (part * WT + s), 1), :].rearrange("p a t -> p (a t)")
                        short_conv(dve, go, conv[s][:, :], z, wcol).then_inc(conv_done, 1)
                    go.leave(WT // 2)

        @block.tensor
        def _(pe):
            pe.sem_inc(conv_turned, 2)
            with pe.Fori(0, 3 * WT // 2) as i:
                for s in range(2):
                    pe.wait_ge(conv_done, i * 2 + (s + 1))
                    pe.wait_ge(rows_out, i * 2 + (s + 1))
                    for r in range(TT):
                        last = pe.transpose(k.banks[s][:, r * P:(r + 1) * P], conv[s][:, r * P:(r + 1) * P],
                                            k.cst[:, C_ID:C_ID + P])
                    last.then_inc(conv_turned, 1)

        @block.scalar
        def _(act):
            act.sem_inc(rows_out, 2)
            for part in range(3):
                with act.Fori(0, WT // 2) as i:
                    for s in range(2):
                        act.wait_ge(conv_turned, i * 2 + (part * WT + s + 3))
                        act.copy(k.uTM[:, part, :, bass.ds(i * (2 * P) + s * P, P)],
                                 k.banks[s][:, 0:TOK].rearrange("p (r c) -> p r c", c=P)).then_inc(rows_out, 1)


def stage_filters(k, ctx):
    nc, io, sem = k.nc, k.io, k.sem
    w1 = k.sb(ctx, "ffn_w1", [33, 64])
    w2 = k.sb(ctx, "ffn_w2", [64, 64])
    w3 = k.sb(ctx, "ffn_w3", [64, 4 * W])
    feat = k.sb(ctx, "features", [33, TOK])
    cols = k.sb(ctx, "ffn_cols", [64, 4])
    win = k.sb(ctx, "window", [P, TT, W])
    bias = k.sb(ctx, "lag0_bias", [1, 2, W])
    hid = [k.sb(ctx, f"hidden{n}", [64, TOK]) for n in range(2)]
    turns = k.sb(ctx, "turns", [64, TOK])
    fw, bw = k.sb(ctx, "filter_fwd", [P, W]), k.sb(ctx, "filter_bwd", [P, W])
    both = k.sb(ctx, "filter_sum_diff", [P, 2, 2, W])
    ffn_in, filt_in = sem("ffn_in"), sem("filter_in")
    hid_mm, arg_ready, hid_ready = sem("hidden_mm"), sem("sin_argument"), sem("hidden_ready")
    filt_mm, filt_read, filt_ready = sem("filter_mm"), sem("filter_read"), sem("filter_ready")
    spec_mm, spec_out = sem("spectrum_mm"), sem("spectrum_out")
    combos = [(name, o) for name in "ps" for o in range(2)]
    first, count = {"p": 0, "s": 1}, {"p": 1, "s": 2}

    with nc.Block() as block:
        @block.sync
        def _(sp):
            sp.dma_start(w1[:, :], io["hy_w1"][0]).then_inc(ffn_in, 16)
            sp.dma_start(w2[:, :], io["hy_w2"][0]).then_inc(ffn_in, 16)
            sp.dma_start(feat[:, 0:PROMPT], io["feat_p"]).then_inc(ffn_in, 16)
            sp.dma_start(feat[:, PROMPT:], io["feat_s"]).then_inc(ffn_in, 16)
            sp.dma_start(cols[:, 0:1], io["hy_b1"][0].unsqueeze(1)).then_inc(ffn_in, 16)
            sp.dma_start(cols[:, 1:2], io["hy_b2"][0].unsqueeze(1)).then_inc(ffn_in, 16)
            sp.dma_start(cols[:, 2:3], io["hy_freq"][0, 0].unsqueeze(1)).then_inc(ffn_in, 16)
            sp.dma_start(cols[:, 3:4], io["hy_freq"][0, 1].unsqueeze(1)).then_inc(ffn_in, 16)
            sp.dma_start(w3[:, :], io["hy_w3"][0]).then_inc(filt_in, 16)
            sp.dma_start(win[:, 0:1, :], io["win_p"]).then_inc(filt_in, 16)
            sp.dma_start(win[:, 1:3, :], io["win_s"]).then_inc(filt_in, 16)
            sp.dma_start(bias[:, :, :], io["hy_bias"]).then_inc(filt_in, 16)
            sp.dma_start(k.dft["p"][:, :, :, :], io["dft_p"]).then_inc(filt_in, 16)
            sp.dma_start(k.dft["s"][:, :, :, :], io["dft_s"]).then_inc(filt_in, 16)

        @block.tensor
        def _(pe):
            pe.wait_ge(ffn_in, 8 * 16)
            pe.matmul(k.banks[0][0:64, 0:TOK], w1[:, :], feat[:, :], start=True, stop=True).then_inc(hid_mm, 1)
            pe.wait_ge(hid_ready, 1)
            pe.matmul(k.banks[0][0:64, 0:TOK], w2[:, :], hid[0][:, :], start=True, stop=True).then_inc(hid_mm, 1)
            pe.wait_ge(hid_ready, 2)
            pe.wait_ge(filt_in, 6 * 16)
            tile, spec = 0, 0
            for n, (name, o) in enumerate(combos):
                for t in range(count[name]):
                    if tile:
                        pe.wait_ge(filt_read, tile)
                    at = (first[name] + t) * P
                    for b in range(4):
                        last = pe.matmul(k.banks[b][:, :], hid[1][:, at:at + P],
                                         w3[:, o * 2 * W + b * 512:o * 2 * W + (b + 1) * 512],
                                         start=True, stop=True)
                    last.then_inc(filt_mm, 1)
                    tile += 1
                pe.wait_ge(filt_ready, n + 1)
                dft = k.dft[name]
                for m in range(count[name]):
                    for part in range(2):
                        for half in range(2):
                            if spec >= 4:
                                pe.wait_ge(spec_out, spec - 3)
                            for t in range(count[name]):
                                last = pe.matmul(k.banks[4 + spec % 4][:, :], dft[:, part, t, m * P:(m + 1) * P],
                                                 both[:, t, part, half * 512:(half + 1) * 512],
                                                 start=(t == 0), stop=(t == count[name] - 1))
                            last.then_inc(spec_mm, 1)
                            spec += 1

        @block.scalar
        def _(act):
            for n in range(2):
                act.wait_ge(arg_ready, n + 1)
                act.activation(hid[n][:, :], hid[n][:, :], ACT.Sin).then_inc(hid_ready, 1)
            spec = 0
            for name, o in combos:
                for m in range(count[name]):
                    for part in range(2):
                        for half in range(2):
                            act.wait_ge(spec_mm, spec + 1)
                            act.copy(k.spec[:, first[name] + m, o, part, half * 512:(half + 1) * 512],
                                     k.banks[4 + spec % 4][:, :]).then_inc(spec_out, 1)
                            spec += 1

        @block.vector
        def _(dve):
            go = Steps(dve, sem("filter_step"))
            dve.wait_ge(ffn_in, 8 * 16)
            for n in range(2):
                dve.wait_ge(hid_mm, n + 1)
                go(dve.tensor_scalar(hid[n][:, :], k.banks[0][0:64, 0:TOK], cols[:, n:n + 1], cols[:, 2 + n:3 + n],
                                     ALU.add, ALU.mult))
                go(dve.tensor_scalar(turns[:, :], hid[n][:, :], 1.0 / (2.0 * math.pi), MAGIC, ALU.mult, ALU.add))
                go(dve.tensor_scalar(turns[:, :], turns[:, :], MAGIC, None, ALU.subtract))
                go(dve.scalar_tensor_tensor(out=hid[n][:, :], in0=turns[:, :], scalar=-TWO_PI_HI, in1=hid[n][:, :],
                                            op0=ALU.mult, op1=ALU.add))
                go(dve.scalar_tensor_tensor(out=hid[n][:, :], in0=turns[:, :], scalar=-TWO_PI_LO, in1=hid[n][:, :],
                                            op0=ALU.mult, op1=ALU.add))
                dve.tensor_scalar(hid[n][:, :], hid[n][:, :], PI_IN, -PI_IN, ALU.min, ALU.max).then_inc(arg_ready, 1)
            dve.wait_ge(filt_in, 6 * 16)
            tile, spec = 0, 0
            for n, (name, o) in enumerate(combos):
                if spec:
                    dve.wait_ge(spec_mm, spec)
                for t in range(count[name]):
                    dve.wait_ge(filt_mm, tile + 1)
                    for b in range(4):
                        dst = (fw, bw)[b // 2][:, b % 2 * 512:(b % 2 + 1) * 512]
                        last = dve.tensor_tensor(dst, k.banks[b][:, :],
                                                 win[:, first[name] + t, b % 2 * 512:(b % 2 + 1) * 512], ALU.mult)
                        if b < 3:
                            go(last, wait=False)
                    last.then_inc(filt_read, 1)
                    tile += 1
                    dve.wait_ge(filt_read, tile)
                    if t == 0:
                        go(dve.tensor_tensor(fw[0:1, :], fw[0:1, :], bias[:, o, :], ALU.add))
                        go(dve.memset(bw[0:1, :], 0.0))
                    go(dve.tensor_tensor(both[:, t, 0, :], fw[:, :], bw[:, :], ALU.add))
                    last = dve.tensor_tensor(both[:, t, 1, :], fw[:, :], bw[:, :], ALU.subtract)
                    if t == count[name] - 1:
                        last.then_inc(filt_ready, 1)
                        dve.wait_ge(filt_ready, n + 1)
                    else:
                        go(last)
                spec += 4 * count[name]


def stage_hyena(k, ctx):
    nc, sem = k.nc, k.sem
    uf = k.sb(ctx, "u_spectrum", [P, TT, 2, W])
    yf = k.sb(ctx, "y_spectrum", [P, TT, 2, W])
    tmp = k.sb(ctx, "product", [P, W])
    u_mm, u_out, y_ready = sem("u_mm"), sem("u_out"), sem("y_spectrum_ready")
    y_mm, rows_ready = sem("y_mm"), sem("hy_rows_ready")
    y_turned, y_stored = sem("hy_y_turned"), sem("hy_y_stored")
    units = [(g, o) for o in range(2) for g in "ps"]
    tiles = {"p": (0,), "s": (1, 2)}
    first = {"p": 0, "s": 1}
    H = lambda half: slice(half * 512, (half + 1) * 512)
    rows = k.uTM[:, 2]

    with nc.Block() as block:
        @block.tensor
        def _(pe):
            u = y = 0
            for o in range(2):
                for g in "ps":
                    if o:
                        pe.wait_ge(rows_ready, 2 * (first[g] + len(tiles[g])))
                    for m in tiles[g]:
                        for part in range(2):
                            for half in range(2):
                                if u >= 4:
                                    pe.wait_ge(u_out, u - 3)
                                for t in tiles[g]:
                                    mt = (m - first[g]) * P
                                    last = pe.matmul(k.banks[u % 4][:, :],
                                                     k.dft[g][:, part, t - first[g], mt:mt + P],
                                                     rows[:, t, H(half)], start=(t == tiles[g][0]),
                                                     stop=(t == tiles[g][-1]))
                                last.then_inc(u_mm, 1)
                                u += 1
                for g in "ps":
                    pe.wait_ge(y_ready, TT * o + first[g] + len(tiles[g]))
                    for t in tiles[g]:
                        for half in range(2):
                            if y >= 4:
                                pe.wait_ge(rows_ready, y - 3)
                            for part in range(2):
                                for m in tiles[g]:
                                    tt = (t - first[g]) * P
                                    last = pe.matmul(k.banks[4 + y % 4][:, :],
                                                     k.dft[g][:, 2 + part, m - first[g], tt:tt + P],
                                                     yf[:, m, part, H(half)],
                                                     start=(part == 0 and m == tiles[g][0]),
                                                     stop=(part == 1 and m == tiles[g][-1]))
                            last.then_inc(y_mm, 1)
                            y += 1
            pe.wait_ge(rows_ready, 4 * TT)
            for c in range(WT):
                if c >= 4:
                    pe.wait_ge(y_stored, c - 3)
                for t in range(TT):
                    last = pe.transpose(k.banks[c % 4][:, t * P:(t + 1) * P], rows[:, t, c * P:(c + 1) * P],
                                        k.cst[:, C_ID:C_ID + P])
                last.then_inc(y_turned, 1)

        @block.scalar
        def _(act):
            u = 0
            for o in range(2):
                for m in range(TT):
                    if o:
                        act.wait_ge(y_ready, m + 1)
                    for part in range(2):
                        for half in range(2):
                            act.wait_ge(u_mm, u + 1)
                            act.copy(uf[:, m, part, H(half)], k.banks[u % 4][:, :]).then_inc(u_out, 1)
                            u += 1
            for c in range(WT):
                act.wait_ge(y_turned, c + 1)
                act.copy(k.yT[0][:, c, :], k.banks[c % 4][:, 0:TOK]).then_inc(y_stored, 1)

        @block.vector
        def _(dve):
            go = Steps(dve, sem("hyena_step"))
            y = 0
            for o in range(2):
                for m in range(TT):
                    dve.wait_ge(u_out, 4 * (TT * o + m + 1))
                    if o:
                        dve.wait_ge(y_mm, 2 * TT)
                    ur, us = uf[:, m, 0, :], uf[:, m, 1, :]
                    hr, hs = k.spec[:, m, o, 0, :], k.spec[:, m, o, 1, :]
                    go(dve.tensor_tensor(yf[:, m, 0, :], ur, hr, ALU.mult), wait=False)
                    go(dve.tensor_tensor(tmp[:, :], us, hs, ALU.mult))
                    go(dve.tensor_tensor(yf[:, m, 0, :], yf[:, m, 0, :], tmp[:, :], ALU.subtract))
                    go(dve.tensor_tensor(yf[:, m, 1, :], ur, hs, ALU.mult), wait=False)
                    go(dve.tensor_tensor(tmp[:, :], us, hr, ALU.mult))
                    dve.tensor_tensor(yf[:, m, 1, :], yf[:, m, 1, :], tmp[:, :], ALU.add).then_inc(y_ready, 1)
                    dve.wait_ge(y_ready, TT * o + m + 1)
                for t in range(TT):
                    for half in range(2):
                        dve.wait_ge(y_mm, y + 1)
                        dve.tensor_tensor(rows[:, t, H(half)], k.banks[4 + y % 4][:, :], k.uTM[:, o, t, H(half)],
                                          ALU.mult).then_inc(rows_ready, 1)
                        y += 1


def chunk_of(group, turn, backward):
    first, count = group
    return turn * -1 + (first + count - 1) if backward else turn + first


def stage_gla(k, ctx, zT):
    nc, io, sem = k.nc, k.io, k.sem
    vTM = k.sb(ctx, "gla_v", [CHUNK, NC, W])
    oTM = k.sb(ctx, "gla_o", [P, NC, W])
    b = k.sb(ctx, "gla_cumulated", [P, 2, HEADS, TOK])
    state = k.sb(ctx, "gla_state", [P, 2, HEADS, DV])
    with ExitStack() as pre:
        gla_prepare(k, pre, zT, vTM, oTM, b, state)
    with ExitStack() as scan:
        gla_scan(k, scan, zT, vTM, oTM, b, state)
    with ExitStack() as post:
        stage_heads_out(k, post, "gla", oTM, zT[:, 16:24, :], ACT.Silu, V_GLAN, k.yT[1])


def rows_of_v(pe, act, k, zT, tile0, vTM, turned, out, banks):
    for n in range(NC * 2):
        if n >= len(banks):
            pe.wait_ge(out, n + 1 - len(banks))
        c, g = n // 2, n % 2
        for t in range(4):
            last = pe.transpose(banks[n % len(banks)][0:CHUNK, t * P:(t + 1) * P],
                                zT[:, tile0 + 4 * g + t, c * CHUNK:(c + 1) * CHUNK], k.cst[:, C_ID:C_ID + P])
        last.then_inc(turned, 1)


def gla_prepare(k, ctx, zT, vTM, oTM, b, state):
    nc, io, sem = k.nc, k.io, k.sem
    wlr = k.sb(ctx, "lr_w", [P, KD, 32])
    blr = k.sb(ctx, "lr_bias", [16, 2])
    a2 = k.sb(ctx, "gla_a2", [17, 2, HEADS * DK])
    lg = k.sb(ctx, "log_gate", [P, TT, 2, HEADS * DK])
    mag = oTM[:, 0:3, :].rearrange("p c (d n) -> p c d n", d=2)
    lr_in, v_turned, v_out = sem("lr_in"), sem("gla_v_turned"), sem("gla_v_out")
    lr_mm, lr_ready, x_mm, x_read = sem("lr_mm"), sem("lr_ready"), sem("gate_mm"), sem("gate_read")
    soft, lg_ready, sum_mm, sum_out = sem("softplus_done"), sem("log_gate_ready"), sem("cumsum_mm"), sem("cumsum_out")

    with nc.Block() as block:
        @block.sync
        def _(sp):
            sp.dma_start(wlr[:, :, :], io["w_in"][0].rearrange("(k p) n -> p k n", p=P)[:, :, COL_LR:COL_ML]
                         ).then_inc(lr_in, 16)
            sp.dma_start(blr[:, :], io["b_in"][0, COL_LR:COL_ML].rearrange("(d r) -> r d", d=2),
                         allow_slow_non_contiguous=True).then_inc(lr_in, 16)
            sp.dma_start(a2[0:16, :, :], io["gla_a2_w"][0].rearrange("d r n -> r d n")).then_inc(lr_in, 16)
            sp.dma_start(a2[16:17, :, :], io["gla_a2_b"]).then_inc(lr_in, 16)
            sp.dma_start(state[:, :, :, :], io["state_gla"][0, 0].rearrange("d h p v -> p d h v")).then_inc(lr_in, 16)
            sp.wait_ge(lr_in, 5 * 16)

        @block.tensor
        def _(pe):
            rows_of_v(pe, None, k, zT, 8, vTM, v_turned, v_out, k.banks[4:8])
            pe.wait_ge(lr_in, 5 * 16)
            for d in range(2):
                for kk in range(KD):
                    last = pe.matmul(k.banks[d][0:16, 0:TOK], wlr[:, kk, 16 * d:16 * d + 16], k.hT[:, kk, :],
                                     start=(kk == 0), stop=(kk == KD - 1))
                last.then_inc(lr_mm, 1)
            pe.wait_ge(lr_ready, 2)
            for n in range(2 * TT):
                t, d = n // 2, n % 2
                if n >= 4:
                    pe.wait_ge(x_read, n - 3)
                pe.matmul(k.banks[n % 4][:, :], k.lrT[:, d, t * P:(t + 1) * P], a2[:, d, :],
                          start=True, stop=True).then_inc(x_mm, 1)
            pe.wait_ge(lg_ready, 1)
            pe.wait_ge(v_out, NC * 2)
            for n in range(2 * HEADS):
                d, h = n // HEADS, n % HEADS
                if n >= 4:
                    pe.wait_ge(sum_out, n - 3)
                for t in range(TT):
                    last = pe.matmul(k.banks[4 + n % 4][:, t * P:(t + 1) * P], lg[:, t, d, h * DK:(h + 1) * DK],
                                     k.cst[:, C_TRI + d * P:C_TRI + (d + 1) * P], start=True, stop=True)
                last.then_inc(sum_mm, 1)

        @block.scalar
        def _(act):
            for n in range(NC * 2):
                act.wait_ge(v_turned, n + 1)
                act.copy(vTM[:, n // 2, n % 2 * 512:(n % 2 + 1) * 512], k.banks[4 + n % 4][0:CHUNK, :]).then_inc(v_out, 1)
            act.wait_ge(x_read, 2 * TT)
            act.activation(mag, mag, ACT.Exp, scale=-1.0).then_inc(soft, 1)
            act.wait_ge(soft, 1)
            act.activation(mag, mag, ACT.Ln, bias=1.0).then_inc(soft, 1)
            for n in range(2 * HEADS):
                act.wait_ge(sum_mm, n + 1)
                act.copy(b[:, n // HEADS, n % HEADS, :], k.banks[4 + n % 4][:, 0:TOK]).then_inc(sum_out, 1)

        @block.vector
        def _(dve):
            go = Steps(dve, sem("gla_prepare_step"))
            dve.memset(k.lrT[:, :, :], 1.0).then_inc(lr_ready, 1)
            dve.wait_ge(lr_ready, 1)
            dve.wait_ge(lr_in, 5 * 16)
            for d in range(2):
                dve.wait_ge(lr_mm, d + 1)
                last = dve.tensor_scalar(k.lrT[0:16, d, :], k.banks[d][0:16, 0:TOK], blr[:, d:d + 1], None, ALU.add)
            last.then_inc(lr_ready, 1)
            for n in range(2 * TT):
                dve.wait_ge(x_mm, n + 1)
                go(dve.tensor_scalar(lg[:, n // 2, n % 2, :], k.banks[n % 4][:, :], 0.0, None, ALU.min))
                dve.scalar_tensor_tensor(out=mag[:, n // 2, n % 2, :], in0=lg[:, n // 2, n % 2, :], scalar=-2.0,
                                         in1=k.banks[n % 4][:, :], op0=ALU.mult, op1=ALU.add).then_inc(x_read, 1)
            dve.wait_ge(x_read, 2 * TT)
            dve.wait_ge(soft, 2)
            dve.tensor_tensor(lg[:, :, :, :], lg[:, :, :, :], mag, ALU.subtract).then_inc(lg_ready, 1)


def gla_scan(k, ctx, zT, vTM, oTM, b, state):
    nc, io, sem = k.nc, k.io, k.sem
    sub_k = [k.sb(ctx, f"gla_sub_k{d}", [P, NSUB, HEADS, CHUNK]) for d in range(2)]
    e3 = [k.sb(ctx, f"gla_e3{d}", [P, 3, HEADS, CHUNK]) for d in range(2)]
    att = [k.sb(ctx, f"gla_att{d}", [CHUNK, HEADS, CHUNK]) for d in range(2)]
    k_rows = [k.sb(ctx, f"gla_k_rows{d}", [CHUNK, HEADS * DK]) for d in range(2)]
    end = [k.sb(ctx, f"gla_end{d}", [P, HEADS]) for d in range(2)]
    v_now = [k.sb(ctx, f"gla_v_now{d}", [CHUNK, W]) for d in range(2)]
    v_ready = sem("gla_v_ready")
    diff_ready, exp_done, prep_done = sem("gla_diff_ready"), sem("gla_exp_done"), sem("gla_prep_done")
    att_mm, att_ready, k_turned, k_out = sem("gla_att_mm"), sem("gla_att_ready"), sem("gla_k_turned"), sem("gla_k_out")
    o_mm, o_read, state_mm, state_ready = sem("gla_o_mm"), sem("gla_o_read"), sem("gla_state_mm"), sem("gla_state_ready")
    state_stored = sem("gla_state_stored")
    runs = ((GROUPS[1], 0, 0), (GROUPS[0], 2 * GROUPS[1][1], 2 * GROUPS[1][1] + 2))
    qs = DK ** -0.5

    def toks(group, i, d):
        return bass.ds(chunk_of(group, i, d) * CHUNK, CHUNK)

    with nc.Block() as block:
        @block.vector
        def _(dve):
            go = Steps(dve, sem("gla_step"))
            go(dve.memset(oTM[0:CHUNK, :, :], 0.0))
            dve.sem_inc(state_ready, 2)
            for group, q0, s0 in runs:
                if q0:
                    dve.wait_ge(state_mm, q0)
                    dve.wait_ge(state_ready, q0 + 2)
                    dve.memset(state[:, :, :, :], 0.0).then_inc(state_ready, 2)
                    dve.wait_ge(state_ready, q0 + 4)
                with dve.Fori(0, group[1]) as i:
                    go.enter(i, 2 * (3 + 4 + 3))
                    for d in range(2):
                        q = i * 2 + (q0 + d)
                        bc = b[:, d, :, toks(group, i, d)]
                        qc, kc = zT[:, 0:4, toks(group, i, d)], zT[:, 4:8, toks(group, i, d)]
                        sub = bc.rearrange("p h (i s) -> p i h s", s=SUB)
                        ref = sub[:, :, :, SUB // 2:SUB // 2 + 1].broadcast_to([P, NSUB, HEADS, CHUNK])
                        dif = sub_k[d]
                        go(dve.tensor_tensor(dif[:, :, :, :], ref, bc.unsqueeze(1).broadcast_to([P, NSUB, HEADS, CHUNK]),
                                             ALU.subtract))
                        go(dve.tensor_scalar(dif[:, :, :, :], dif[:, :, :, :], MAX_EXP, None, ALU.min), wait=False)
                        own = bc.rearrange("p h (i s) -> p h i s", s=SUB)
                        go(dve.tensor_tensor(e3[d][:, 0].rearrange("p h (i s) -> p h i s", s=SUB), own,
                                             own[:, :, :, SUB // 2:SUB // 2 + 1].broadcast_to([P, HEADS, NSUB, SUB]),
                                             ALU.subtract), wait=False)
                        last = bc[:, :, 0:1] if d else bc[:, :, CHUNK - 1:CHUNK]
                        dve.tensor_tensor(e3[d][:, 1], last.broadcast_to([P, HEADS, CHUNK]), bc, ALU.subtract
                                          ).then_inc(diff_ready, 1)
                    for d in range(2):
                        q = i * 2 + (q0 + d)
                        qc, kc = zT[:, 0:4, toks(group, i, d)], zT[:, 4:8, toks(group, i, d)]
                        dve.wait_ge(exp_done, q * 3 + 3)
                        at = 0 if d else CHUNK - 1
                        go(dve.tensor_copy(end[d][:, :].unsqueeze(2), e3[d][:, 2, :, at:at + 1]))
                        go(dve.tensor_tensor(sub_k[d][:, :, :, :], sub_k[d][:, :, :, :],
                                             kc.unsqueeze(1).broadcast_to([P, NSUB, HEADS, CHUNK]), ALU.mult), wait=False)
                        go(dve.scalar_tensor_tensor(out=e3[d][:, 0], in0=e3[d][:, 0], scalar=qs, in1=qc,
                                                    op0=ALU.mult, op1=ALU.mult), wait=False)
                        go(dve.tensor_tensor(e3[d][:, 1], e3[d][:, 1], kc, ALU.mult), wait=False)
                        dve.scalar_tensor_tensor(out=e3[d][:, 2], in0=e3[d][:, 2], scalar=qs, in1=qc,
                                                 op0=ALU.mult, op1=ALU.mult).then_inc(prep_done, 1)
                    for d in range(2):
                        q = i * 2 + (q0 + d)
                        dve.wait_ge(att_mm, q + 1)
                        mask = k.cst[0:CHUNK, C_GMASK + d * CHUNK:C_GMASK + (d + 1) * CHUNK]
                        dve.tensor_tensor(att[d][:, :, :], k.banks[d][0:CHUNK, 0:HEADS * CHUNK].rearrange(
                            "p (h t) -> p h t", h=HEADS), mask.unsqueeze(1).broadcast_to([CHUNK, HEADS, CHUNK]),
                            ALU.mult).then_inc(att_ready, 1)
                    for d in range(2):
                        q = i * 2 + (q0 + d)
                        dve.wait_ge(o_mm, q + 1)
                        for half in range(2):
                            o = oTM[0:CHUNK, bass.ds(chunk_of(group, i, d), 1), half * 512:(half + 1) * 512]
                            add = dve.tensor_tensor(o, k.banks[4 + half][0:CHUNK, :].unsqueeze(1), o, ALU.add)
                        add.then_inc(o_read, 1)
                        dve.wait_ge(state_mm, q + 1)
                        for h in range(HEADS):
                            part = dve.scalar_tensor_tensor(
                                out=state[:, d, h, :], in0=state[:, d, h, :], scalar=end[d][:, h:h + 1],
                                in1=k.banks[6 + h // 2][:, h % 2 * DV:(h % 2 + 1) * DV], op0=ALU.mult, op1=ALU.add)
                            if h < HEADS - 1:
                                go(part, wait=False)
                        part.then_inc(state_ready, 1)
                    go.leave(group[1])

        @block.scalar
        def _(act):
            for group, q0, s0 in runs:
                with act.Fori(0, group[1]) as i:
                    for d in range(2):
                        q = i * 2 + (q0 + d)
                        act.wait_ge(diff_ready, q + 1)
                        act.activation(sub_k[d][:, :, :, :], sub_k[d][:, :, :, :], ACT.Exp).then_inc(exp_done, 1)
                        act.activation(e3[d][:, 0:2], e3[d][:, 0:2], ACT.Exp).then_inc(exp_done, 1)
                        act.activation(e3[d][:, 2], b[:, d, :, toks(group, i, d)], ACT.Exp).then_inc(exp_done, 1)
                    for d in range(2):
                        act.wait_ge(k_turned, i * 2 + (q0 + d + 1))
                        act.copy(k_rows[d][:, :], k.banks[2 + d][0:CHUNK, :]).then_inc(k_out, 1)
                    for d in range(2):
                        act.wait_ge(state_ready, i * 2 + (s0 + d + 1))
                        act.copy(v_now[d][:, :].unsqueeze(1), vTM[:, bass.ds(chunk_of(group, i, d), 1), :]
                                 ).then_inc(v_ready, 1)

        @block.tensor
        def _(pe):
            for group, q0, s0 in runs:
                with pe.Fori(0, group[1]) as i:
                    for d in range(2):
                        q = i * 2 + (q0 + d)
                        pe.wait_ge(prep_done, q + 1)
                        for h in range(HEADS):
                            for s in range(NSUB):
                                at = h * CHUNK + s * SUB
                                mm = pe.matmul(k.banks[d][0:CHUNK, at:at + SUB], sub_k[d][:, s, h, :],
                                               e3[d][:, 0, h, s * SUB:(s + 1) * SUB], start=True, stop=True)
                        mm.then_inc(att_mm, 1)
                        for h in range(HEADS):
                            mm = pe.transpose(k.banks[2 + d][0:CHUNK, h * DK:(h + 1) * DK], e3[d][:, 1, h, :],
                                              k.cst[:, C_ID:C_ID + P])
                        mm.then_inc(k_turned, 1)
                    for d in range(2):
                        q = i * 2 + (q0 + d)
                        v = lambda h: v_now[d][:, h * DV:(h + 1) * DV]
                        pe.wait_ge(att_ready, q + 1)
                        pe.wait_ge(v_ready, q + 1)
                        pe.wait_ge(o_read, q)
                        pe.wait_ge(state_ready, i * 2 + (s0 + d + 1))
                        for h in range(HEADS):
                            out = k.banks[4 + h // 2][0:CHUNK, h % 2 * DV:(h % 2 + 1) * DV]
                            pe.matmul(out, e3[d][:, 2, h, :], state[:, d, h, :], start=True, stop=False)
                            mm = pe.matmul(out, att[d][:, h, :], v(h), start=False, stop=True)
                        mm.then_inc(o_mm, 1)
                        pe.wait_ge(k_out, q + 1)
                        pe.wait_ge(state_ready, i * 2 + (s0 + d + 2))
                        for h in range(HEADS):
                            mm = pe.matmul(k.banks[6 + h // 2][:, h % 2 * DV:(h % 2 + 1) * DV],
                                           k_rows[d][:, h * DK:(h + 1) * DK], v(h), start=True, stop=True)
                        mm.then_inc(state_mm, 1)

        @block.sync
        def _(sp):
            sp.wait_ge(state_ready, 2 * NC + 4)
            sp.dma_start(io["new_state_gla"][0, 0].rearrange("d h p v -> p d h v"), state[:, :, :, :]
                         ).then_inc(state_stored, 16)
            sp.wait_ge(state_stored, 16)


def stage_heads_out(k, ctx, name, oTM, gateT, func, gain, yT):
    nc, sem = k.nc, k.sem
    sq = k.sb(ctx, name + "_squares", [CHUNK, W])
    ss = k.sb(ctx, name + "_head_sums", [CHUNK, NC, HEADS])
    sums_ready, root_done, scaled = sem(name + "_sums_ready"), sem(name + "_root_done"), sem(name + "_scaled")
    gate_done, turned, written = sem(name + "_gate_done"), sem(name + "_turned"), sem(name + "_written")
    with nc.Block() as block:
        @block.scalar
        def _(act):
            act.activation(gateT, gateT, func).then_inc(gate_done, 1)
            act.wait_ge(sums_ready, 1)
            act.activation(ss[:, :, :], ss[:, :, :], ACT.Sqrt).then_inc(root_done, 1)

        @block.vector
        def _(dve):
            go = Steps(dve, sem(name + "_head_step"))
            for c in range(NC):
                o = oTM[0:CHUNK, c, :]
                go(dve.tensor_tensor(sq[:, :], o, o, ALU.mult))
                go(dve.tensor_reduce(ss[:, c, :], sq[:, :].rearrange("p (h v) -> p h v", h=HEADS), AX_X, ALU.add))
            dve.tensor_scalar(ss[:, :, :], ss[:, :, :], 1.0 / DV, EPS, ALU.mult, ALU.add).then_inc(sums_ready, 1)
            dve.wait_ge(root_done, 1)
            go(dve.reciprocal(ss[:, :, :], ss[:, :, :]))
            for c in range(NC):
                o = oTM[0:CHUNK, c, :].rearrange("p (h v) -> p h v", h=HEADS)
                dve.tensor_tensor(o, o, ss[:, c, :].unsqueeze(2).broadcast_to([CHUNK, HEADS, DV]), ALU.mult
                                  ).then_inc(scaled, 1)
            dve.wait_ge(gate_done, 1)
            for t in range(WT):
                dve.wait_ge(turned, t + 1)
                g = gain + t % 2
                dve.scalar_tensor_tensor(out=yT[:, t, :], in0=k.banks[t % 4][:, 0:TOK], scalar=k.vcol[:, g:g + 1],
                                         in1=gateT[:, t, :], op0=ALU.mult, op1=ALU.mult).then_inc(written, 1)

        @block.tensor
        def _(pe):
            pe.wait_ge(scaled, NC)
            for t in range(WT):
                if t >= 4:
                    pe.wait_ge(written, t - 3)
                for c in range(NC):
                    mm = pe.transpose(k.banks[t % 4][:, c * CHUNK:(c + 1) * CHUNK],
                                      oTM[0:CHUNK, c, t * P:(t + 1) * P], k.cst[0:CHUNK, C_ID:C_ID + CHUNK])
                mm.then_inc(turned, 1)


def stage_mlstm(k, ctx, zT):
    nc, io = k.nc, k.io
    rows = k.sb(ctx, "ml_rows", [HEADS, 2, 2, TOK])
    cols = k.sb(ctx, "ml_cols", [CHUNK, 3, 2, NC, HEADS])
    keep = k.sb(ctx, "ml_keep", [P, 2, NC, HEADS])
    state = k.sb(ctx, "ml_state", [P, 2, 2 * HEADS, DV])
    norm = k.sb(ctx, "ml_norm", [P, 2, 2 * HEADS])
    with ExitStack() as pre:
        mlstm_prepare(k, pre, zT, rows, cols, keep, state, norm)
    with ExitStack() as scan:
        oTM = k.sb(scan, "ml_o", [CHUNK, NC, W])
        with ExitStack() as inner:
            mlstm_scan(k, inner, zT, oTM, rows, cols, keep, state, norm)
        with ExitStack() as post:
            stage_heads_out(k, post, "ml", oTM, zT[:, 24:32, :], ACT.Sigmoid, V_MLN, k.yT[2])


def mlstm_prepare(k, ctx, zT, rows, cols, keep, state, norm):
    nc, io, sem = k.nc, k.io, k.sem
    wg = k.sb(ctx, "ml_gate_w", [P, KD, 16])
    bg = k.sb(ctx, "ml_gate_bias", [HEADS, 2, 2, 2])
    gates = k.sb(ctx, "ml_gates", [HEADS, 2, 2, TOK])
    mag = k.sb(ctx, "ml_gate_mag", [HEADS, 2, TOK])
    zero = k.sb(ctx, "ml_zero", [HEADS, CHUNK])
    b = k.sb(ctx, "ml_b", [HEADS, 2, TOK])
    top = k.sb(ctx, "ml_running_max", [HEADS, 2, TOK])
    quant = k.sb(ctx, "ml_quantities", [HEADS, 3, 2, TOK])
    enter = k.sb(ctx, "ml_m_enter", [HEADS, 2, NC])
    leave = k.sb(ctx, "ml_m_leave", [HEADS, 2, NC])
    decay = k.sb(ctx, "ml_decay", [HEADS, 2, NC])
    m0 = k.sb(ctx, "ml_m_start", [HEADS, 2])
    conv = k.sb(ctx, "ml_conv", [P, TOK])
    g_in, state_in, m_stored = sem("ml_gate_in"), sem("ml_state_in"), sem("ml_m_stored")
    g_mm, g_read, soft, m_ready = sem("ml_gate_mm"), sem("ml_gate_read"), sem("ml_softplus"), sem("ml_m_ready")
    exps_ready, exps_done, turned = sem("ml_exps_ready"), sem("ml_exps_done"), sem("ml_cols_turned")
    cols_out = sem("ml_cols_out")

    with nc.Block() as block:
        @block.sync
        def _(sp):
            sp.dma_start(wg[:, :, :], io["w_in"][0].rearrange("(k p) n -> p k n", p=P)[:, :, COL_IF:COL_GATE]
                         ).then_inc(g_in, 16)
            for x in range(2):
                at = COL_IF + x * 2 * HEADS
                sp.dma_start(bg[:, 0, x, :], io["b_in"][0, at:at + 2 * HEADS].rearrange("(d h) -> h d", h=HEADS),
                             allow_slow_non_contiguous=True).then_inc(g_in, 16)
                sp.dma_start(bg[:, 1, x, :], io["ml_gate_b"][0, :, x, :].rearrange("d h -> h d"),
                             allow_slow_non_contiguous=True).then_inc(g_in, 16)
            sp.dma_start(m0[:, :], io["state_mlstm_m"][0, 0].rearrange("d h -> h d"),
                         allow_slow_non_contiguous=True).then_inc(g_in, 16)
            for d in range(2):
                sp.dma_start(state[:, d, :, :], io["state_mlstm_C"][0, 0, d].rearrange("h (j p) v -> p (h j) v", p=P)
                             ).then_inc(state_in, 16)
                sp.dma_start(norm[:, d, :], io["state_mlstm_n"][0, 0, d].rearrange("h (j p) -> p (h j)", p=P),
                             allow_slow_non_contiguous=True).then_inc(state_in, 16)
            sp.wait_ge(state_in, 4 * 16)
            sp.wait_ge(m_ready, 1)
            for d in range(2):
                sp.dma_start(io["new_state_mlstm_m"][0, 0, d].unsqueeze(1), leave[:, d, 1 - d:2 - d],
                             allow_slow_non_contiguous=True).then_inc(m_stored, 16)
            sp.wait_ge(m_stored, 32)

        @block.tensor
        def _(pe):
            pe.wait_ge(g_in, 6 * 16)
            for n in range(4):
                for kk in range(KD):
                    mm = pe.matmul(k.banks[n][0:HEADS, 0:TOK], wg[:, kk, n * HEADS:(n + 1) * HEADS], k.hT[:, kk, :],
                                   start=(kk == 0), stop=(kk == KD - 1))
                mm.then_inc(g_mm, 1)
            pe.wait_ge(exps_done, 3)
            pe.wait_ge(g_read, 4)
            for n in range(3 * 2 * NC):
                q, d, c = n // (2 * NC), n // NC % 2, n % NC
                pe.transpose(k.banks[4][0:CHUNK, n * HEADS:(n + 1) * HEADS],
                             quant[:, q, d, c * CHUNK:(c + 1) * CHUNK], k.cst[0:HEADS, C_ID:C_ID + HEADS])
            for h in range(HEADS):
                mm = pe.matmul(k.banks[5][:, h * 2 * NC:(h + 1) * 2 * NC], k.cst[0:HEADS, C_SEL + h * P:C_SEL + (h + 1) * P],
                               decay[:, :, :].rearrange("h d c -> h (d c)"), start=True, stop=True)
            mm.then_inc(turned, 1)

        @block.scalar
        def _(act):
            act.wait_ge(g_read, 5)
            act.activation(mag[:, :, :], mag[:, :, :], ACT.Exp, scale=-1.0).then_inc(soft, 1)
            act.wait_ge(soft, 1)
            act.activation(mag[:, :, :], mag[:, :, :], ACT.Ln, bias=1.0).then_inc(soft, 1)
            act.wait_ge(exps_ready, 1)
            act.activation(rows[:, 1], rows[:, 1], ACT.Exp).then_inc(exps_done, 1)
            act.activation(quant[:, 1:3], quant[:, 1:3], ACT.Exp).then_inc(exps_done, 1)
            act.activation(decay[:, :, :], decay[:, :, :], ACT.Exp).then_inc(exps_done, 1)

        @block.vector
        def _(dve):
            go = Steps(dve, sem("ml_prepare_step"))
            go(dve.memset(zero[:, :], 0.0))
            dve.wait_ge(g_in, 6 * 16)
            go(dve.tensor_tensor(bg[:, 0], bg[:, 0], bg[:, 1], ALU.add))
            for n in range(4):
                dve.wait_ge(g_mm, n + 1)
                dve.tensor_scalar(gates[:, n // 2, n % 2, :], k.banks[n][0:HEADS, 0:TOK],
                                  bg[:, 0, n // 2, n % 2:n % 2 + 1], None, ALU.add).then_inc(g_read, 1)
            dve.wait_ge(g_read, 4)
            go(dve.tensor_scalar(mag[:, :, :], gates[:, 1], 0.0, None, ALU.min))
            dve.scalar_tensor_tensor(out=mag[:, :, :], in0=mag[:, :, :], scalar=-2.0, in1=gates[:, 1],
                                     op0=ALU.mult, op1=ALU.add).then_inc(g_read, 1)
            dve.wait_ge(g_read, 5)
            go(dve.tensor_scalar(gates[:, 1], gates[:, 1], 0.0, None, ALU.min))
            dve.wait_ge(soft, 2)
            go(dve.tensor_tensor(gates[:, 1], gates[:, 1], mag[:, :, :], ALU.subtract))
            cut = lambda t, d, c: t[:, d, c * CHUNK:(c + 1) * CHUNK][:, ::-1 if d else 1]
            a = quant[:, 0]
            for d in range(2):
                for c in range(NC):
                    go(dve.tensor_tensor_scan(cut(b, d, c), cut(gates[:, 1], d, c), zero[:, :], 0.0,
                                              ALU.add, ALU.add), wait=False)
            go(dve.memset(enter[:, :, :], 0.0))
            go(dve.tensor_tensor(a, gates[:, 0], b[:, :, :], ALU.subtract))
            for d in range(2):
                for c in range(NC):
                    go(dve.tensor_tensor_scan(cut(top, d, c), cut(a, d, c), cut(a, d, c), -3.0e38,
                                              ALU.max, ALU.max), wait=False)
            go(dve.tensor_copy(enter[:, 0, 2:3], m0[:, 0:1]), wait=False)
            go(dve.tensor_copy(enter[:, 1, NC - 1:NC], m0[:, 1:2]))
            mu = rows[:, 0]
            for group in GROUPS:
                for i in range(group[1]):
                    for d in range(2):
                        c = chunk_of(group, i, d)
                        end = c * CHUNK if d else (c + 1) * CHUNK - 1
                        go(dve.tensor_scalar(mu[:, d, c * CHUNK:(c + 1) * CHUNK], top[:, d, c * CHUNK:(c + 1) * CHUNK],
                                             enter[:, d, c:c + 1], None, ALU.max))
                        go(dve.tensor_tensor(leave[:, d, c:c + 1], b[:, d, end:end + 1], mu[:, d, end:end + 1], ALU.add))
                        if i + 1 < group[1]:
                            to = chunk_of(group, i + 1, d)
                            go(dve.tensor_copy(enter[:, d, to:to + 1], leave[:, d, c:c + 1]))
            per = lambda t: t.rearrange("h (c s) -> h c s", s=CHUNK)
            for d in range(2):
                at = 0 if d else CHUNK - 1
                end = per(mu[:, d])[:, :, at:at + 1]
                m = enter[:, d, :].unsqueeze(2)
                go(dve.tensor_tensor(per(rows[:, 1, d]), m.broadcast_to([HEADS, NC, CHUNK]), per(mu[:, d]),
                                     ALU.subtract), wait=False)
                go(dve.scalar_tensor_tensor(out=quant[:, 1, d], in0=b[:, d, :], scalar=-1.0, in1=mu[:, d],
                                            op0=ALU.mult, op1=ALU.subtract), wait=False)
                go(dve.tensor_tensor(per(quant[:, 2, d]), per(a[:, d]), end.broadcast_to([HEADS, NC, CHUNK]),
                                     ALU.subtract), wait=False)
                go(dve.tensor_tensor(decay[:, d, :].unsqueeze(2), m, end, ALU.subtract))
            go(dve.tensor_scalar(mu, mu, -1.0, None, ALU.mult))
            dve.memset(zero[:, :], 0.0).then_inc(exps_ready, 1)
            dve.sem_inc(m_ready, 1)
            dve.wait_ge(turned, 1)
            go(dve.tensor_copy(cols[:, :, :, :, :].rearrange("p q d c h -> p (q d c h)"),
                               k.banks[4][0:CHUNK, 0:3 * 2 * NC * HEADS]), wait=False)
            go(dve.tensor_copy(keep[:, :, :, :].rearrange("p d c h -> p (d c) h"),
                               k.banks[5][:, 0:2 * NC * HEADS].rearrange("p (h n) -> p n h", h=HEADS)), wait=False)
            for part in range(2):
                with dve.Fori(0, WT) as i:
                    go.enter(i, 6)
                    z = zT[:, bass.ds(i + part * WT, 1), :].rearrange("p a t -> p (a t)")
                    last = short_conv(dve, go, conv[:, :], z, lambda tap: k.vcol[
                        :, bass.ds(i + (V_MLCONV + (part * 3 + tap) * WT), 1)])
                    go(last)
                    go(dve.tensor_scalar(z, conv[:, :], 0.0625 if part else 1.0, None, ALU.mult))
                    go.leave(WT)


def mlstm_scan(k, ctx, zT, oTM, rows, cols, keep, state, norm):
    nc, io, sem = k.nc, k.io, k.sem
    two = range(2)
    now = [k.sb(ctx, f"ml_qkv_now{d}", [P, 3 * WT, CHUNK]) for d in two]
    row_now = [k.sb(ctx, f"ml_rows_now{d}", [HEADS, 2, CHUNK]) for d in two]
    q_decayed = [k.sb(ctx, f"ml_q_decayed{d}", [P, 2 * HEADS, CHUNK]) for d in two]
    k_rows = [k.sb(ctx, f"ml_k_rows{d}", [CHUNK, W]) for d in two]
    v_rows = [k.sb(ctx, f"ml_v_rows{d}", [CHUNK, W]) for d in two]
    weight = [k.sb(ctx, f"ml_weight{d}", [CHUNK, HEADS, CHUNK]) for d in two]
    den = [k.sb(ctx, f"ml_den{d}", [CHUNK, 2, HEADS]) for d in two]
    hid = k.sb(ctx, "ml_hidden", [CHUNK, W])
    now_ready, weight_done, v_out = sem("ml_now_ready"), sem("ml_weight_done"), sem("ml_v_out")
    qk_mm, spread_mm, k_turned, v_turned = sem("ml_qk_mm"), sem("ml_spread_mm"), sem("ml_k_turned"), sem("ml_v_turned")
    q_ready, att_ready, k_ready = sem("ml_q_ready"), sem("ml_att_ready"), sem("ml_k_ready")
    o_mm, o_read, state_mm, half_read = sem("ml_o_mm"), sem("ml_o_read"), sem("ml_state_mm"), sem("ml_half_read")
    state_ready, state_stored = sem("ml_state_ready"), sem("ml_state_stored")
    runs = ((GROUPS[1], 0, 0), (GROUPS[0], 2 * GROUPS[1][1], 2 * GROUPS[1][1] + 2))

    with nc.Block() as block:
        @block.scalar
        def _(act):
            for group, q0, s0 in runs:
                with act.Fori(0, group[1]) as i:
                    for d in two:
                        act.wait_ge(state_ready, i * 2 + (s0 + d + 1))
                        at = bass.ds(chunk_of(group, i, d) * CHUNK, CHUNK)
                        act.copy(now[d][:, :, :], zT[:, 0:3 * WT, at]).then_inc(now_ready, 1)
                        act.copy(row_now[d][:, :, :], rows[:, :, d, at]).then_inc(now_ready, 1)
                    for d in two:
                        c = chunk_of(group, i, d)
                        act.wait_ge(qk_mm, i * 2 + (q0 + d + 1))
                        for h in range(HEADS):
                            e = k.banks[0][0:CHUNK, (HEADS + h) * CHUNK:(HEADS + h + 1) * CHUNK]
                            act.activation(weight[d][:, h, :], e, ACT.Exp, bias=cols[:, 0, d, bass.ds(c, 1), h]
                                           ).then_inc(weight_done, 1)
                        for half in two:
                            act.wait_ge(v_turned, i * 4 + (2 * (q0 + d) + half + 1))
                            act.copy(v_rows[d][:, half * 512:(half + 1) * 512], k.banks[7 - 3 * half][0:CHUNK, :]
                                     ).then_inc(v_out, 1)

        @block.tensor
        def _(pe):
            ident = k.cst[:, C_ID:C_ID + P]
            for group, q0, s0 in runs:
                with pe.Fori(0, group[1]) as i:
                    pe.wait_ge(state_ready, i * 2 + (s0 + 2))
                    for d in two:
                        q = i * 2 + (q0 + d)
                        pe.wait_ge(now_ready, q * 2 + 2)
                        pe.wait_ge(att_ready, q)
                        for h in range(HEADS):
                            for j in two:
                                pe.matmul(k.banks[0][0:CHUNK, h * CHUNK:(h + 1) * CHUNK], now[d][:, WT + 2 * h + j, :],
                                          now[d][:, 2 * h + j, :], start=(j == 0), stop=(j == 1))
                        e = k.banks[0][0:CHUNK, HEADS * CHUNK:2 * HEADS * CHUNK]
                        mask = k.cst[0:CHUNK, C_NEG + d * CHUNK:C_NEG + (d + 1) * CHUNK]
                        pe.matmul(e.rearrange("p (h t) -> p h t", h=HEADS), k.cst[0:CHUNK, C_ID:C_ID + CHUNK],
                                  mask.unsqueeze(1).broadcast_to([CHUNK, HEADS, CHUNK]), start=True, stop=False)
                        for h in range(HEADS):
                            sel = C_SEL + h * P
                            mm = pe.matmul(e[:, h * CHUNK:(h + 1) * CHUNK], k.cst[0:HEADS, sel:sel + CHUNK],
                                           row_now[d][:, 0, :], start=False, stop=(h == HEADS - 1))
                        mm.then_inc(qk_mm, 1)
                        pe.wait_ge(q_ready, q)
                        pe.wait_ge(k_ready, q)
                        pe.wait_ge(v_out, q * 2)
                        for h in range(HEADS):
                            mm = pe.matmul(k.banks[1][:, h * CHUNK:(h + 1) * CHUNK],
                                           k.cst[0:HEADS, C_SEL + h * P:C_SEL + (h + 1) * P], row_now[d][:, 1, :],
                                           start=True, stop=True)
                        mm.then_inc(spread_mm, 1)
                        for t in range(WT):
                            mm = pe.transpose(k.banks[5 + t // 4][0:CHUNK, t % 4 * P:(t % 4 + 1) * P],
                                              now[d][:, WT + t, :], ident)
                        mm.then_inc(k_turned, 1)
                        for half in two:
                            for t in range(4):
                                mm = pe.transpose(k.banks[7 - 3 * half][0:CHUNK, t * P:(t + 1) * P],
                                                  now[d][:, 2 * WT + 4 * half + t, :], ident)
                            mm.then_inc(v_turned, 1)
                    for d in two:
                        q = i * 2 + (q0 + d)
                        pe.wait_ge(att_ready, q + 1)
                        pe.wait_ge(q_ready, q + 1)
                        pe.wait_ge(v_out, i * 4 + (2 * q0 + 4))
                        pe.wait_ge(o_read, q)
                        for h in range(HEADS):
                            out = k.banks[2 + h // 2][0:CHUNK, h % 2 * DV:(h % 2 + 1) * DV]
                            for j in two:
                                pe.matmul(out, q_decayed[d][:, 2 * h + j, :], state[:, d, 2 * h + j, :],
                                          start=(j == 0), stop=False)
                            pe.matmul(out, weight[d][:, h, :], v_rows[d][:, h * DV:(h + 1) * DV], start=False, stop=True)
                        for h in range(HEADS):
                            out = k.banks[4][0:CHUNK, h:h + 1]
                            for j in two:
                                pe.matmul(out, q_decayed[d][:, 2 * h + j, :], norm[:, d, 2 * h + j:2 * h + j + 1],
                                          start=(j == 0), stop=False)
                            mm = pe.matmul(out, weight[d][:, h, :], k.cst[0:CHUNK, C_ONE:C_ONE + 1], start=False, stop=True)
                        mm.then_inc(o_mm, 1)
                        pe.wait_ge(k_ready, i * 2 + (q0 + 2))
                        pe.wait_ge(state_ready, i * 2 + (s0 + d + 2))
                        for h in range(HEADS):
                            if h == 2:
                                pe.wait_ge(half_read, q + 1)
                            for j in two:
                                pe.matmul(k.banks[5 + h % 2][:, j * DV:(j + 1) * DV],
                                          k_rows[d][:, (2 * h + j) * P:(2 * h + j + 1) * P],
                                          v_rows[d][:, h * DV:(h + 1) * DV], start=True, stop=True)
                                mm = pe.matmul(k.banks[1][:, 256 + 2 * h + j:257 + 2 * h + j],
                                               k_rows[d][:, (2 * h + j) * P:(2 * h + j + 1) * P],
                                               k.cst[0:CHUNK, C_ONE:C_ONE + 1], start=True, stop=True)
                            if h % 2:
                                mm.then_inc(state_mm, 1)

        @block.vector
        def _(dve):
            go = Steps(dve, sem("ml_scan_step"))
            go(dve.memset(oTM[0:CHUNK, :, :], 0.0))
            dve.sem_inc(state_ready, 2)
            for group, q0, s0 in runs:
                if q0:
                    dve.wait_ge(state_ready, q0 + 2)
                    go(dve.memset(norm[:, :, :], 0.0))
                    dve.memset(state[:, :, :, :], 0.0).then_inc(state_ready, 2)
                    dve.wait_ge(state_ready, q0 + 4)
                with dve.Fori(0, group[1]) as i:
                    go.enter(i, 2 * (1 + 4 + 2 + 7 + 1))
                    for d in two:
                        q = i * 2 + (q0 + d)
                        c = chunk_of(group, i, d)
                        dve.wait_ge(spread_mm, q + 1)
                        spread = k.banks[1][:, 0:HEADS * CHUNK].rearrange("p (h t) -> p h t", h=HEADS)
                        dve.tensor_tensor(q_decayed[d][:, :, :].rearrange("p (h j) t -> p h j t", j=2),
                                          spread.unsqueeze(2).broadcast_to([P, HEADS, 2, CHUNK]),
                                          now[d][:, 0:WT, :].rearrange("p (h j) t -> p h j t", j=2),
                                          ALU.mult).then_inc(q_ready, 1)
                        dve.wait_ge(k_turned, q + 1)
                        for half in two:
                            wk = cols[:, 2, d, bass.ds(c, 1), 2 * half:2 * half + 2].rearrange("p a h -> p (a h)")
                            last = dve.tensor_tensor(
                                k_rows[d][:, half * 512:(half + 1) * 512].rearrange("p (h v) -> p h v", h=2),
                                k.banks[5 + half][0:CHUNK, :].rearrange("p (h v) -> p h v", h=2),
                                wk.unsqueeze(2).broadcast_to([CHUNK, 2, DV]), ALU.mult)
                            if half == 0:
                                go(last, wait=False)
                        last.then_inc(k_ready, 1)
                        dve.wait_ge(weight_done, q * 4 + 4)
                        dve.tensor_tensor(weight[d][:, :, :], k.banks[0][0:CHUNK, 0:HEADS * CHUNK].rearrange(
                            "p (h t) -> p h t", h=HEADS), weight[d][:, :, :], ALU.mult).then_inc(att_ready, 1)
                    for d in two:
                        q = i * 2 + (q0 + d)
                        c = chunk_of(group, i, d)
                        dve.wait_ge(o_mm, q + 1)
                        low, up = den[d][:, 0, :], den[d][:, 1, :]
                        em = cols[:, 1, d, bass.ds(c, 1), :].rearrange("p a h -> p (a h)")
                        go(dve.tensor_copy(low, k.banks[4][0:CHUNK, 0:HEADS]))
                        go(dve.scalar_tensor_tensor(out=up, in0=low, scalar=-1.0, in1=low, op0=ALU.mult, op1=ALU.max))
                        go(dve.tensor_tensor(up, up, em, ALU.max))
                        go(dve.reciprocal(low, up))
                        for half in two:
                            last = dve.tensor_tensor(
                                hid[:, half * 512:(half + 1) * 512].rearrange("p (h v) -> p h v", h=2),
                                k.banks[2 + half][0:CHUNK, :].rearrange("p (h v) -> p h v", h=2),
                                low[:, 2 * half:2 * half + 2].unsqueeze(2).broadcast_to([CHUNK, 2, DV]), ALU.mult)
                            if half == 0:
                                go(last, wait=False)
                        last.then_inc(o_read, 1)
                        dve.wait_ge(o_read, q + 1)
                        o = oTM[0:CHUNK, bass.ds(c, 1), :]
                        go(dve.tensor_tensor(o, o, hid[:, :].unsqueeze(1), ALU.add))
                        for h in range(HEADS):
                            if h % 2 == 0:
                                dve.wait_ge(state_mm, q * 2 + (h // 2 + 1))
                            for j in two:
                                part = dve.scalar_tensor_tensor(
                                    out=state[:, d, 2 * h + j, :], in0=state[:, d, 2 * h + j, :],
                                    scalar=keep[:, d, bass.ds(c, 1), h], in1=k.banks[5 + h % 2][:, j * DV:(j + 1) * DV],
                                    op0=ALU.mult, op1=ALU.add)
                                if (h, j) == (1, 1):
                                    part.then_inc(half_read, 1)
                                else:
                                    go(part, wait=False)
                        n8 = norm[:, d, :].rearrange("p (h j) -> p h j", j=2)
                        kp = keep[:, d, bass.ds(c, 1), :].rearrange("p a h -> p (a h)")
                        go(dve.tensor_tensor(n8, n8, kp.unsqueeze(2).broadcast_to([P, HEADS, 2]), ALU.mult))
                        dve.tensor_tensor(norm[:, d, :], k.banks[1][:, 256:264], norm[:, d, :], ALU.add
                                          ).then_inc(state_ready, 1)
                    go.leave(group[1])

        @block.sync
        def _(sp):
            sp.wait_ge(state_ready, 2 * NC + 4)
            for d in two:
                sp.dma_start(io["new_state_mlstm_C"][0, 0, d].rearrange("h (j p) v -> p (h j) v", p=P),
                             state[:, d, :, :]).then_inc(state_stored, 16)
                sp.dma_start(io["new_state_mlstm_n"][0, 0, d].rearrange("h (j p) -> p (h j)", p=P), norm[:, d, :],
                             allow_slow_non_contiguous=True).then_inc(state_stored, 16)
            sp.wait_ge(state_stored, 64)


def stage_merge(k, ctx):
    nc, io, sem = k.nc, k.io, k.sem
    SLOTS = 2
    wg = [k.sb(ctx, f"merge_gate_w{s}", [P, 3, KD, P]) for s in range(SLOTS)]
    wb = [k.sb(ctx, f"merge_branch_w{s}", [P, 3, WT, P]) for s in range(SLOTS)]
    sig = k.sb(ctx, "merge_sigmoid", [P, 3, TOK])
    tmp = k.sb(ctx, "merge_product", [P, TOK])
    slot_in = [sem(f"merge_w_in{s}") for s in range(SLOTS)]
    g_mm, b_mm, sig_done, prod_done = sem("merge_gate_mm"), sem("merge_branch_mm"), sem("merge_sig_done"), sem("merge_prod_done")
    gate_w = io["w_in"][0][:, COL_GATE:].rearrange("(k p) (b n) -> p b k n", p=P, b=3)
    branch_w = io["w_branch"][0].rearrange("b (k p) n -> p b k n", p=P)

    with nc.Block() as block:
        @block.sync
        def _(sp):
            def load(s, at):
                for b in range(3):
                    sp.dma_start(wg[s][:, b], gate_w[:, b, :, at]).then_inc(slot_in[s], 16)
                    sp.dma_start(wb[s][:, b], branch_w[:, b, :, at]).then_inc(slot_in[s], 16)
            for s in range(SLOTS):
                load(s, slice(s * P, (s + 1) * P))
            with sp.Fori(1, KD // SLOTS) as i:
                for s in range(SLOTS):
                    sp.wait_ge(b_mm, i * (3 * SLOTS) + 3 * (s + 1 - SLOTS))
                    load(s, bass.ds(i * (SLOTS * P) + s * P, P))

        @block.tensor
        def _(pe):
            with pe.Fori(0, KD // SLOTS) as i:
                for s in range(SLOTS):
                    pe.wait_ge(slot_in[s], i * 96 + 96)
                    for b in range(3):
                        done = i * (3 * SLOTS) + (3 * s + b + 1)
                        pe.wait_ge(sig_done, done)
                        for kk in range(KD):
                            mm = pe.matmul(k.banks[b][:, 0:TOK], wg[s][:, b, kk, :], k.hT[:, kk, :],
                                           start=(kk == 0), stop=(kk == KD - 1))
                        mm.then_inc(g_mm, 1)
                        pe.wait_ge(prod_done, done)
                        for kk in range(WT):
                            mm = pe.matmul(k.banks[3 + b][:, 0:TOK], wb[s][:, b, kk, :], k.yT[b][:, kk, :],
                                           start=(kk == 0), stop=(kk == WT - 1))
                        mm.then_inc(b_mm, 1)

        @block.scalar
        def _(act):
            act.sem_inc(sig_done, 3)
            with act.Fori(0, KD // SLOTS) as i:
                for s in range(SLOTS):
                    for b in range(3):
                        done = i * (3 * SLOTS) + (3 * s + b + 1)
                        act.wait_ge(g_mm, done)
                        act.wait_ge(prod_done, done)
                        act.activation(sig[:, b, :], k.banks[b][:, 0:TOK], ACT.Sigmoid,
                                       bias=k.vcol[:, bass.ds(i * SLOTS + (V_GATE + b * KD + s), 1)]
                                       ).then_inc(sig_done, 1)

        @block.vector
        def _(dve):
            go = Steps(dve, sem("merge_step"))
            dve.sem_inc(prod_done, 3)
            with dve.Fori(0, KD // SLOTS) as i:
                go.enter(i, 2 * SLOTS)
                for s in range(SLOTS):
                    out = k.mergedT[:, bass.ds(i * SLOTS + s, 1), :]
                    for b in range(3):
                        done = i * (3 * SLOTS) + (3 * s + b + 1)
                        dve.wait_ge(b_mm, done)
                        dve.wait_ge(sig_done, done + 3)
                        to = out if b == 0 else tmp[:, :].unsqueeze(1)
                        dve.tensor_tensor(to, k.banks[3 + b][:, 0:TOK].unsqueeze(1), sig[:, b:b + 1, :], ALU.mult
                                          ).then_inc(prod_done, 1)
                        dve.wait_ge(prod_done, done + 3)
                        if b:
                            go(dve.tensor_tensor(out, out, tmp[:, :].unsqueeze(1), ALU.add))
                go.leave(KD // SLOTS)


def stage_out(k, ctx):
    nc, io, sem = k.nc, k.io, k.sem
    COLS = 512
    N = D // COLS
    ring = [k.sb(ctx, f"out_w{s}", [P, KD, COLS]) for s in range(2)]
    x = k.sb(ctx, "out_x", [P, TT, D])
    gt = k.sb(ctx, "out_gt", [P, 2, D])
    tmp = k.sb(ctx, "out_product", [P, COLS])
    slot_in = [sem(f"out_w_in{s}") for s in range(2)]
    x_in, mm_done, added, stored = sem("out_x_in"), sem("out_mm"), sem("out_added"), sem("x1_stored")
    w = io["w_out"][0].rearrange("(k p) n -> p k n", p=P)
    with nc.Block() as block:
        @block.sync
        def _(sp):
            for n in range(N):
                if n >= 2:
                    sp.wait_ge(mm_done, TT * (n - 1))
                sp.dma_start(ring[n % 2][:, :, :], w[:, :, n * COLS:(n + 1) * COLS]).then_inc(slot_in[n % 2], 16)
                if n == 0:
                    sp.dma_start(x[:, 0, :], io["x_prompt"][0]).then_inc(x_in, 16)
                    sp.dma_start(x[:, 1:3, :], io["x_sample"][0].rearrange("(t p) d -> p t d", p=P)).then_inc(x_in, 16)
                    for g in range(2):
                        sp.dma_start(gt[:, g, :], k.gt_dram[0, g:g + 1].broadcast_to([P, D])).then_inc(x_in, 16)
            sp.wait_ge(added, TT * N)
            sp.dma_start(k.x1_dram.rearrange("t p d -> p t d"), x[:, :, :]).then_inc(stored, 16)
            sp.wait_ge(stored, 16)

        @block.tensor
        def _(pe):
            for n in range(N):
                pe.wait_ge(slot_in[n % 2], 16 * (n // 2 + 1))
                for t in range(TT):
                    u = TT * n + t
                    if u >= 8:
                        pe.wait_ge(added, u - 7)
                    for kk in range(KD):
                        mm = pe.matmul(k.banks[u % 8][:, :], k.mergedT[:, kk, t * P:(t + 1) * P], ring[n % 2][:, kk, :],
                                       start=(kk == 0), stop=(kk == KD - 1))
                    mm.then_inc(mm_done, 1)

        @block.vector
        def _(dve):
            go = Steps(dve, sem("out_step"))
            dve.wait_ge(x_in, 64)
            for n in range(N):
                for t in range(TT):
                    u = TT * n + t
                    dve.wait_ge(mm_done, u + 1)
                    cols = slice(n * COLS, (n + 1) * COLS)
                    go(dve.tensor_tensor(tmp[:, :], k.banks[u % 8][:, :], gt[:, min(t, 1), cols], ALU.mult))
                    dve.tensor_tensor(x[:, t, cols], x[:, t, cols], tmp[:, :], ALU.add).then_inc(added, 1)
                    dve.wait_ge(added, u + 1)


def stage_queries(k, ctx):
    nc, io, sem = k.nc, k.io, k.sem
    SLOTS, COLS = 4, 256
    TURNS = D // COLS // SLOTS
    PER = SLOTS * COLS // P
    ring = [k.sb(ctx, f"wq{s}", [P, KD, COLS]) for s in range(SLOTS)]
    keys = k.sb(ctx, "keys", [NKEYS, 2 * PEER_H, P])
    keysT = k.sb(ctx, "keysT", [P, 2 * PEER_H, NKEYS])
    qT = [k.sb(ctx, f"queryT{s}", [P, TOK]) for s in range(2)]
    slot_in = [sem(f"wq_in{s}") for s in range(SLOTS)]
    keys_in, keys_turned, keys_out = sem("keys_in"), sem("keys_turned"), sem("keys_out")
    q_mm, q_out, s_mm, s_out = sem("query_mm"), sem("query_out"), sem("score_mm"), sem("score_out")
    h_turned, h_out = sem("h2_turned"), sem("h2_out")
    w = io["peer_wq"][0].rearrange("(k p) n -> p k n", p=P)
    with nc.Block() as block:
        @block.sync
        def _(sp):
            for t in range(2 * PEER_H):
                sp.dma_start(keys[:, t, :], io["peer_keys"][0, t // 2, t % 2]).then_inc(keys_in, 16)
            for s in range(SLOTS):
                sp.dma_start(ring[s][:, :, :], w[:, :, s * COLS:(s + 1) * COLS]).then_inc(slot_in[s], 16)
            with sp.Fori(1, TURNS) as i:
                for s in range(SLOTS):
                    sp.wait_ge(q_mm, i * PER + (2 * (s + 1) - PER))
                    sp.dma_start(ring[s][:, :, :], w[:, :, bass.ds(i * (SLOTS * COLS) + s * COLS, COLS)]
                                 ).then_inc(slot_in[s], 16)

        @block.tensor
        def _(pe):
            ident = k.cst[:, C_ID:C_ID + P]
            for r in range(TT):
                for g in range(4):
                    n = r * 4 + g
                    if n >= 4:
                        pe.wait_ge(h_out, n - 3)
                    for t in range(4):
                        mm = pe.transpose(k.banks[4 + n % 4][:, t * P:(t + 1) * P],
                                          k.hT[:, 4 * g + t, r * P:(r + 1) * P], ident)
                    mm.then_inc(h_turned, 1)
            pe.wait_ge(keys_in, 16 * 2 * PEER_H)
            for n in range(4):
                for t in range(4):
                    mm = pe.transpose(k.banks[n][:, t * P:(t + 1) * P], keys[:, 4 * n + t, :], ident)
                mm.then_inc(keys_turned, 1)
            pe.wait_ge(keys_out, 4)
            pe.wait_ge(h_out, 12)

            def scores(i, j):
                pe.wait_ge(q_out, i * PER + (j + 1))
                pe.wait_ge(s_out, i * PER + (j + 1))
                for r in range(TT):
                    mm = pe.matmul(k.banks[2 + j % 2][:, r * P:(r + 1) * P], qT[j % 2][:, r * P:(r + 1) * P],
                                   keysT[:, bass.ds(i * PER + j, 1), :].rearrange("p a n -> p (a n)"),
                                   start=True, stop=True)
                mm.then_inc(s_mm, 1)
            with pe.Fori(0, TURNS) as i:
                for j in range(PER):
                    s, half = j // 2, j % 2
                    if half == 0:
                        pe.wait_ge(slot_in[s], i * 16 + 16)
                    for kk in range(KD):
                        mm = pe.matmul(k.banks[j % 2][:, 0:TOK], ring[s][:, kk, half * P:(half + 1) * P],
                                       k.hT[:, kk, :], start=(kk == 0), stop=(kk == KD - 1))
                    mm.then_inc(q_mm, 1)
                    if j:
                        scores(i, j - 1)
                scores(i, PER - 1)

        @block.scalar
        def _(act):
            for n in range(12):
                act.wait_ge(h_turned, n + 1)
                rows = k.h2_prompt if n < 4 else k.h2_sample[:, n // 4 - 1]
                act.copy(rows[:, n % 4 * 512:(n % 4 + 1) * 512], k.banks[4 + n % 4][:, :]).then_inc(h_out, 1)
            for n in range(4):
                act.wait_ge(keys_turned, n + 1)
                act.copy(keysT[:, 4 * n:4 * n + 4, :], k.banks[n][:, :].rearrange("p (t n) -> p t n", t=4)
                         ).then_inc(keys_out, 1)
            with act.Fori(0, TURNS) as i:
                for j in range(PER):
                    act.wait_ge(q_mm, i * PER + (j + 1))
                    act.wait_ge(s_mm, i * PER + j)
                    act.copy(qT[j % 2][:, :], k.banks[j % 2][:, 0:TOK]).then_inc(q_out, 1)

        @block.vector
        def _(dve):
            sample = k.scores_sample[:, :, :].rearrange("p (r t) n -> p r t n", r=TT - 1)
            dve.sem_inc(s_mm, 1)
            dve.sem_inc(s_out, 2)
            with dve.Fori(0, TURNS) as i:
                for j in range(PER):
                    dve.wait_ge(s_mm, i * PER + (j + 2))
                    bank = k.banks[2 + j % 2]
                    dve.tensor_copy(k.scores_prompt[:, bass.ds(i * PER + j, 1), :], bank[:, 0:P].unsqueeze(1))
                    dve.tensor_copy(sample[:, :, bass.ds(i * PER + j, 1), :],
                                    bank[:, P:TOK].rearrange("p (r a n) -> p r a n", r=TT - 1, a=1)
                                    ).then_inc(s_out, 1)


def top16(dve, go, waited, values, index, src, rest):
    dve.sem_inc(waited, 1)
    go(dve.max(values[:, 0:8], src))
    dve.sem_inc(waited, 1)
    go(dve.max_index(index[:, 0:8], values[:, 0:8], src), wait=False)
    go(dve.match_replace(rest, values[:, 0:8], src, NEG))
    dve.sem_inc(waited, 1)
    go(dve.max(values[:, 8:16], rest))
    dve.sem_inc(waited, 1)
    go(dve.max_index(index[:, 8:16], values[:, 8:16], rest))


class TopK:
    STEPS = 1 + 3 * 5 + 1 + 4 + 6 + 2

    def __init__(self, k, ctx):
        sb = lambda name, shape, dt=F32: k.sb(ctx, name, shape, dt)
        self.k = k
        self.now = sb("scores_now", [P, 2, NKEYS])
        self.rest = sb("scores_rest", [P, 256])
        self.val = sb("key_values", [P, 2, TOPK])
        self.ind = sb("key_index", [P, 2, TOPK], U32)
        self.indf = sb("key_index_f", [P, 2, TOPK])
        self.cand = sb("candidates", [P, TOPK, TOPK])
        self.best = sb("best", [P, TOPK])
        self.bi = sb("best_index", [P, TOPK], U32)
        self.part = sb("best_parts", [P, 2, TOPK], U32)
        self.partf = sb("best_parts_f", [P, 2, TOPK])
        self.eq = sb("one_hot", [P, TOPK, TOPK])
        self.sel = sb("selected", [P, 2, TOPK])
        self.neg = sb("neg_best", [P, 1])
        self.ex = sb("best_exp", [P, TOPK])
        self.tot = sb("best_sum", [P, 1])

    def begin(self, phase):
        sem = self.k.sem
        self.best_ready, self.exp_done = sem(f"best_ready_{phase}"), sem(f"best_exp_done_{phase}")
        self.index_ready, self.waited = sem(f"index_ready_{phase}"), sem(f"topk_waited_{phase}")

    def vector(self, dve, go, scores, head, turn, pairs=None):
        k, val, sel = self.k, self.val, self.sel
        go(dve.tensor_copy(self.now[:, :, :], scores))
        for s in range(2):
            top16(dve, go, self.waited, val[:, s, :], self.ind[:, s, :], self.now[:, s, :],
                  self.rest[:, s * P:(s + 1) * P])
        go(dve.tensor_tensor(self.cand[:, :, :], val[:, 0, :].unsqueeze(2).broadcast_to([P, TOPK, TOPK]),
                             val[:, 1, :].unsqueeze(1).broadcast_to([P, TOPK, TOPK]), ALU.add))
        top16(dve, go, self.waited, self.best, self.bi, self.cand[:, :, :].rearrange("p a b -> p (a b)"),
              self.rest[:, :])
        dve.tensor_scalar(self.neg[:, :], self.best[:, 0:1], -1.0, None, ALU.mult).then_inc(self.best_ready, 1)
        go(dve.tensor_copy(self.indf[:, :, :], self.ind[:, :, :]), wait=False)
        go(dve.tensor_scalar(self.part[:, 0, :], self.bi[:, :], 4, None, ALU.logical_shift_right), wait=False)
        go(dve.tensor_scalar(self.part[:, 1, :], self.bi[:, :], 15, None, ALU.bitwise_and))
        go(dve.tensor_copy(self.partf[:, :, :], self.part[:, :, :]))
        iota = k.cst[:, C_IOTA:C_IOTA + TOPK].unsqueeze(1).broadcast_to([P, TOPK, TOPK])
        for s in range(2):
            go(dve.tensor_tensor(self.eq[:, :, :], self.partf[:, s, :].unsqueeze(2).broadcast_to([P, TOPK, TOPK]),
                                 iota, ALU.is_equal))
            go(dve.tensor_tensor(self.eq[:, :, :], self.eq[:, :, :],
                                 self.indf[:, s, :].unsqueeze(1).broadcast_to([P, TOPK, TOPK]), ALU.mult))
            go(dve.tensor_reduce(sel[:, s, :], self.eq[:, :, :], AX_X, ALU.add))
        dve.scalar_tensor_tensor(out=k.index[:, bass.ds(head, 1), :], in0=sel[:, 0:1, :], scalar=float(NKEYS),
                                 in1=sel[:, 1:2, :], op0=ALU.mult, op1=ALU.add).then_inc(self.index_ready, 1)
        if pairs is not None:
            go(dve.tensor_copy(pairs, sel[:, :, :].unsqueeze(2)))
        dve.wait_ge(self.exp_done, turn + 1)
        go(dve.reciprocal(self.tot[:, :], self.tot[:, :]))
        go(dve.tensor_scalar(k.gate[:, bass.ds(head, 1), :], self.ex[:, :].unsqueeze(1), self.tot[:, 0:1], None,
                             ALU.mult))

    def scalar(self, act, turn):
        act.wait_ge(self.best_ready, turn + 1)
        act.activation(self.ex[:, :], self.best[:, :], ACT.Exp, bias=self.neg[:, 0:1], accum_out=self.tot[:, 0:1]
                       ).then_inc(self.exp_done, 1)


def stage_sample_dots(k, ctx, topk):
    nc, io, sem = k.nc, k.io, k.sem
    R, N = 8, (TT - 1) * PEER_H
    u = [k.sb(ctx, f"u_rows{s}", [P, D]) for s in range(R)]
    idx = [k.sb(ctx, f"index_now{s}", [P, TOPK], U32) for s in range(2)]
    dots = k.sb(ctx, "dots", [P, TOPK])
    u_in = [sem(f"u_in{s}") for s in range(R)]
    idx_copied, dot_done, gelu_done, slot_free = (
        sem("index_now_copied"), sem("dot_done"), sem("gelu_done"), sem("gather_slot_free"))
    weights_ready = sem("sample_weights_ready")
    u_tab = io["peer_u"][0]
    topk.begin("sample")

    with nc.Block() as block:
        @block.gpsimd
        def _(pool):
            with pool.Fori(0, N // 2) as i:
                for odd in range(2):
                    pool.wait_ge(topk.index_ready, i * 2 + (odd + 1))
                    pool.tensor_copy(idx[odd][:, :].unsqueeze(1), k.index[:, bass.ds(i * 2 + odd, 1), :]
                                     ).then_inc(idx_copied, 1)
                    pool.wait_ge(idx_copied, i * 2 + (odd + 1))
                    for n in range(TOPK):
                        pool.wait_ge(dot_done, i * (2 * TOPK) + (odd * TOPK + n + 1))
                        pool.sem_inc(slot_free, 1)
                        pool.indirect_dma_start(
                            out=u[n % R][:, :], out_offset=None, in_=u_tab,
                            in_offset=bass.IndirectOffsetOnAxis(ap=idx[odd][:, n:n + 1], axis=0)
                            ).then_inc(u_in[n % R], 16)

        @block.vector
        def _(dve):
            go = Steps(dve, sem("topk_step_sample"))
            dve.sem_inc(dot_done, R)
            dve.sem_inc(gelu_done, 1)

            def find(head):
                topk.vector(dve, go, k.scores_sample[:, bass.ds(head * 2, 2), :], head, head,
                            k.pairs[:, :, bass.ds(head, 1), :])

            def products(head, tile):
                dve.wait_ge(gelu_done, head + 1)
                for n in range(TOPK):
                    dve.wait_ge(u_in[n % R], head * 32 + 16 * (n // R + 1))
                    dve.scalar_tensor_tensor(out=u[n % R][:, :], in0=u[n % R][:, :], scalar=1.0,
                                             in1=k.h2_sample[:, tile, :], op0=ALU.mult, op1=ALU.mult,
                                             accum_out=dots[:, n:n + 1]).then_inc(dot_done, 1)

            find(0)
            for tile in range(TT - 1):
                n = PEER_H - (tile == TT - 2)
                with dve.Fori(0, n) as i:
                    go.enter(i, TopK.STEPS + 1)
                    find(i + (tile * PEER_H + 1))
                    products(i + tile * PEER_H, tile)
                    go.leave(n)
            topk.vector(dve, go, k.scores_prompt[:, 0:2, :], N, N)
            products(N - 1, TT - 2)
            dve.wait_ge(gelu_done, N + 1)
            dve.tensor_tensor(k.weight[:, :, :], k.weight[:, :, :], k.gate[:, 0:N, :], ALU.mult
                              ).then_inc(weights_ready, 1)

        @block.scalar
        def _(act):
            topk.scalar(act, 0)
            with act.Fori(0, N) as i:
                topk.scalar(act, i + 1)
                act.wait_ge(dot_done, i * TOPK + (TOPK + R))
                act.activation(k.weight[:, bass.ds(i, 1), :], dots[:, :].unsqueeze(1), ACT.Gelu_apprx_tanh
                               ).then_inc(gelu_done, 1)


def stage_experts(k, ctx, topk):
    nc, io, sem = k.nc, k.io, k.sem
    RU, RV, RS = 4, 2, 8
    S_HEADS = (TT - 1) * PEER_H
    HALF, HCOLS = NKEYS // 2, D // 2
    G8, GROUPS8 = 8, SAMPLE // 8
    assert GROUPS8 == 2 * TOPK
    SPLIT = 4
    u = [k.sb(ctx, f"u_slot{s}", [P, D]) for s in range(RU)]
    v = [k.sb(ctx, f"v_slot{s}", [P, D]) for s in range(RV)]
    table = [k.sb(ctx, f"v_table{s}", [P, HCOLS]) for s in range(RS)]
    G = k.sb(ctx, "spread_weights", [P, HALF, SAMPLE])
    hot2 = [k.sb(ctx, f"one_hot_i2_{s}", [P, G8, NKEYS]) for s in range(2)]
    hot1 = [k.sb(ctx, f"one_hot_i1_{s}", [P, G8, HALF]) for s in range(2)]
    pairsT = k.sb(ctx, "pairsT", [P, 3, SAMPLE])
    out = k.sb(ctx, "sums_out", [P, 2, 512])
    idx = [k.sb(ctx, f"index_slot{s}", [P, TOPK], U32) for s in range(2)]
    dots = k.sb(ctx, "prompt_dots", [P, TOPK])
    wgt = k.sb(ctx, "prompt_weights", [P, TOPK])
    u_in, v_in = [sem(f"u_slot_in{s}") for s in range(RU)], [sem(f"v_slot_in{s}") for s in range(RV)]
    table_in = [sem(f"v_table_in{s}") for s in range(RS)]
    idx_copied, dot_done, gelu_done, w_ready, acc_done, slot_free = (
        sem("p_" + n) for n in ("index_copied", "dot_done", "gelu_done", "weights_ready", "acc_done", "slot_free"))
    zeroed, pairs_turned, pairs_out = sem("acc_zeroed"), sem("pairs_turned"), sem("pairs_out")
    hot_ready, build_mm, g_out = sem("one_hots_ready"), sem("spread_mm"), sem("spread_out")
    table_mm, sums_read = sem("v_table_mm"), sem("sums_read")
    sums_stored = [sem(f"sums_stored{s}") for s in range(2)]
    u_tab, v_tab = io["peer_u"][0], io["peer_v"][0]
    v_cut = v_tab.rearrange("(a b) d -> b a d", b=NKEYS)
    topk.begin("prompt")

    with nc.Block() as block:
        @block.sync
        def _(sp):
            for quarter in range(4):
                half, cols = quarter // 2, quarter % 2 * HCOLS
                with sp.Fori(0, HALF // RS) as i:
                    for s in range(RS):
                        sp.wait_ge(table_mm, i * RS + (quarter * HALF + s + 1))
                        sp.dma_start(table[s][:, :].unsqueeze(1),
                                     v_cut[:, bass.ds(i * RS + (half * HALF + s), 1), cols:cols + HCOLS]
                                     ).then_inc(table_in[s], 16)

        @block.gpsimd
        def _(pool):
            with pool.Fori(0, PEER_H // 2) as i:
                for odd in range(2):
                    pool.wait_ge(topk.index_ready, i * 2 + (odd + 1))
                    pool.tensor_copy(idx[odd][:, :].unsqueeze(1), k.index[:, bass.ds(i * 2 + (S_HEADS + odd), 1), :]
                                     ).then_inc(idx_copied, 1)
                    pool.wait_ge(idx_copied, i * 2 + (odd + 1))
                    for tab, ring, arrived, used in ((u_tab, u, u_in, dot_done), (v_tab, v, v_in, acc_done)):
                        for n in range(TOPK):
                            pool.wait_ge(used, i * (2 * TOPK) + (odd * TOPK + n + 1))
                            pool.sem_inc(slot_free, 1)
                            pool.indirect_dma_start(
                                out=ring[n % len(ring)][:, :], out_offset=None, in_=tab,
                                in_offset=bass.IndirectOffsetOnAxis(ap=idx[odd][:, n:n + 1], axis=0)
                                ).then_inc(arrived[n % len(ring)], 16)

        @block.tensor
        def _(pe):
            for a, src in enumerate((k.pairs[:, 0], k.pairs[:, 1], k.weight)):
                for t in range(TT - 1):
                    n = 2 * a + t
                    last = pe.transpose(k.banks[4 + n // 4][:, n % 4 * P:(n % 4 + 1) * P],
                                        src[:, t * PEER_H:(t + 1) * PEER_H, :].rearrange("p h s -> p (h s)"),
                                        k.cst[:, C_ID:C_ID + P])
            last.then_inc(pairs_turned, 1)
            for half in range(2):
                if half:
                    pe.wait_ge(sums_read, 8)
                with pe.Fori(0, GROUPS8 // 2) as i:
                    for s in range(2):
                        pe.wait_ge(hot_ready, i * 2 + (half * GROUPS8 + s + 1))
                        pe.wait_ge(g_out, i * 2 + (half * GROUPS8 + s + 1))
                        for j in range(G8):
                            last = pe.matmul(k.banks[6 + s][:, j * HALF:(j + 1) * HALF], hot2[s][:, j, :],
                                             hot1[s][:, j, :], start=True, stop=True)
                        last.then_inc(build_mm, 1)
                pe.wait_ge(g_out, 2 + (half + 1) * GROUPS8)

                def multiply(quarter, i, last_turn):
                    for s in range(RS):
                        pe.wait_ge(table_in[s], i * 16 + 16 * (quarter * (HALF // RS) + 1))
                        weights = G[:, bass.ds(i * RS + s, 1), :].rearrange("p a t -> p (a t)")
                        for dt in range(HCOLS // P):
                            last = pe.matmul(
                                k.banks[4 * (quarter % 2) + dt // 2][:, dt % 2 * SAMPLE:(dt % 2 + 1) * SAMPLE],
                                table[s][:, dt * P:(dt + 1) * P], weights,
                                start=False, stop=(last_turn and s == RS - 1 and dt % 2 == 1))
                        last.then_inc(table_mm, 1)
                for quarter in (2 * half, 2 * half + 1):
                    for b in range(4):
                        pe.matmul(k.banks[4 * (quarter % 2) + b][:, :], k.cst[:, C_ID:C_ID + P],
                                  k.cst[:, C_ZERO:C_ZERO + 1].broadcast_to([P, 2 * SAMPLE]), start=True, stop=False)
                    with pe.Fori(0, HALF // RS - 1) as i:
                        multiply(quarter, i, False)
                    multiply(quarter, HALF // RS - 1, True)

        @block.vector
        def _(dve):
            go = Steps(dve, sem("topk_step_prompt"))
            for s, n in ((dot_done, RU), (acc_done, RV), (table_mm, RS), (build_mm, 2), (g_out, 2),
                         (topk.index_ready, 1)):
                dve.sem_inc(s, n)
            dve.memset(k.acc[:, :], 0.0).then_inc(zeroed, 1)
            dve.wait_ge(pairs_turned, 1)
            dve.tensor_copy(pairsT[:, 0:2, :], k.banks[4][:, :].rearrange("p (a t) -> p a t", a=2)
                            ).then_inc(pairs_out, 1)
            dve.tensor_copy(pairsT[:, 2, :], k.banks[5][:, 0:SAMPLE]).then_inc(pairs_out, 1)
            dve.wait_ge(pairs_out, 2)
            dve.wait_ge(zeroed, 1)

            def one_hots(g):
                half, s = g // GROUPS8, g % 2
                dve.wait_ge(build_mm, g + 1)
                at = slice(g % GROUPS8 * G8, (g % GROUPS8 + 1) * G8)
                spread = lambda a, n: pairsT[:, a, at].unsqueeze(2).broadcast_to([P, G8, n])
                iota = lambda a, n: k.cst[:, C_IOTA + a:C_IOTA + a + n].unsqueeze(1).broadcast_to([P, G8, n])
                go(dve.tensor_tensor(hot1[s][:, :, :], iota(half * HALF, HALF), spread(0, HALF), ALU.is_equal))
                dve.tensor_tensor(hot2[s][:, :, :], iota(0, NKEYS), spread(1, NKEYS), ALU.is_equal)
                dve.tensor_tensor(hot1[s][:, :, :], hot1[s][:, :, :], spread(2, HALF), ALU.mult
                                  ).then_inc(hot_ready, 1)

            def head(h, more, half=None):
                if more:
                    topk.vector(dve, go, k.scores_prompt[:, bass.ds(h * 2 + 2, 2), :], h + (S_HEADS + 1), h)
                for n in range(TOPK):
                    dve.wait_ge(u_in[n % RU], h * (16 * TOPK // RU) + 16 * (n // RU + 1))
                    dve.scalar_tensor_tensor(out=u[n % RU][:, :], in0=u[n % RU][:, :], scalar=1.0,
                                             in1=k.h2_prompt[:, :], op0=ALU.mult, op1=ALU.mult,
                                             accum_out=dots[:, n:n + 1]).then_inc(dot_done, 1)
                    if half is not None:
                        one_hots(half * GROUPS8 + n)
                dve.wait_ge(gelu_done, h + 1)
                dve.tensor_tensor(wgt[:, :].unsqueeze(1), wgt[:, :].unsqueeze(1),
                                  k.gate[:, bass.ds(h + S_HEADS, 1), :], ALU.mult).then_inc(w_ready, 1)
                dve.wait_ge(w_ready, h + 1)
                for n in range(TOPK):
                    dve.wait_ge(v_in[n % RV], h * (16 * TOPK // RV) + 16 * (n // RV + 1))
                    dve.wait_ge(acc_done, h * TOPK + (n + RV))
                    dve.scalar_tensor_tensor(out=k.acc[:, :], in0=v[n % RV][:, :], scalar=wgt[:, n:n + 1],
                                             in1=k.acc[:, :], op0=ALU.mult, op1=ALU.add).then_inc(acc_done, 1)
                    if half is not None:
                        one_hots(half * GROUPS8 + TOPK + n)

            def heads(first, end):
                with dve.Fori(0, end - first) as i:
                    go.enter(i, TopK.STEPS)
                    head(i + first, True)
                    go.leave(end - first)

            head(0, True, half=0)
            heads(1, SPLIT)
            head(SPLIT, True, half=1)
            heads(SPLIT + 1, PEER_H - 1)
            head(PEER_H - 1, False)

        @block.scalar
        def _(act):
            def spread_out(groups):
                for g in groups:
                    act.wait_ge(build_mm, g + 3)
                    at = g % GROUPS8 * G8
                    act.copy(G[:, :, at:at + G8], k.banks[6 + g % 2][:, :].rearrange("p (t a) -> p a t", a=HALF)
                             ).then_inc(g_out, 1)

            def head(h, more, half=None):
                if more:
                    topk.scalar(act, h)
                if half is not None:
                    spread_out(range(half * GROUPS8, half * GROUPS8 + TOPK - 1))
                act.wait_ge(dot_done, h * TOPK + (TOPK + RU))
                act.wait_ge(acc_done, h * TOPK + RV)
                act.activation(wgt[:, :], dots[:, :], ACT.Gelu_apprx_tanh).then_inc(gelu_done, 1)
                if half is not None:
                    spread_out(range(half * GROUPS8 + TOPK - 1, (half + 1) * GROUPS8))

            def heads(first, end):
                with act.Fori(0, end - first) as i:
                    head(i + first, True)

            def sums_out(half):
                for b in range(8):
                    n = 8 * half + b
                    act.wait_ge(table_mm, RS + (2 * half + b // 4 + 1) * HALF)
                    if n >= 2:
                        act.wait_ge(sums_stored[n % 2], 16 * (n // 2))
                    act.copy(out[:, n % 2, :], k.banks[b][:, :]).then_inc(sums_read, 1)
                    act.wait_ge(sums_read, n + 1)
                    act.dma_start(k.sums_dram[half, b], out[:, n % 2, :]).then_inc(sums_stored[n % 2], 16)

            head(0, True, half=0)
            heads(1, SPLIT)
            sums_out(0)
            head(SPLIT, True, half=1)
            heads(SPLIT + 1, PEER_H - 1)
            head(PEER_H - 1, False)
            sums_out(1)
            act.wait_ge(sums_stored[0], 16 * 8)
            act.wait_ge(sums_stored[1], 16 * 8)


def stage_final(k, ctx):
    nc, io, sem = k.nc, k.io, k.sem
    x = k.sb(ctx, "final_x", [P, TT, D])
    gt = k.sb(ctx, "final_gt", [P, 2, D])
    gain = k.sb(ctx, "final_gain", [P, D])
    junk = k.sb(ctx, "final_squares", [P, D])
    ss = k.sb(ctx, "final_sums", [P, TT])
    parts = k.sb(ctx, "sample_sums", [P, 2, 8, 512])
    tmp = [k.sb(ctx, f"final_product{s}", [P, 512]) for s in range(2)]
    parts_in = [sem(f"final_parts_in{c}") for c in range(2)]
    x_in, joined, turned, added, squared, rms, root, done, stored = (
        sem("final_" + n) for n in ("x_in", "joined", "turned", "added", "squared", "rms", "root",
                                    "done", "stored"))
    with nc.Block() as block:
        @block.sync
        def _(sp):
            sp.dma_start(x[:, :, :], k.x1_dram.rearrange("t p d -> p t d")).then_inc(x_in, 16)
            for g in range(2):
                sp.dma_start(gt[:, g, :], k.gt_dram[1, g:g + 1].broadcast_to([P, D])).then_inc(x_in, 16)
            sp.dma_start(gain[:, :], io["final_g"].unsqueeze(0).broadcast_to([P, D])).then_inc(x_in, 16)
            sp.wait_ge(done, 1)
            sp.dma_start(io["y_prompt"][0], x[:, 0, :]).then_inc(stored, 16)
            for t in range(1, TT):
                sp.wait_ge(done, t + 1)
                sp.dma_start(io["y_sample"][0, (t - 1) * P:t * P, :], x[:, t, :]).then_inc(stored, 16)
            sp.wait_ge(stored, 16 * TT)

        @block.vector
        def _(dve):
            go = Steps(dve, sem("final_step"))
            for c in range(2):
                dve.wait_ge(parts_in[c], 32)
                dve.tensor_tensor(parts[:, 0, 4 * c:4 * c + 4], parts[:, 0, 4 * c:4 * c + 4],
                                  parts[:, 1, 4 * c:4 * c + 4], ALU.add).then_inc(joined, 1)
            dve.wait_ge(x_in, 64)
            go(dve.tensor_tensor(k.acc[:, :], k.acc[:, :], gt[:, 0, :], ALU.mult))
            dve.tensor_tensor(x[:, 0, :], x[:, 0, :], k.acc[:, :], ALU.add).then_inc(added, 4)
            for n in range(4 * (TT - 1)):
                t, c = 1 + n // 4, slice(n % 4 * 512, (n % 4 + 1) * 512)
                dve.wait_ge(turned, n + 1)
                if n >= 2:
                    dve.wait_ge(added, n + 3)
                go(dve.tensor_tensor(tmp[n % 2][:, :], k.banks[n % 4][:, :], gt[:, 1, c], ALU.mult))
                dve.tensor_tensor(x[:, t, c], x[:, t, c], tmp[n % 2][:, :], ALU.add).then_inc(added, 1)
            dve.wait_ge(squared, TT)
            dve.tensor_scalar(ss[:, :], ss[:, :], 1.0 / D, EPS, ALU.mult, ALU.add).then_inc(rms, 1)
            dve.wait_ge(root, 1)
            go(dve.reciprocal(ss[:, :], ss[:, :]))
            for t in range(TT):
                dve.scalar_tensor_tensor(out=x[:, t, :], in0=x[:, t, :], scalar=ss[:, t:t + 1], in1=gain[:, :],
                                         op0=ALU.mult, op1=ALU.mult).then_inc(done, 1)

        @block.tensor
        def _(pe):
            for n in range(4 * (TT - 1)):
                t = n // 4
                pe.wait_ge(joined, n % 4 // 2 + 1)
                if n >= 4:
                    pe.wait_ge(added, n + 1)
                for j in range(4):
                    dt = 4 * (n % 4) + j
                    at = dt % 2 * SAMPLE + t * P
                    last = pe.transpose(k.banks[n % 4][:, j * P:(j + 1) * P], parts[:, 0, dt // 2, at:at + P],
                                        k.cst[:, C_ID:C_ID + P])
                last.then_inc(turned, 1)

        @block.scalar
        def _(act):
            for c in range(2):
                for half in range(2):
                    act.dma_start(parts[:, half, 4 * c:4 * c + 4],
                                  k.sums_dram[half, 4 * c:4 * c + 4].rearrange("b p n -> p b n")
                                  ).then_inc(parts_in[c], 16)
            for t in range(TT):
                act.wait_ge(added, 4 * (t + 1))
                act.activation(junk[:, :], x[:, t, :], ACT.Square, accum_out=ss[:, t:t + 1]).then_inc(squared, 1)
                act.wait_ge(squared, t + 1)
            act.wait_ge(rms, 1)
            act.activation(ss[:, :], ss[:, :], ACT.Sqrt).then_inc(root, 1)


_INS = ['x_prompt', 'x_sample', 'c', 'state_gla', 'state_mlstm_C', 'state_mlstm_n', 'state_mlstm_m', 'c_ctx',
        'mod_w', 'mod_b', 'norm1_g', 'norm2_g', 'final_g', 'w_in', 'b_in', 'hy_conv', 'hy_w1', 'hy_b1', 'hy_w2',
        'hy_b2', 'hy_w3', 'hy_freq', 'hy_bias', 'gla_a2_w', 'gla_a2_b', 'gla_norm_g', 'ml_conv', 'ml_gate_b',
        'ml_norm_g', 'w_branch', 'w_out', 'peer_wq', 'peer_keys', 'peer_u', 'peer_v']
_OUTS = {'y_prompt': (1, 128, 2048), 'y_sample': (1, 256, 2048), 'new_state_gla': (1, 1, 2, 4, 128, 256),
         'new_state_mlstm_C': (1, 1, 2, 4, 256, 256), 'new_state_mlstm_n': (1, 1, 2, 4, 256),
         'new_state_mlstm_m': (1, 1, 2, 4)}


def kernel(**inputs):
    import concourse.bacc as _bacc
    from concourse.bass_utils import run_bass_kernel_spmd as _run

    nc = _bacc.Bacc("TRN2", target_bir_lowering=False, num_devices=1)
    arrays, io = {}, {}
    for name, a in [(n, np.ascontiguousarray(inputs[n])) for n in _INS] + list(shape_constants().items()):
        arrays["in_" + name] = a
        io[name] = nc.dram_tensor("in_" + name, a.shape, mybir.dt.from_np(a.dtype), kind="ExternalInput").ap()
    for name, shape in _OUTS.items():
        io[name] = nc.dram_tensor("out_" + name, shape, F32, kind="ExternalOutput").ap()
    build(nc, io)
    r = _run(nc, [arrays], core_ids=[0])
    return tuple(r.results[0]["out_" + name] for name in _OUTS)
```

```python
from contextlib import ExitStack
import math

import numpy as np

import concourse.bass as bass
from concourse import mybir

ALU = mybir.AluOpType
ACT = mybir.ActivationFunctionType
AX_X = mybir.AxisListType.X
F32 = mybir.dt.float32
U32 = mybir.dt.uint32

P = 128
D = 2048
KD = D // P
PROMPT, SAMPLE = 128, 256
TOK = PROMPT + SAMPLE
TT = TOK // P
CHUNK = 64
NC = TOK // CHUNK
GROUPS = ((0, 2), (2, 4))
EPS = 1e-6
W = 1024
WT = W // P
HEADS = 4
DK, DV = 128, 256
SUB = 16
NSUB = CHUNK // SUB
MAX_EXP = 50.0
NEG = -1.0e30
COL_HY, COL_GLA, COL_LR, COL_ML, COL_IF, COL_GATE = 0, 3072, 6144, 6176, 10272, 10288
PEER_H, NKEYS, TOPK = 8, 128, 16
MAGIC = 12582912.0
TWO_PI_HI = 6.28125
TWO_PI_LO = 2.0 * math.pi - TWO_PI_HI
PI_IN = 3.1415925

C_ID = 0
C_TRI = 128
C_GMASK = C_TRI + 2 * P
C_NEG = C_GMASK + 2 * CHUNK
C_SEL = C_NEG + 2 * CHUNK
C_IOTA = C_SEL + 4 * P
C_ONE = C_IOTA + NKEYS
C_ZERO = C_ONE + 1
C_END = C_ZERO + 2
V_HY, V_GLA, V_ML, V_GATE = 0, 24, 48, 80
V_HYCONV, V_MLCONV = 128, 128 + 72
V_N1, V_N2, V_GLAN, V_MLN = 256, 272, 288, 290


def shape_constants():
    c = np.zeros((P, C_END), np.float32)
    c[:, C_ID:C_ID + P] = np.eye(P)
    t = np.arange(P)
    same = (t[:, None] // CHUNK) == (t[None, :] // CHUNK)
    c[:, C_TRI:C_TRI + P] = (same & (t[:, None] <= t[None, :])) / 16.0
    c[:, C_TRI + P:C_TRI + 2 * P] = (same & (t[:, None] >= t[None, :])) / 16.0
    s = np.arange(CHUNK)
    fwd = s[:, None] <= s[None, :]
    bwd = s[:, None] >= s[None, :]
    for n, m in enumerate((fwd, bwd)):
        c[:CHUNK, C_GMASK + n * CHUNK:C_GMASK + (n + 1) * CHUNK] = m
        c[:CHUNK, C_NEG + n * CHUNK:C_NEG + (n + 1) * CHUNK] = np.where(m, 0.0, NEG)
    for h in range(HEADS):
        c[h, C_SEL + h * P:C_SEL + (h + 1) * P] = 1.0
    c[:, C_IOTA:C_IOTA + NKEYS] = np.arange(NKEYS)
    c[:, C_ONE] = c[:, C_ZERO + 1] = 1.0
    out = {"cst": c}
    for name, n in (("p", PROMPT), ("s", SAMPLE)):
        k = np.arange(n)
        ang = np.pi * ((2 * k[None, :] + 1) * k[:, None] % (4 * n)) / (2 * n)
        mats = np.stack([np.cos(ang), np.sin(ang), np.cos(ang).T / n, np.sin(ang).T / n])
        out["dft_" + name] = np.ascontiguousarray(
            mats.reshape(4, n // P, P, n).transpose(2, 0, 1, 3)).astype(np.float32)
        t = np.arange(n, dtype=np.float32)
        tn = t / np.float32(n - 1)
        bands = np.linspace(1e-4, 15, 16, dtype=np.float32)
        an = (np.float32(2.0 * math.pi / n) * t[:, None] * bands[None, :]).astype(np.float32)
        z = np.concatenate([tn[:, None], np.cos(an), -np.sin(an)], -1)
        out["feat_" + name] = np.ascontiguousarray(z.T).astype(np.float32)
        lo, hi = math.log(1e-2) / 1.5, math.log(1e-2) / 0.3
        deltas = np.abs(np.linspace(lo, hi, W, dtype=np.float32))
        win = np.exp(-tn[:, None] * deltas[None, :]).astype(np.float32)
        out["win_" + name] = np.ascontiguousarray(win.reshape(n // P, P, W).transpose(1, 0, 2))
    return out


class Steps:

    def __init__(self, eng, sem):
        self.eng, self.sem, self.n, self.base = eng, sem, 0, 0

    def __call__(self, ins, wait=True):
        self.n += 1
        ins.then_inc(self.sem, 1)
        if wait:
            self.eng.wait_ge(self.sem, self.base + self.n)

    def enter(self, turn, per):
        self.before, self.base, self.n = self.n, turn * per + self.n, 0
        self.per = per

    def leave(self, turns):
        assert self.n == self.per, (self.n, self.per)
        self.base, self.n = 0, self.before + turns * self.per


class Core:
    pass


def build(nc, io, upto=99):
    k = Core()
    k.nc, k.io = nc, io
    with ExitStack() as top:
        k.banks = [top.enter_context(nc.psum_tensor(f"bank{i}", [P, 512], F32)) for i in range(8)]

        handles = []

        def sem(name):
            handles.append(nc.alloc_semaphore(name=name))
            return handles[-1]

        def clear_semaphores():
            with nc.Block() as block:
                @block.gpsimd
                def _(pool):
                    for s in handles:
                        pool.sem_clear(s)
            for s in handles:
                nc.release_semaphore(s)
            handles.clear()

        def sb(ctx, name, shape, dt=F32):
            return ctx.enter_context(nc.sbuf_tensor(name, shape, dt))

        k.sem, k.sb = sem, sb
        k.cst = sb(top, "cst", [P, C_END])
        k.vcol = sb(top, "vcol", [P, 3 * P])
        k.h2cols = sb(top, "h2cols", [P, 2, KD, 2])
        k.gt_dram = nc.dram_tensor("gt_rows", (2, 2, D), F32, kind="Internal").ap()
        k.x1_dram = nc.dram_tensor("x1_rows", (TT, P, D), F32, kind="Internal").ap()
        k.sums_dram = nc.dram_tensor("sample_sum_columns", (2, 8, P, 2 * SAMPLE), F32, kind="Internal").ap()
        with ExitStack() as mix:
            k.hT = sb(mix, "hT", [P, KD, TOK])
            k.h1cols = sb(mix, "h1cols", [P, 2, KD, 2])
            with ExitStack() as ctx:
                stage_modulation(k, ctx)
            if upto < 2: return
            k.yT = [sb(mix, "yT_hyena", [P, WT, TOK])]
            with ExitStack() as ctx:
                k.uTM = sb(ctx, "hyena_rows", [P, TT, 3 * W])
                with ExitStack() as in1:
                    zT = sb(in1, "z_hyena", [P, 24, TOK])
                    stage_project(k, in1, "hy", COL_HY, V_HY, zT, 24, hyena_rows)
                if upto < 3: return
                k.dft = {"p": sb(ctx, "dft_prompt", [P, 4, 1, PROMPT]),
                         "s": sb(ctx, "dft_sample", [P, 4, 2, SAMPLE])}
                k.spec = sb(ctx, "filter_spectra", [P, 3, 2, 2, W])
                with ExitStack() as in1:
                    stage_filters(k, in1)
                with ExitStack() as in1:
                    stage_hyena(k, in1)
            if upto < 4: return
            k.yT.append(sb(mix, "yT_gla", [P, WT, TOK]))
            with ExitStack() as ctx:
                zT = sb(ctx, "z_gla", [P, 24, TOK])
                k.lrT = sb(ctx, "low_rank", [17, 2, TOK])
                mem = gla_memory(k, ctx)
                with ExitStack() as in1:
                    stage_project(k, in1, "gla", COL_GLA, V_GLA, zT, 24,
                                  lambda *args: gla_prepare(*args, *mem))
                with ExitStack() as in1:
                    stage_gla(k, in1, zT, mem)
            if upto < 5: return
            k.yT.append(sb(mix, "yT_mlstm", [P, WT, TOK]))
            with ExitStack() as ctx:
                zT = sb(ctx, "z_mlstm", [P, 32, TOK])
                mem = mlstm_memory(k, ctx)
                with ExitStack() as in1:
                    stage_project(k, in1, "ml", COL_ML, V_ML, zT, 32,
                                  lambda *args: mlstm_prepare(*args, *mem))
                with ExitStack() as in1:
                    stage_mlstm(k, in1, zT, mem)
            if upto < 6: return
            clear_semaphores()
            k.mergedT = sb(mix, "mergedT", [P, KD, TOK])
            with ExitStack() as ctx:
                stage_merge(k, ctx)
            with ExitStack() as ctx:
                stage_out(k, ctx)
        if upto < 7: return
        with ExitStack() as tail:
            sample_heads = (TT - 1) * PEER_H
            k.index = sb(tail, "expert_index", [P, TT * PEER_H, TOPK], U32)
            k.gate = sb(tail, "expert_gate", [P, TT * PEER_H, TOPK])
            k.pairs = sb(tail, "expert_pairs", [P, 2, sample_heads, TOPK])
            k.weight = sb(tail, "expert_weight", [P, sample_heads, TOPK])
            k.h2_prompt = sb(tail, "h2_prompt_rows", [P, D])
            k.scores_prompt = sb(tail, "prompt_scores", [P, 2 * PEER_H, NKEYS])
            topk = TopK(k, tail)
            with ExitStack() as sample:
                k.h2_sample = sb(sample, "h2_sample_rows", [P, TT - 1, D])
                k.scores_sample = sb(sample, "sample_scores", [P, 2 * sample_heads, NKEYS])
                with ExitStack() as ctx:
                    k.hT = sb(ctx, "h2T", [P, KD, TOK])
                    with ExitStack() as in1:
                        stage_queries(k, in1)
                with ExitStack() as ctx:
                    stage_sample_dots(k, ctx, topk)
            if upto < 9: return
            k.acc = sb(tail, "prompt_expert_sum", [P, D])
            k.u_slots = [sb(tail, f"u_slot{s}", [P, D]) for s in range(4)]
            k.v_slots = [sb(tail, f"v_slot{s}", [P, D]) for s in range(2)]
            k.final_in = sem("final_in")
            with ExitStack() as ctx:
                stage_experts(k, ctx, topk)
            with ExitStack() as ctx:
                stage_final(k, ctx)


def stage_modulation(k, ctx):
    nc, io, sem = k.nc, k.io, k.sem
    SLOTS, COLS = 4, 256
    TURNS = 6 * D // COLS // SLOTS
    ring = [k.sb(ctx, f"mod_w{s}", [P, KD, COLS]) for s in range(SLOTS)]
    rows = k.sb(ctx, "mod_rows", [2, 6 * D])
    folded = [k.sb(ctx, f"mod_folded{g}", [P, COLS]) for g in range(2)]
    vrow = k.sb(ctx, "vector_rows", [P, 3, P])
    crow = k.sb(ctx, "c_rows", [2 * KD, P])
    cT = k.sb(ctx, "cT", [P, KD, 2])
    norm = Norm(k, ctx, 1)
    const_in, vec_in, c_in, bias_in = sem("const_in"), sem("vec_in"), sem("c_in"), sem("mod_bias_in")
    slot_in = [sem(f"mod_w_in{s}") for s in range(SLOTS)]
    c_turned, fold_done = sem("c_turned"), sem("mod_fold_done")
    last_done, last_out = sem("mod_last_slot_done"), sem("mod_last_slot_out")
    MULT, FOLDS = SLOTS - 1, 2 * KD
    silu_done, part_done, part_out = sem("silu_done"), sem("mod_part_done"), sem("mod_part_out")
    zeroed, vec_turned, vec_out = sem("vec_zeroed"), sem("vec_turned"), sem("vec_out")
    mod_turned, gt_stored = sem("mod_turned"), sem("gt_stored")
    w = io["mod_w"][0].rearrange("(k p) n -> p k n", p=P)
    b_in = io["b_in"][0]

    with nc.Block() as block:
        @block.sync
        def _(sp):
            sp.dma_start(crow[0:KD, :], io["c_ctx"].rearrange("(k p) -> k p", p=P)).then_inc(c_in, 16)
            sp.dma_start(crow[KD:, :], io["c"][0].rearrange("(k p) -> k p", p=P)).then_inc(c_in, 16)
            for s in range(SLOTS):
                sp.dma_start(ring[s][:, :, :], w[:, :, s * COLS:(s + 1) * COLS]).then_inc(slot_in[s], 16)
            with sp.Fori(1, TURNS) as i:
                for s in range(MULT):
                    sp.wait_ge(part_done, i * MULT + (s + 1 - MULT))
                    sp.dma_start(ring[s][:, :, :], w[:, :, bass.ds(i * (SLOTS * COLS) + s * COLS, COLS)]
                                 ).then_inc(slot_in[s], 16)

        @block.scalar
        def _(act):
            act.dma_start(k.cst[:, :], io["cst"]).then_inc(const_in, 16)
            act.wait_ge(c_turned, 1)
            act.activation(cT[:, :, :], k.banks[5][:, 0:2 * KD].rearrange("p (g t) -> p t g", g=2), ACT.Silu
                           ).then_inc(silu_done, 1)
            act.dma_start(rows[:, :], io["mod_b"].broadcast_to([2, 6 * D])).then_inc(bias_in, 16)
            act.wait_ge(zeroed, 1)
            act.dma_start(vrow[0:48, 0, :], b_in[0:COL_LR].rearrange("(r c) -> r c", c=P)).then_inc(vec_in, 16)
            act.dma_start(vrow[48:80, 0, :], b_in[COL_ML:COL_IF].rearrange("(r c) -> r c", c=P)).then_inc(vec_in, 16)
            act.dma_start(vrow[80:128, 0, :], b_in[COL_GATE:].rearrange("(r c) -> r c", c=P)).then_inc(vec_in, 16)
            act.dma_start(vrow[0:72, 1, :], io["hy_conv"][0].rearrange("a b (r c) -> (a b r) c", c=P)).then_inc(vec_in, 16)
            act.dma_start(vrow[72:120, 1, :], io["ml_conv"][0].rearrange("a b (r c) -> (a b r) c", c=P)).then_inc(vec_in, 16)
            act.dma_start(vrow[0:16, 2, :], io["norm1_g"][0].rearrange("(r c) -> r c", c=P)).then_inc(vec_in, 16)
            act.dma_start(vrow[16:32, 2, :], io["norm2_g"][0].rearrange("(r c) -> r c", c=P)).then_inc(vec_in, 16)
            act.dma_start(vrow[32:34, 2, :], io["gla_norm_g"][0].rearrange("(r c) -> r c", c=P)).then_inc(vec_in, 16)
            act.dma_start(vrow[34:36, 2, :], io["ml_norm_g"][0].rearrange("(r c) -> r c", c=P)).then_inc(vec_in, 16)
            norm.load(act)
            norm.scalar(act)
            with act.Fori(1, TURNS) as i:
                act.wait_ge(fold_done, i * FOLDS)
                act.dma_start(ring[MULT][:, :, :], w[:, :, bass.ds(i * (SLOTS * COLS) + MULT * COLS, COLS)]
                              ).then_inc(slot_in[MULT], 16)
            act.wait_ge(part_out, MULT + TURNS * MULT)
            act.wait_ge(last_out, 1 + TURNS)
            act.dma_start(k.gt_dram[0], rows[:, 2 * D:3 * D]).then_inc(gt_stored, 16)
            act.dma_start(k.gt_dram[1], rows[:, 5 * D:6 * D]).then_inc(gt_stored, 16)
            act.wait_ge(gt_stored, 32)

        @block.tensor
        def _(pe):
            pe.wait_ge(const_in, 16)
            ident = k.cst[:, C_ID:C_ID + P]
            pe.wait_ge(c_in, 32)
            pe.transpose(k.banks[5][:, 0:2 * KD], crow[:, :], k.cst[0:2 * KD, C_ID:C_ID + 2 * KD]).then_inc(c_turned, 1)
            pe.wait_ge(silu_done, 1)

            def products(i):
                for s in range(MULT):
                    pe.wait_ge(slot_in[s], i * 16 + 16)
                    pe.wait_ge(part_out, i * MULT + (s + 1))
                    for kk in range(KD):
                        last = pe.matmul(k.banks[s][0:2, 0:COLS], cT[:, kk, :], ring[s][:, kk, :],
                                         start=(kk == 0), stop=(kk == KD - 1))
                    last.then_inc(part_done, 1)

            def fold_sums(i):
                pe.wait_ge(fold_done, i * FOLDS + FOLDS)
                pe.wait_ge(last_out, i + 1)
                for g, col in enumerate((C_ONE, C_ZERO)):
                    last = pe.matmul(k.banks[3][0:2, 0:COLS], k.cst[:, col:col + 2], folded[g][:, :],
                                     start=(g == 0), stop=(g == 1))
                last.then_inc(last_done, 1)
            products(0)
            with pe.Fori(1, TURNS) as i:
                products(i)
                fold_sums(i - 1)
            fold_sums(TURNS - 1)
            pe.wait_ge(vec_in, 9 * 16)
            for n in range(3):
                last = pe.transpose(k.banks[7][:, n * P:(n + 1) * P], vrow[:, n, :], ident)
            last.then_inc(vec_turned, 1)
            pe.wait_ge(part_out, MULT + TURNS * MULT)
            pe.wait_ge(last_out, 1 + TURNS)
            for n, part in enumerate((0, 1, 3, 4)):
                for t in range(KD):
                    at = part * D + t * P
                    last = pe.transpose(k.banks[6][:, (n * KD + t) * 2:(n * KD + t) * 2 + 2],
                                        rows[:, at:at + P], k.cst[0:2, C_ID:C_ID + 2])
            last.then_inc(mod_turned, 1)
            norm.tensor(pe)

        @block.vector
        def _(dve):
            dve.memset(vrow[:, :, :], 0.0).then_inc(zeroed, 1)
            dve.sem_inc(part_out, MULT)
            dve.sem_inc(last_out, 1)
            norm.vector_sums(dve)
            dve.wait_ge(bias_in, 16)
            dve.wait_ge(silu_done, 1)

            def add(i, s, done):
                at = bass.ds(i * (SLOTS * COLS) + s * COLS, COLS)
                dve.tensor_tensor(rows[:, at], k.banks[s][0:2, 0:COLS], rows[:, at], ALU.add).then_inc(done, 1)

            def adds(i):
                for s in range(MULT):
                    dve.wait_ge(part_done, i * MULT + (s + 1))
                    add(i, s, part_out)

            def add_last(i):
                dve.wait_ge(last_done, i + 1)
                add(i, MULT, last_out)

            def fold(i):
                dve.wait_ge(slot_in[MULT], i * 16 + 16)
                for kk in range(KD):
                    for g in range(2):
                        if kk:
                            dve.wait_ge(fold_done, i * FOLDS + (2 * (kk - 1) + g + 1))
                            dve.scalar_tensor_tensor(out=folded[g][:, :], in0=ring[MULT][:, kk, :],
                                                     scalar=cT[:, kk, g:g + 1], in1=folded[g][:, :],
                                                     op0=ALU.mult, op1=ALU.add).then_inc(fold_done, 1)
                        else:
                            dve.tensor_scalar(folded[g][:, :], ring[MULT][:, 0, :], cT[:, 0, g:g + 1], None,
                                              ALU.mult).then_inc(fold_done, 1)
            adds(0)
            fold(0)
            with dve.Fori(1, TURNS) as i:
                adds(i)
                add_last(i - 1)
                fold(i)
            add_last(TURNS - 1)
            dve.wait_ge(vec_turned, 1)
            dve.tensor_copy(k.vcol[:, :], k.banks[7][:, 0:3 * P]).then_inc(vec_out, 1)
            dve.wait_ge(vec_out, 1)
            dve.wait_ge(mod_turned, 1)
            cols = k.banks[6][:, 0:4 * KD * 2].rearrange("p (n t g) -> p n t g", n=4, t=KD)
            for n, (dst, v) in enumerate(((k.h1cols, V_N1), (k.h2cols, V_N2))):
                gain = k.vcol[:, v:v + KD].unsqueeze(2).broadcast_to([P, KD, 2])
                dve.scalar_tensor_tensor(out=dst[:, 0, :, :], in0=cols[:, 2 * n + 1], scalar=1.0, in1=gain,
                                         op0=ALU.add, op1=ALU.mult).then_inc(vec_out, 1)
                dve.tensor_copy(dst[:, 1, :, :], cols[:, 2 * n]).then_inc(vec_out, 1)
            dve.wait_ge(vec_out, 1 + 4)
            norm.vector_columns(dve, k.h1cols)


class Norm:

    def __init__(self, k, ctx, which):
        self.k, self.which = k, which
        self.x = k.sb(ctx, f"norm{which}_x", [P, TT, D])
        self.junk = k.sb(ctx, f"norm{which}_squares", [P, D])
        self.ss = k.sb(ctx, f"norm{which}_sums", [P, TT])
        self.x_in, self.squared, self.root, self.scaled, self.turned, self.written, self.rms = (
            k.sem(f"norm{which}_{n}") for n in ("x_in", "squared", "root", "scaled", "turned", "written", "rms"))

    def load(self, eng):
        io, x = self.k.io, self.x
        if self.which == 1:
            eng.dma_start(x[:, 0, :], io["x_prompt"][0]).then_inc(self.x_in, 16)
            eng.dma_start(x[:, 1:3, :], io["x_sample"][0].rearrange("(t p) d -> p t d", p=P)).then_inc(self.x_in, 16)
        else:
            eng.dma_start(x[:, :, :], self.k.x1_dram.rearrange("t p d -> p t d")).then_inc(self.x_in, 32)

    def scalar(self, act):
        x, ss = self.x, self.ss
        act.wait_ge(self.x_in, 32)
        for t in range(TT):
            act.activation(self.junk[:, :], x[:, t, :], ACT.Square, accum_out=ss[:, t:t + 1]).then_inc(self.squared, 1)
            act.wait_ge(self.squared, t + 1)
        act.wait_ge(self.rms, 1)
        act.activation(ss[:, :], ss[:, :], ACT.Sqrt).then_inc(self.root, 1)
        act.wait_ge(self.rms, 2)
        for t in range(TT):
            act.activation(x[:, t, :], x[:, t, :], ACT.Copy, scale=ss[:, t:t + 1]).then_inc(self.scaled, 1)

    def vector_sums(self, dve):
        ss = self.ss
        dve.wait_ge(self.squared, TT)
        dve.tensor_scalar(ss[:, :], ss[:, :], 1.0 / D, EPS, ALU.mult, ALU.add).then_inc(self.rms, 1)
        dve.wait_ge(self.root, 1)
        dve.reciprocal(ss[:, :], ss[:, :]).then_inc(self.rms, 1)

    def tensor(self, pe):
        k = self.k
        for t in range(KD):
            for r in range(TT):
                pe.wait_ge(self.scaled, r + 1)
                if t >= 4:
                    pe.wait_ge(self.written, 2 * (t - 3))
                last = pe.transpose(k.banks[t % 4][:, r * P:(r + 1) * P], self.x[:, r, t * P:(t + 1) * P],
                                    k.cst[:, C_ID:C_ID + P])
            last.then_inc(self.turned, 1)

    def vector_columns(self, dve, cols):
        k = self.k
        for t in range(KD):
            dve.wait_ge(self.turned, t + 1)
            for g, (a, b) in enumerate(((0, PROMPT), (PROMPT, TOK))):
                dve.tensor_scalar(k.hT[:, t, a:b], k.banks[t % 4][:, a:b], cols[:, 0, t, g:g + 1],
                                  cols[:, 1, t, g:g + 1], ALU.mult, ALU.add).then_inc(self.written, 1)


class Side:

    def __init__(self, **parts):
        self.parts = parts

    def __call__(self, name, *args):
        if name in self.parts:
            self.parts[name](*args)


def stage_project(k, ctx, name, col0, v0, zT, tiles, make_side):
    nc, io, sem = k.nc, k.io, k.sem
    SLOTS, COLS, BANKS = 2, 256, 4
    TURNS = tiles * P // COLS // SLOTS
    PER = SLOTS * COLS // P
    assert PER == BANKS
    ring = [k.sb(ctx, f"{name}_w{s}", [P, KD, COLS]) for s in range(SLOTS)]
    slot_in = [sem(f"{name}_w_in{s}") for s in range(SLOTS)]
    tile_done, tile_out = sem(f"{name}_tile_done"), sem(f"{name}_tile_out")
    w = io["w_in"][0].rearrange("(k p) n -> p k n", p=P)
    side = make_side(k, ctx, zT, tile_out, BANKS, TURNS)

    with nc.Block() as block:
        @block.sync
        def _(sp):
            side("sync_early", sp)
            for s in range(SLOTS):
                at = col0 + s * COLS
                sp.dma_start(ring[s][:, :, :], w[:, :, at:at + COLS]).then_inc(slot_in[s], 16)
            side("sync_states", sp)
            with sp.Fori(1, TURNS) as i:
                for s in range(SLOTS):
                    sp.wait_ge(tile_done, i * PER + (2 * (s + 1) - PER))
                    sp.dma_start(ring[s][:, :, :], w[:, :, bass.ds(i * (SLOTS * COLS) + (col0 + s * COLS), COLS)]
                                 ).then_inc(slot_in[s], 16)
            side("sync_last", sp)

        @block.tensor
        def _(pe):
            side("tensor_early", pe)

            def turn(i):
                for j in range(PER):
                    s, half = j // 2, j % 2
                    if half == 0:
                        pe.wait_ge(slot_in[s], i * 16 + 16)
                    pe.wait_ge(tile_out, i * PER + (j + 1))
                    for kk in range(KD):
                        last = pe.matmul(k.banks[j % BANKS][:, 0:TOK], ring[s][:, kk, half * P:(half + 1) * P],
                                         k.hT[:, kk, :], start=(kk == 0), stop=(kk == KD - 1))
                    last.then_inc(tile_done, 1)
            turn(0)
            side("tensor_late", pe)
            with pe.Fori(1, TURNS) as i:
                turn(i)
                side("tensor_turn", pe, i - 1)
            side("tensor_last", pe)

        @block.scalar
        def _(act):
            act.sem_inc(tile_out, BANKS)
            side("scalar_early", act)

            def turn(i):
                for j in range(PER):
                    act.wait_ge(tile_done, i * PER + (j + 1))
                    act.activation(zT[:, bass.ds(i * PER + j, 1), :], k.banks[j % BANKS][:, 0:TOK].unsqueeze(1),
                                   ACT.Identity, bias=k.vcol[:, bass.ds(i * PER + (v0 + j), 1)]
                                   ).then_inc(tile_out, 1)
            turn(0)
            side("scalar_late", act)
            with act.Fori(1, TURNS) as i:
                turn(i)
                side("scalar_turn", act, i - 1)
            side("scalar_last", act)

        @block.vector
        def _(dve):
            side("vector", dve)


def short_conv(dve, go, out, z, wcol):
    go(dve.tensor_scalar(out, z, wcol(1), None, ALU.mult))
    for tap in (0, 2):
        for a, b, n in ((0, PROMPT, PROMPT), (PROMPT, TOK, CHUNK)):
            o = out[:, a:b].rearrange("p (r c) -> p r c", c=n)
            i = z[:, a:b].rearrange("p (r c) -> p r c", c=n)
            o, i = (o[:, :, 1:], i[:, :, :-1]) if tap == 0 else (o[:, :, :-1], i[:, :, 1:])
            last = dve.scalar_tensor_tensor(out=o, in0=i, scalar=wcol(tap), in1=o, op0=ALU.mult, op1=ALU.add)
            if tap == 0 or a == 0:
                go(last)
    return last


def hyena_rows(k, ctx, zT, tile_out, per, turns):
    sem = k.sem
    conv = [k.sb(ctx, f"hy_conv{s}", [P, TOK]) for s in range(per)]
    conv_done, conv_turned, rows_out = sem("hy_conv_done"), sem("hy_conv_turned"), sem("hy_rows_out")

    def vector(dve):
        go = Steps(dve, sem("hy_conv_step"))
        dve.sem_inc(conv_turned, per)
        n = WT // per
        for part in range(3):
            with dve.Fori(0, n) as i:
                go.enter(i, 4 * per)
                for s in range(per):
                    dve.wait_ge(tile_out, i * per + (part * WT + s + 1 + per))
                    dve.wait_ge(conv_turned, i * per + (part * WT + s + 1))

                    def wcol(tap, s=s):
                        return k.vcol[:, bass.ds(i * per + (V_HYCONV + (part * 3 + tap) * WT + s), 1)]
                    z = zT[:, bass.ds(i * per + (part * WT + s), 1), :].rearrange("p a t -> p (a t)")
                    short_conv(dve, go, conv[s][:, :], z, wcol).then_inc(conv_done, 1)
                go.leave(n)

    def tensor(pe, turn):
        for s in range(per):
            pe.wait_ge(conv_done, turn * per + (s + 1))
            pe.wait_ge(rows_out, turn * per + (s + 1))
            for r in range(TT):
                last = pe.transpose(k.banks[4 + s][:, r * P:(r + 1) * P], conv[s][:, r * P:(r + 1) * P],
                                    k.cst[:, C_ID:C_ID + P])
            last.then_inc(conv_turned, 1)

    def scalar(act, turn):
        for s in range(per):
            act.wait_ge(conv_turned, turn * per + (s + 1 + per))
            act.copy(k.uTM[:, :, bass.ds(turn * (per * P) + s * P, P)],
                     k.banks[4 + s][:, 0:TOK].rearrange("p (r c) -> p r c", c=P)).then_inc(rows_out, 1)

    return Side(vector=vector, tensor_turn=tensor, tensor_last=lambda pe: tensor(pe, turns - 1),
                scalar_early=lambda act: act.sem_inc(rows_out, per), scalar_turn=scalar,
                scalar_last=lambda act: scalar(act, turns - 1))


def stage_filters(k, ctx):
    nc, io, sem = k.nc, k.io, k.sem
    w1 = k.sb(ctx, "ffn_w1", [33, 64])
    w2 = k.sb(ctx, "ffn_w2", [64, 64])
    w3 = k.sb(ctx, "ffn_w3", [64, 4 * W])
    feat = k.sb(ctx, "features", [33, TOK])
    cols = k.sb(ctx, "ffn_cols", [64, 4])
    win = k.sb(ctx, "window", [P, TT, W])
    bias = k.sb(ctx, "lag0_bias", [1, 2, W])
    hid = [k.sb(ctx, f"hidden{n}", [64, TOK]) for n in range(2)]
    turns = k.sb(ctx, "turns", [64, TOK])
    fw, bw = k.sb(ctx, "filter_fwd", [P, W]), k.sb(ctx, "filter_bwd", [P, W])
    both = k.sb(ctx, "filter_sum_diff", [P, 2, 2, W])
    ffn_in, filt_in = sem("ffn_in"), sem("filter_in")
    hid_mm, arg_ready, hid_ready = sem("hidden_mm"), sem("sin_argument"), sem("hidden_ready")
    filt_mm, filt_read, filt_ready = sem("filter_mm"), sem("filter_read"), sem("filter_ready")
    spec_mm, spec_out = sem("spectrum_mm"), sem("spectrum_out")
    combos = [(name, o) for name in "ps" for o in range(2)]
    first, count = {"p": 0, "s": 1}, {"p": 1, "s": 2}

    with nc.Block() as block:
        @block.sync
        def _(sp):
            sp.dma_start(w1[:, :], io["hy_w1"][0]).then_inc(ffn_in, 16)
            sp.dma_start(w2[:, :], io["hy_w2"][0]).then_inc(ffn_in, 16)
            sp.dma_start(feat[:, 0:PROMPT], io["feat_p"]).then_inc(ffn_in, 16)
            sp.dma_start(feat[:, PROMPT:], io["feat_s"]).then_inc(ffn_in, 16)
            sp.dma_start(cols[:, 0:1], io["hy_b1"][0].unsqueeze(1)).then_inc(ffn_in, 16)
            sp.dma_start(cols[:, 1:2], io["hy_b2"][0].unsqueeze(1)).then_inc(ffn_in, 16)
            sp.dma_start(cols[:, 2:3], io["hy_freq"][0, 0].unsqueeze(1)).then_inc(ffn_in, 16)
            sp.dma_start(cols[:, 3:4], io["hy_freq"][0, 1].unsqueeze(1)).then_inc(ffn_in, 16)
            sp.dma_start(w3[:, :], io["hy_w3"][0]).then_inc(filt_in, 16)
            sp.dma_start(win[:, 0:1, :], io["win_p"]).then_inc(filt_in, 16)
            sp.dma_start(win[:, 1:3, :], io["win_s"]).then_inc(filt_in, 16)
            sp.dma_start(bias[:, :, :], io["hy_bias"]).then_inc(filt_in, 16)
            sp.dma_start(k.dft["p"][:, :, :, :], io["dft_p"]).then_inc(filt_in, 16)
            sp.dma_start(k.dft["s"][:, :, :, :], io["dft_s"]).then_inc(filt_in, 16)

        @block.tensor
        def _(pe):
            pe.wait_ge(ffn_in, 8 * 16)
            pe.matmul(k.banks[0][0:64, 0:TOK], w1[:, :], feat[:, :], start=True, stop=True).then_inc(hid_mm, 1)
            pe.wait_ge(hid_ready, 1)
            pe.matmul(k.banks[0][0:64, 0:TOK], w2[:, :], hid[0][:, :], start=True, stop=True).then_inc(hid_mm, 1)
            pe.wait_ge(hid_ready, 2)
            pe.wait_ge(filt_in, 6 * 16)
            tile, spec = 0, 0
            for n, (name, o) in enumerate(combos):
                for t in range(count[name]):
                    if tile:
                        pe.wait_ge(filt_read, tile)
                    at = (first[name] + t) * P
                    for b in range(4):
                        last = pe.matmul(k.banks[b][:, :], hid[1][:, at:at + P],
                                         w3[:, o * 2 * W + b * 512:o * 2 * W + (b + 1) * 512],
                                         start=True, stop=True)
                    last.then_inc(filt_mm, 1)
                    tile += 1
                pe.wait_ge(filt_ready, n + 1)
                dft = k.dft[name]
                for m in range(count[name]):
                    for part in range(2):
                        for half in range(2):
                            if spec >= 4:
                                pe.wait_ge(spec_out, spec - 3)
                            for t in range(count[name]):
                                last = pe.matmul(k.banks[4 + spec % 4][:, :], dft[:, part, t, m * P:(m + 1) * P],
                                                 both[:, t, part, half * 512:(half + 1) * 512],
                                                 start=(t == 0), stop=(t == count[name] - 1))
                            last.then_inc(spec_mm, 1)
                            spec += 1

        @block.scalar
        def _(act):
            for n in range(2):
                act.wait_ge(arg_ready, n + 1)
                act.activation(hid[n][:, :], hid[n][:, :], ACT.Sin).then_inc(hid_ready, 1)
            spec = 0
            for name, o in combos:
                for m in range(count[name]):
                    for part in range(2):
                        for half in range(2):
                            act.wait_ge(spec_mm, spec + 1)
                            act.copy(k.spec[:, first[name] + m, o, part, half * 512:(half + 1) * 512],
                                     k.banks[4 + spec % 4][:, :]).then_inc(spec_out, 1)
                            spec += 1

        @block.vector
        def _(dve):
            go = Steps(dve, sem("filter_step"))
            dve.wait_ge(ffn_in, 8 * 16)
            for n in range(2):
                dve.wait_ge(hid_mm, n + 1)
                go(dve.tensor_scalar(hid[n][:, :], k.banks[0][0:64, 0:TOK], cols[:, n:n + 1], cols[:, 2 + n:3 + n],
                                     ALU.add, ALU.mult))
                go(dve.tensor_scalar(turns[:, :], hid[n][:, :], 1.0 / (2.0 * math.pi), MAGIC, ALU.mult, ALU.add))
                go(dve.tensor_scalar(turns[:, :], turns[:, :], MAGIC, None, ALU.subtract))
                go(dve.scalar_tensor_tensor(out=hid[n][:, :], in0=turns[:, :], scalar=-TWO_PI_HI, in1=hid[n][:, :],
                                            op0=ALU.mult, op1=ALU.add))
                go(dve.scalar_tensor_tensor(out=hid[n][:, :], in0=turns[:, :], scalar=-TWO_PI_LO, in1=hid[n][:, :],
                                            op0=ALU.mult, op1=ALU.add))
                dve.tensor_scalar(hid[n][:, :], hid[n][:, :], PI_IN, -PI_IN, ALU.min, ALU.max).then_inc(arg_ready, 1)
            dve.wait_ge(filt_in, 6 * 16)
            tile, spec = 0, 0
            for n, (name, o) in enumerate(combos):
                if spec:
                    dve.wait_ge(spec_mm, spec)
                for t in range(count[name]):
                    dve.wait_ge(filt_mm, tile + 1)
                    for b in range(4):
                        dst = (fw, bw)[b // 2][:, b % 2 * 512:(b % 2 + 1) * 512]
                        last = dve.tensor_tensor(dst, k.banks[b][:, :],
                                                 win[:, first[name] + t, b % 2 * 512:(b % 2 + 1) * 512], ALU.mult)
                        if b < 3:
                            go(last, wait=False)
                    last.then_inc(filt_read, 1)
                    tile += 1
                    dve.wait_ge(filt_read, tile)
                    if t == 0:
                        go(dve.tensor_tensor(fw[0:1, :], fw[0:1, :], bias[:, o, :], ALU.add))
                        go(dve.memset(bw[0:1, :], 0.0))
                    go(dve.tensor_tensor(both[:, t, 0, :], fw[:, :], bw[:, :], ALU.add))
                    last = dve.tensor_tensor(both[:, t, 1, :], fw[:, :], bw[:, :], ALU.subtract)
                    if t == count[name] - 1:
                        last.then_inc(filt_ready, 1)
                        dve.wait_ge(filt_ready, n + 1)
                    else:
                        go(last)
                spec += 4 * count[name]


def stage_hyena(k, ctx):
    nc, sem = k.nc, k.sem
    uf = k.sb(ctx, "u_spectrum", [P, TT, 2, W])
    yf = k.sb(ctx, "y_spectrum", [P, TT, 2, W])
    tmp = k.sb(ctx, "product", [P, W])
    u_mm, u_out, y_ready = sem("u_mm"), sem("u_out"), sem("y_spectrum_ready")
    y_mm, rows_ready = sem("y_mm"), sem("hy_rows_ready")
    y_turned, y_stored = sem("hy_y_turned"), sem("hy_y_stored")
    units = [(g, o) for o in range(2) for g in "ps"]
    tiles = {"p": (0,), "s": (1, 2)}
    first = {"p": 0, "s": 1}
    H = lambda half: slice(half * 512, (half + 1) * 512)
    rows = k.uTM[:, :, 2 * W:]

    with nc.Block() as block:
        @block.tensor
        def _(pe):
            u = y = 0
            for o in range(2):
                for g in "ps":
                    if o:
                        pe.wait_ge(rows_ready, 2 * (first[g] + len(tiles[g])))
                    for m in tiles[g]:
                        for part in range(2):
                            for half in range(2):
                                if u >= 4:
                                    pe.wait_ge(u_out, u - 3)
                                for t in tiles[g]:
                                    mt = (m - first[g]) * P
                                    last = pe.matmul(k.banks[u % 4][:, :],
                                                     k.dft[g][:, part, t - first[g], mt:mt + P],
                                                     rows[:, t, H(half)], start=(t == tiles[g][0]),
                                                     stop=(t == tiles[g][-1]))
                                last.then_inc(u_mm, 1)
                                u += 1
                for g in "ps":
                    pe.wait_ge(y_ready, TT * o + first[g] + len(tiles[g]))
                    for t in tiles[g]:
                        for half in range(2):
                            if y >= 4:
                                pe.wait_ge(rows_ready, y - 3)
                            for part in range(2):
                                for m in tiles[g]:
                                    tt = (t - first[g]) * P
                                    last = pe.matmul(k.banks[4 + y % 4][:, :],
                                                     k.dft[g][:, 2 + part, m - first[g], tt:tt + P],
                                                     yf[:, m, part, H(half)],
                                                     start=(part == 0 and m == tiles[g][0]),
                                                     stop=(part == 1 and m == tiles[g][-1]))
                            last.then_inc(y_mm, 1)
                            y += 1
            pe.wait_ge(rows_ready, 4 * TT)
            for c in range(WT):
                if c >= 4:
                    pe.wait_ge(y_stored, c - 3)
                for t in range(TT):
                    last = pe.transpose(k.banks[c % 4][:, t * P:(t + 1) * P], rows[:, t, c * P:(c + 1) * P],
                                        k.cst[:, C_ID:C_ID + P])
                last.then_inc(y_turned, 1)

        @block.scalar
        def _(act):
            u = 0
            for o in range(2):
                for m in range(TT):
                    if o:
                        act.wait_ge(y_ready, m + 1)
                    for part in range(2):
                        for half in range(2):
                            act.wait_ge(u_mm, u + 1)
                            act.copy(uf[:, m, part, H(half)], k.banks[u % 4][:, :]).then_inc(u_out, 1)
                            u += 1
            for c in range(WT):
                act.wait_ge(y_turned, c + 1)
                act.copy(k.yT[0][:, c, :], k.banks[c % 4][:, 0:TOK]).then_inc(y_stored, 1)

        @block.vector
        def _(dve):
            go = Steps(dve, sem("hyena_step"))
            y = 0
            for o in range(2):
                for m in range(TT):
                    dve.wait_ge(u_out, 4 * (TT * o + m + 1))
                    if o:
                        dve.wait_ge(y_mm, 2 * TT)
                    ur, us = uf[:, m, 0, :], uf[:, m, 1, :]
                    hr, hs = k.spec[:, m, o, 0, :], k.spec[:, m, o, 1, :]
                    go(dve.tensor_tensor(yf[:, m, 0, :], ur, hr, ALU.mult), wait=False)
                    go(dve.tensor_tensor(tmp[:, :], us, hs, ALU.mult))
                    go(dve.tensor_tensor(yf[:, m, 0, :], yf[:, m, 0, :], tmp[:, :], ALU.subtract))
                    go(dve.tensor_tensor(yf[:, m, 1, :], ur, hs, ALU.mult), wait=False)
                    go(dve.tensor_tensor(tmp[:, :], us, hr, ALU.mult))
                    dve.tensor_tensor(yf[:, m, 1, :], yf[:, m, 1, :], tmp[:, :], ALU.add).then_inc(y_ready, 1)
                    dve.wait_ge(y_ready, TT * o + m + 1)
                for t in range(TT):
                    for half in range(2):
                        dve.wait_ge(y_mm, y + 1)
                        dve.tensor_tensor(rows[:, t, H(half)], k.banks[4 + y % 4][:, :], k.uTM[:, t, o * W + half * 512:o * W + (half + 1) * 512],
                                          ALU.mult).then_inc(rows_ready, 1)
                        y += 1


def chunk_of(group, turn, backward):
    first, count = group
    return turn * -1 + (first + count - 1) if backward else turn + first


def gla_memory(k, ctx):
    vTM = k.sb(ctx, "gla_v", [CHUNK, NC, W])
    oTM = k.sb(ctx, "gla_o", [P, NC, W])
    b = k.sb(ctx, "gla_cumulated", [P, 2, HEADS, TOK])
    state = k.sb(ctx, "gla_state", [P, 2, HEADS, DV])
    return vTM, oTM, b, state


def stage_gla(k, ctx, zT, mem):
    with ExitStack() as scan:
        gla_scan(k, scan, zT, *mem)
    with ExitStack() as post:
        stage_heads_out(k, post, "gla", mem[1], zT[:, 16:24, :], ACT.Silu, V_GLAN, k.yT[1])


def gla_prepare(k, ctx, zT, tile_out, per, turns, vTM, oTM, b, state):
    nc, io, sem = k.nc, k.io, k.sem
    wlr = k.sb(ctx, "lr_w", [P, KD, 32])
    blr = k.sb(ctx, "lr_bias", [16, 2])
    a2 = k.sb(ctx, "gla_a2", [17, 2, HEADS * DK])
    lg = oTM[:, 3:6, :].rearrange("p c (d n) -> p c d n", d=2)
    mag = oTM[:, 0:3, :].rearrange("p c (d n) -> p c d n", d=2)
    lr_in, state_in, v_turned, v_out = sem("lr_in"), sem("gla_state_in"), sem("gla_v_turned"), sem("gla_v_out")
    lr_mm, lr_ready, x_mm, x_read = sem("lr_mm"), sem("lr_ready"), sem("gate_mm"), sem("gate_read")
    soft, lg_ready, sum_mm, sum_out = sem("softplus_done"), sem("log_gate_ready"), sem("cumsum_mm"), sem("cumsum_out")

    def sync_early(sp):
        sp.dma_start(wlr[:, :, :], io["w_in"][0].rearrange("(k p) n -> p k n", p=P)[:, :, COL_LR:COL_ML]
                     ).then_inc(lr_in, 16)
        sp.dma_start(blr[:, :], io["b_in"][0, COL_LR:COL_ML].rearrange("(d r) -> r d", d=2),
                     allow_slow_non_contiguous=True).then_inc(lr_in, 16)
        sp.dma_start(a2[0:16, :, :], io["gla_a2_w"][0].rearrange("d r n -> r d n")).then_inc(lr_in, 16)
        sp.dma_start(a2[16:17, :, :], io["gla_a2_b"]).then_inc(lr_in, 16)

    def sync_states(sp):
        sp.dma_start(state[:, :, :, :], io["state_gla"][0, 0].rearrange("d h p v -> p d h v")).then_inc(state_in, 16)

    def sync_last(sp):
        sp.wait_ge(state_in, 16)

    def tensor_early(pe):
        pe.wait_ge(lr_in, 4 * 16)
        for d in range(2):
            for kk in range(KD):
                last = pe.matmul(k.banks[4 + d][0:16, 0:TOK], wlr[:, kk, 16 * d:16 * d + 16], k.hT[:, kk, :],
                                 start=(kk == 0), stop=(kk == KD - 1))
            last.then_inc(lr_mm, 1)
        pe.wait_ge(lr_ready, 2)
        for n in range(2 * TT):
            t, d = n // 2, n % 2
            if n >= 4:
                pe.wait_ge(x_read, n - 3)
            pe.matmul(k.banks[4 + n % 4][:, :], k.lrT[:, d, t * P:(t + 1) * P], a2[:, d, :],
                      start=True, stop=True).then_inc(x_mm, 1)

    def tensor_late(pe):
        pe.wait_ge(lg_ready, 1)
        for n in range(2 * HEADS):
            d, h = n // HEADS, n % HEADS
            if n >= 4:
                pe.wait_ge(sum_out, n - 3)
            for t in range(TT):
                last = pe.matmul(k.banks[4 + n % 4][:, t * P:(t + 1) * P], lg[:, t, d, h * DK:(h + 1) * DK],
                                 k.cst[:, C_TRI + d * P:C_TRI + (d + 1) * P], start=True, stop=True)
            last.then_inc(sum_mm, 1)

    def tensor_last(pe):
        pe.wait_ge(tile_out, per * (turns + 1))
        pe.wait_ge(sum_out, 2 * HEADS)
        for n in range(NC * 2):
            if n >= 4:
                pe.wait_ge(v_out, n - 3)
            c, g = n // 2, n % 2
            for t in range(4):
                last = pe.transpose(k.banks[4 + n % 4][0:CHUNK, t * P:(t + 1) * P],
                                    zT[:, 8 + 4 * g + t, c * CHUNK:(c + 1) * CHUNK], k.cst[:, C_ID:C_ID + P])
            last.then_inc(v_turned, 1)

    def scalar_early(act):
        act.wait_ge(x_read, 2 * TT)
        act.activation(mag, mag, ACT.Exp, scale=-1.0).then_inc(soft, 1)
        act.wait_ge(soft, 1)
        act.activation(mag, mag, ACT.Ln, bias=1.0).then_inc(soft, 1)

    def scalar_late(act):
        for n in range(2 * HEADS):
            act.wait_ge(sum_mm, n + 1)
            act.copy(b[:, n // HEADS, n % HEADS, :], k.banks[4 + n % 4][:, 0:TOK]).then_inc(sum_out, 1)

    def scalar_last(act):
        for n in range(NC * 2):
            act.wait_ge(v_turned, n + 1)
            act.copy(vTM[:, n // 2, n % 2 * 512:(n % 2 + 1) * 512], k.banks[4 + n % 4][0:CHUNK, :]).then_inc(v_out, 1)

    def vector(dve):
        go = Steps(dve, sem("gla_prepare_step"))
        dve.memset(k.lrT[:, :, :], 1.0).then_inc(lr_ready, 1)
        dve.wait_ge(lr_ready, 1)
        dve.wait_ge(lr_in, 4 * 16)
        for d in range(2):
            dve.wait_ge(lr_mm, d + 1)
            last = dve.tensor_scalar(k.lrT[0:16, d, :], k.banks[4 + d][0:16, 0:TOK], blr[:, d:d + 1], None, ALU.add)
        last.then_inc(lr_ready, 1)
        for n in range(2 * TT):
            dve.wait_ge(x_mm, n + 1)
            go(dve.tensor_scalar(lg[:, n // 2, n % 2, :], k.banks[4 + n % 4][:, :], 0.0, None, ALU.min))
            dve.scalar_tensor_tensor(out=mag[:, n // 2, n % 2, :], in0=lg[:, n // 2, n % 2, :], scalar=-2.0,
                                     in1=k.banks[4 + n % 4][:, :], op0=ALU.mult, op1=ALU.add).then_inc(x_read, 1)
        dve.wait_ge(x_read, 2 * TT)
        dve.wait_ge(soft, 2)
        dve.tensor_tensor(lg, lg, mag, ALU.subtract).then_inc(lg_ready, 1)

    return Side(sync_early=sync_early, sync_states=sync_states, sync_last=sync_last, tensor_early=tensor_early,
                tensor_late=tensor_late, tensor_last=tensor_last, scalar_early=scalar_early,
                scalar_late=scalar_late, scalar_last=scalar_last, vector=vector)


def gla_scan(k, ctx, zT, vTM, oTM, b, state):
    nc, io, sem = k.nc, k.io, k.sem
    sub_k = [k.sb(ctx, f"gla_sub_k{d}", [P, NSUB, HEADS, CHUNK]) for d in range(2)]
    e3 = [k.sb(ctx, f"gla_e3{d}", [P, 3, HEADS, CHUNK]) for d in range(2)]
    att = [k.sb(ctx, f"gla_att{d}", [CHUNK, HEADS, CHUNK]) for d in range(2)]
    k_rows = [k.sb(ctx, f"gla_k_rows{d}", [CHUNK, HEADS * DK]) for d in range(2)]
    end = [k.sb(ctx, f"gla_end{d}", [P, HEADS]) for d in range(2)]
    v_now = [k.sb(ctx, f"gla_v_now{d}", [CHUNK, W]) for d in range(2)]
    v_ready = sem("gla_v_ready")
    diff_ready, exp_done, prep_done = sem("gla_diff_ready"), sem("gla_exp_done"), sem("gla_prep_done")
    inter_exp_done, inter_done = sem("gla_inter_exp_done"), sem("gla_inter_done")
    att_mm, att_ready, k_turned, k_out = sem("gla_att_mm"), sem("gla_att_ready"), sem("gla_k_turned"), sem("gla_k_out")
    o_mm, o_read, state_mm, state_ready = sem("gla_o_mm"), sem("gla_o_read"), sem("gla_state_mm"), sem("gla_state_ready")
    state_stored = sem("gla_state_stored")
    runs = ((GROUPS[1], 0, 0), (GROUPS[0], 2 * GROUPS[1][1], 2 * GROUPS[1][1] + 2))
    qs = DK ** -0.5

    def toks(group, i, d):
        return bass.ds(chunk_of(group, i, d) * CHUNK, CHUNK)

    with nc.Block() as block:
        @block.vector
        def _(dve):
            go = Steps(dve, sem("gla_step"))
            go(dve.memset(oTM[0:CHUNK, :, :], 0.0))
            dve.sem_inc(o_read, 1)
            dve.sem_inc(state_ready, 2)

            def differences(group, i, q0):
                for d in range(2):
                    bc = b[:, d, :, toks(group, i, d)]
                    sub = bc.rearrange("p h (i s) -> p i h s", s=SUB)
                    ref = sub[:, :, :, SUB // 2:SUB // 2 + 1].broadcast_to([P, NSUB, HEADS, CHUNK])
                    dif = sub_k[d]
                    go(dve.tensor_tensor(dif[:, :, :, :], ref, bc.unsqueeze(1).broadcast_to([P, NSUB, HEADS, CHUNK]),
                                         ALU.subtract))
                    go(dve.tensor_scalar(dif[:, :, :, :], dif[:, :, :, :], MAX_EXP, None, ALU.min), wait=False)
                    own = bc.rearrange("p h (i s) -> p h i s", s=SUB)
                    go(dve.tensor_tensor(e3[d][:, 0].rearrange("p h (i s) -> p h i s", s=SUB), own,
                                         own[:, :, :, SUB // 2:SUB // 2 + 1].broadcast_to([P, HEADS, NSUB, SUB]),
                                         ALU.subtract), wait=False)
                    last = bc[:, :, 0:1] if d else bc[:, :, CHUNK - 1:CHUNK]
                    dve.tensor_tensor(e3[d][:, 1], last.broadcast_to([P, HEADS, CHUNK]), bc, ALU.subtract
                                      ).then_inc(diff_ready, 1)

            def turn(group, i, q0, more):
                for d in range(2):
                    q = i * 2 + (q0 + d)
                    qc, kc = zT[:, 0:4, toks(group, i, d)], zT[:, 4:8, toks(group, i, d)]
                    dve.wait_ge(exp_done, q * 2 + 2)
                    go(dve.tensor_tensor(sub_k[d][:, :, :, :], sub_k[d][:, :, :, :],
                                         kc.unsqueeze(1).broadcast_to([P, NSUB, HEADS, CHUNK]), ALU.mult), wait=False)
                    go(dve.scalar_tensor_tensor(out=e3[d][:, 0], in0=e3[d][:, 0], scalar=qs, in1=qc,
                                                op0=ALU.mult, op1=ALU.mult), wait=False)
                    dve.tensor_tensor(e3[d][:, 1], e3[d][:, 1], kc, ALU.mult).then_inc(prep_done, 1)
                for d in range(2):
                    q = i * 2 + (q0 + d)
                    dve.wait_ge(inter_exp_done, q + 1)
                    at = 0 if d else CHUNK - 1
                    go(dve.tensor_copy(end[d][:, :].unsqueeze(2), e3[d][:, 2, :, at:at + 1]))
                    dve.scalar_tensor_tensor(out=e3[d][:, 2], in0=e3[d][:, 2], scalar=qs,
                                             in1=zT[:, 0:4, toks(group, i, d)],
                                             op0=ALU.mult, op1=ALU.mult).then_inc(inter_done, 1)
                for d in range(2):
                    q = i * 2 + (q0 + d)
                    dve.wait_ge(att_mm, q + 1)
                    mask = k.cst[0:CHUNK, C_GMASK + d * CHUNK:C_GMASK + (d + 1) * CHUNK]
                    dve.tensor_tensor(att[d][:, :, :], k.banks[d][0:CHUNK, 0:HEADS * CHUNK].rearrange(
                        "p (h t) -> p h t", h=HEADS), mask.unsqueeze(1).broadcast_to([CHUNK, HEADS, CHUNK]),
                        ALU.mult).then_inc(att_ready, 1)
                if more:
                    dve.wait_ge(k_turned, i * 2 + (q0 + 2))
                    differences(group, i + 1, q0)
                for d in range(2):
                    q = i * 2 + (q0 + d)
                    dve.wait_ge(o_mm, q + 1)
                    for half in range(2):
                        o = oTM[0:CHUNK, bass.ds(chunk_of(group, i, d), 1), half * 512:(half + 1) * 512]
                        add = dve.tensor_tensor(o, k.banks[4 + half][0:CHUNK, :].unsqueeze(1), o, ALU.add)
                    add.then_inc(o_read, 1)
                    dve.wait_ge(state_mm, q + 1)
                    for h in range(HEADS):
                        part = dve.scalar_tensor_tensor(
                            out=state[:, d, h, :], in0=state[:, d, h, :], scalar=end[d][:, h:h + 1],
                            in1=k.banks[6 + h // 2][:, h % 2 * DV:(h % 2 + 1) * DV], op0=ALU.mult, op1=ALU.add)
                        if h < HEADS - 1:
                            go(part, wait=False)
                    part.then_inc(state_ready, 1)

            for group, q0, s0 in runs:
                if q0:
                    dve.wait_ge(state_mm, q0)
                    dve.wait_ge(state_ready, q0 + 2)
                    dve.memset(state[:, :, :, :], 0.0).then_inc(state_ready, 2)
                    dve.wait_ge(state_ready, q0 + 4)
                differences(group, 0, q0)
                with dve.Fori(0, group[1] - 1) as i:
                    go.enter(i, 2 * (2 + 1 + 3 + 3))
                    turn(group, i, q0, True)
                    go.leave(group[1] - 1)
                turn(group, group[1] - 1, q0, False)

        @block.scalar
        def _(act):
            def exps(group, i, q0):
                for d in range(2):
                    act.wait_ge(diff_ready, i * 2 + (q0 + d + 1))
                    act.activation(sub_k[d][:, :, :, :], sub_k[d][:, :, :, :], ACT.Exp).then_inc(exp_done, 1)
                    act.activation(e3[d][:, 0:2], e3[d][:, 0:2], ACT.Exp).then_inc(exp_done, 1)

            def turn(group, i, q0, s0, more):
                for d in range(2):
                    q = i * 2 + (q0 + d)
                    act.wait_ge(state_ready, i * 2 + (s0 + d + 1))
                    act.activation(e3[d][:, 2], b[:, d, :, toks(group, i, d)], ACT.Exp).then_inc(inter_exp_done, 1)
                    act.copy(v_now[d][:, :].unsqueeze(1), vTM[:, bass.ds(chunk_of(group, i, d), 1), :]
                             ).then_inc(v_ready, 1)
                    act.wait_ge(k_turned, q + 1)
                    act.copy(k_rows[d][:, :], k.banks[2 + d][0:CHUNK, :]).then_inc(k_out, 1)
                if more:
                    exps(group, i + 1, q0)

            for group, q0, s0 in runs:
                exps(group, 0, q0)
                with act.Fori(0, group[1] - 1) as i:
                    turn(group, i, q0, s0, True)
                turn(group, group[1] - 1, q0, s0, False)

        @block.tensor
        def _(pe):
            for group, q0, s0 in runs:
                with pe.Fori(0, group[1]) as i:
                    for d in range(2):
                        q = i * 2 + (q0 + d)
                        pe.wait_ge(prep_done, q + 1)
                        for h in range(HEADS):
                            for s in range(NSUB):
                                at = h * CHUNK + s * SUB
                                mm = pe.matmul(k.banks[d][0:CHUNK, at:at + SUB], sub_k[d][:, s, h, :],
                                               e3[d][:, 0, h, s * SUB:(s + 1) * SUB], start=True, stop=True)
                        mm.then_inc(att_mm, 1)
                        for h in range(HEADS):
                            mm = pe.transpose(k.banks[2 + d][0:CHUNK, h * DK:(h + 1) * DK], e3[d][:, 1, h, :],
                                              k.cst[:, C_ID:C_ID + P])
                        mm.then_inc(k_turned, 1)
                    for d in range(2):
                        q = i * 2 + (q0 + d)
                        v = lambda h: v_now[d][:, h * DV:(h + 1) * DV]
                        pe.wait_ge(att_ready, q + 1)
                        pe.wait_ge(v_ready, q + 1)
                        pe.wait_ge(inter_done, q + 1)
                        pe.wait_ge(o_read, q + 1)
                        pe.wait_ge(state_ready, i * 2 + (s0 + d + 1))
                        for h in range(HEADS):
                            out = k.banks[4 + h // 2][0:CHUNK, h % 2 * DV:(h % 2 + 1) * DV]
                            pe.matmul(out, e3[d][:, 2, h, :], state[:, d, h, :], start=True, stop=False)
                            mm = pe.matmul(out, att[d][:, h, :], v(h), start=False, stop=True)
                        mm.then_inc(o_mm, 1)
                        pe.wait_ge(k_out, q + 1)
                        pe.wait_ge(state_ready, i * 2 + (s0 + d + 2))
                        for h in range(HEADS):
                            mm = pe.matmul(k.banks[6 + h // 2][:, h % 2 * DV:(h % 2 + 1) * DV],
                                           k_rows[d][:, h * DK:(h + 1) * DK], v(h), start=True, stop=True)
                        mm.then_inc(state_mm, 1)

        @block.sync
        def _(sp):
            sp.wait_ge(state_ready, 2 * NC + 4)
            sp.dma_start(io["new_state_gla"][0, 0].rearrange("d h p v -> p d h v"), state[:, :, :, :]
                         ).then_inc(state_stored, 16)
            sp.wait_ge(state_stored, 16)


def stage_heads_out(k, ctx, name, oTM, gateT, func, gain, yT):
    nc, sem = k.nc, k.sem
    sq = [k.sb(ctx, f"{name}_squares{n}", [CHUNK, W]) for n in range(2)]
    ss = k.sb(ctx, name + "_head_sums", [CHUNK, NC, HEADS])
    squared, sums_ready, root_done = sem(name + "_squared"), sem(name + "_sums_ready"), sem(name + "_root_done")
    inverse, scaled = sem(name + "_inverse"), [sem(f"{name}_scaled{n}") for n in range(2)]
    gate_done, turned, written = sem(name + "_gate_done"), sem(name + "_turned"), sem(name + "_written")
    head = lambda h: slice(h * DV, (h + 1) * DV)
    with nc.Block() as block:
        @block.scalar
        def _(act):
            for c in range(1, NC, 2):
                for h in range(HEADS):
                    if c > 1:
                        act.wait_ge(squared, c // 2 * HEADS + h - HEADS + 1)
                    act.activation(sq[1][:, head(h)], oTM[0:CHUNK, c, head(h)], ACT.Square,
                                   accum_out=ss[:, c, h:h + 1]).then_inc(squared, 1)
            act.activation(gateT, gateT, func).then_inc(gate_done, 1)
            act.wait_ge(sums_ready, 1)
            act.activation(ss[:, :, :], ss[:, :, :], ACT.Sqrt).then_inc(root_done, 1)
            act.wait_ge(inverse, 1)
            for c in range(1, NC, 2):
                for h in range(HEADS):
                    act.activation(oTM[0:CHUNK, c, head(h)], oTM[0:CHUNK, c, head(h)], ACT.Copy,
                                   scale=ss[:, c, h:h + 1]).then_inc(scaled[1], 1)

        @block.vector
        def _(dve):
            go = Steps(dve, sem(name + "_head_step"))
            for c in range(0, NC, 2):
                o = oTM[0:CHUNK, c, :]
                go(dve.tensor_tensor(sq[0][:, :], o, o, ALU.mult))
                go(dve.tensor_reduce(ss[:, c, :], sq[0][:, :].rearrange("p (h v) -> p h v", h=HEADS), AX_X, ALU.add))
            dve.wait_ge(squared, NC // 2 * HEADS)
            dve.tensor_scalar(ss[:, :, :], ss[:, :, :], 1.0 / DV, EPS, ALU.mult, ALU.add).then_inc(sums_ready, 1)
            dve.wait_ge(root_done, 1)
            dve.reciprocal(ss[:, :, :], ss[:, :, :]).then_inc(inverse, 1)
            dve.wait_ge(inverse, 1)
            for c in range(0, NC, 2):
                o = oTM[0:CHUNK, c, :].rearrange("p (h v) -> p h v", h=HEADS)
                dve.tensor_tensor(o, o, ss[:, c, :].unsqueeze(2).broadcast_to([CHUNK, HEADS, DV]), ALU.mult
                                  ).then_inc(scaled[0], 1)
            dve.wait_ge(gate_done, 1)
            for t in range(WT):
                dve.wait_ge(turned, t + 1)
                g = gain + t % 2
                dve.scalar_tensor_tensor(out=yT[:, t, :], in0=k.banks[t][:, 0:TOK], scalar=k.vcol[:, g:g + 1],
                                         in1=gateT[:, t, :], op0=ALU.mult, op1=ALU.mult).then_inc(written, 1)

        @block.tensor
        def _(pe):
            for c in range(NC):
                pe.wait_ge(scaled[c % 2], (c // 2 + 1) * (HEADS if c % 2 else 1))
                for t in range(WT):
                    mm = pe.transpose(k.banks[t][:, c * CHUNK:(c + 1) * CHUNK],
                                      oTM[0:CHUNK, c, t * P:(t + 1) * P], k.cst[0:CHUNK, C_ID:C_ID + CHUNK])
                    if c == NC - 1:
                        mm.then_inc(turned, 1)


def mlstm_memory(k, ctx):
    rows = k.sb(ctx, "ml_rows", [HEADS, 2, 2, TOK])
    cols = k.sb(ctx, "ml_cols", [CHUNK, 3, 2, NC, HEADS])
    keep = k.sb(ctx, "ml_keep", [P, 2, NC, HEADS])
    state = k.sb(ctx, "ml_state", [P, 2, 2 * HEADS, DV])
    norm = k.sb(ctx, "ml_norm", [P, 2, 2 * HEADS])
    return rows, cols, keep, state, norm


def stage_mlstm(k, ctx, zT, mem):
    oTM = k.sb(ctx, "ml_o", [CHUNK, NC, W])
    with ExitStack() as inner:
        mlstm_scan(k, inner, zT, oTM, *mem)
    with ExitStack() as post:
        stage_heads_out(k, post, "ml", oTM, zT[:, 24:32, :], ACT.Sigmoid, V_MLN, k.yT[2])


def mlstm_prepare(k, ctx, zT, tile_out, per, turns, rows, cols, keep, state, norm):
    nc, io, sem = k.nc, k.io, k.sem
    wg = k.sb(ctx, "ml_gate_w", [P, KD, 16])
    bg = k.sb(ctx, "ml_gate_bias", [HEADS, 2, 2, 2])
    gates = k.sb(ctx, "ml_gates", [HEADS, 2, 2, TOK])
    mag = k.sb(ctx, "ml_gate_mag", [HEADS, 2, TOK])
    zero = k.sb(ctx, "ml_zero", [HEADS, CHUNK])
    b = k.sb(ctx, "ml_b", [HEADS, 2, TOK])
    top = k.sb(ctx, "ml_running_max", [HEADS, 2, TOK])
    quant = k.sb(ctx, "ml_quantities", [HEADS, 3, 2, TOK])
    enter = k.sb(ctx, "ml_m_enter", [HEADS, 2, NC])
    leave = k.sb(ctx, "ml_m_leave", [HEADS, 2, NC])
    decay = k.sb(ctx, "ml_decay", [HEADS, 2, NC])
    m0 = k.sb(ctx, "ml_m_start", [HEADS, 2])
    conv = k.sb(ctx, "ml_conv", [P, TOK])
    g_in, state_in, m_stored = sem("ml_gate_in"), sem("ml_state_in"), sem("ml_m_stored")
    g_mm, g_read, soft, m_ready = sem("ml_gate_mm"), sem("ml_gate_read"), sem("ml_softplus"), sem("ml_m_ready")
    exps_ready, exps_done, turned = sem("ml_exps_ready"), sem("ml_exps_done"), sem("ml_cols_turned")
    cols_out = sem("ml_cols_out")

    def sync_early(sp):
        sp.dma_start(wg[:, :, :], io["w_in"][0].rearrange("(k p) n -> p k n", p=P)[:, :, COL_IF:COL_GATE]
                     ).then_inc(g_in, 16)
        for x in range(2):
            at = COL_IF + x * 2 * HEADS
            sp.dma_start(bg[:, 0, x, :], io["b_in"][0, at:at + 2 * HEADS].rearrange("(d h) -> h d", h=HEADS),
                         allow_slow_non_contiguous=True).then_inc(g_in, 16)
            sp.dma_start(bg[:, 1, x, :], io["ml_gate_b"][0, :, x, :].rearrange("d h -> h d"),
                         allow_slow_non_contiguous=True).then_inc(g_in, 16)
        sp.dma_start(m0[:, :], io["state_mlstm_m"][0, 0].rearrange("d h -> h d"),
                     allow_slow_non_contiguous=True).then_inc(g_in, 16)

    def sync_states(sp):
        for d in range(2):
            sp.dma_start(state[:, d, :, :], io["state_mlstm_C"][0, 0, d].rearrange("h (j p) v -> p (h j) v", p=P)
                         ).then_inc(state_in, 16)
            sp.dma_start(norm[:, d, :], io["state_mlstm_n"][0, 0, d].rearrange("h (j p) -> p (h j)", p=P),
                         allow_slow_non_contiguous=True).then_inc(state_in, 16)

    def sync_last(sp):
        sp.wait_ge(state_in, 4 * 16)
        sp.wait_ge(m_ready, 1)
        for d in range(2):
            sp.dma_start(io["new_state_mlstm_m"][0, 0, d].unsqueeze(1), leave[:, d, 1 - d:2 - d],
                         allow_slow_non_contiguous=True).then_inc(m_stored, 16)
        sp.wait_ge(m_stored, 32)

    def tensor_early(pe):
        pe.wait_ge(g_in, 6 * 16)
        for n in range(4):
            for kk in range(KD):
                mm = pe.matmul(k.banks[4 + n][0:HEADS, 0:TOK], wg[:, kk, n * HEADS:(n + 1) * HEADS], k.hT[:, kk, :],
                               start=(kk == 0), stop=(kk == KD - 1))
            mm.then_inc(g_mm, 1)

    def tensor_late(pe):
        pe.wait_ge(exps_done, 3)
        pe.wait_ge(g_read, 4)
        for n in range(3 * 2 * NC):
            q, d, c = n // (2 * NC), n // NC % 2, n % NC
            pe.transpose(k.banks[4][0:CHUNK, n * HEADS:(n + 1) * HEADS],
                         quant[:, q, d, c * CHUNK:(c + 1) * CHUNK], k.cst[0:HEADS, C_ID:C_ID + HEADS])
        for h in range(HEADS):
            mm = pe.matmul(k.banks[5][:, h * 2 * NC:(h + 1) * 2 * NC], k.cst[0:HEADS, C_SEL + h * P:C_SEL + (h + 1) * P],
                           decay[:, :, :].rearrange("h d c -> h (d c)"), start=True, stop=True)
        mm.then_inc(turned, 1)

    def scalar_early(act):
        act.wait_ge(g_read, 5)
        act.activation(mag[:, :, :], mag[:, :, :], ACT.Exp, scale=-1.0).then_inc(soft, 1)
        act.wait_ge(soft, 1)
        act.activation(mag[:, :, :], mag[:, :, :], ACT.Ln, bias=1.0).then_inc(soft, 1)

    def scalar_late(act):
        act.wait_ge(exps_ready, 1)
        act.activation(rows[:, 1], rows[:, 1], ACT.Exp).then_inc(exps_done, 1)
        act.activation(quant[:, 1:3], quant[:, 1:3], ACT.Exp).then_inc(exps_done, 1)
        act.activation(decay[:, :, :], decay[:, :, :], ACT.Exp).then_inc(exps_done, 1)

    def vector(dve):
        go = Steps(dve, sem("ml_prepare_step"))
        go(dve.memset(zero[:, :], 0.0))
        dve.wait_ge(g_in, 6 * 16)
        go(dve.tensor_tensor(bg[:, 0], bg[:, 0], bg[:, 1], ALU.add))
        for n in range(4):
            dve.wait_ge(g_mm, n + 1)
            dve.tensor_scalar(gates[:, n // 2, n % 2, :], k.banks[4 + n][0:HEADS, 0:TOK],
                              bg[:, 0, n // 2, n % 2:n % 2 + 1], None, ALU.add).then_inc(g_read, 1)
        dve.wait_ge(g_read, 4)
        go(dve.tensor_scalar(mag[:, :, :], gates[:, 1], 0.0, None, ALU.min))
        dve.scalar_tensor_tensor(out=mag[:, :, :], in0=mag[:, :, :], scalar=-2.0, in1=gates[:, 1],
                                 op0=ALU.mult, op1=ALU.add).then_inc(g_read, 1)
        dve.wait_ge(g_read, 5)
        go(dve.tensor_scalar(gates[:, 1], gates[:, 1], 0.0, None, ALU.min))
        dve.wait_ge(soft, 2)
        go(dve.tensor_tensor(gates[:, 1], gates[:, 1], mag[:, :, :], ALU.subtract))
        cut = lambda t, d, c: t[:, d, c * CHUNK:(c + 1) * CHUNK][:, ::-1 if d else 1]
        a = quant[:, 0]
        for d in range(2):
            for c in range(NC):
                go(dve.tensor_tensor_scan(cut(b, d, c), cut(gates[:, 1], d, c), zero[:, :], 0.0,
                                          ALU.add, ALU.add), wait=False)
        go(dve.memset(enter[:, :, :], 0.0))
        go(dve.tensor_tensor(a, gates[:, 0], b[:, :, :], ALU.subtract))
        for d in range(2):
            for c in range(NC):
                go(dve.tensor_tensor_scan(cut(top, d, c), cut(a, d, c), cut(a, d, c), -3.0e38,
                                          ALU.max, ALU.max), wait=False)
        go(dve.tensor_copy(enter[:, 0, 2:3], m0[:, 0:1]), wait=False)
        go(dve.tensor_copy(enter[:, 1, NC - 1:NC], m0[:, 1:2]))
        mu = rows[:, 0]
        for group in GROUPS:
            for i in range(group[1]):
                for d in range(2):
                    c = chunk_of(group, i, d)
                    end = c * CHUNK if d else (c + 1) * CHUNK - 1
                    go(dve.tensor_scalar(mu[:, d, c * CHUNK:(c + 1) * CHUNK], top[:, d, c * CHUNK:(c + 1) * CHUNK],
                                         enter[:, d, c:c + 1], None, ALU.max))
                    go(dve.tensor_tensor(leave[:, d, c:c + 1], b[:, d, end:end + 1], mu[:, d, end:end + 1], ALU.add))
                    if i + 1 < group[1]:
                        to = chunk_of(group, i + 1, d)
                        go(dve.tensor_copy(enter[:, d, to:to + 1], leave[:, d, c:c + 1]))
        cut_up = lambda t: t.rearrange("h (c s) -> h c s", s=CHUNK)
        for d in range(2):
            at = 0 if d else CHUNK - 1
            end = cut_up(mu[:, d])[:, :, at:at + 1]
            m = enter[:, d, :].unsqueeze(2)
            go(dve.tensor_tensor(cut_up(rows[:, 1, d]), m.broadcast_to([HEADS, NC, CHUNK]), cut_up(mu[:, d]),
                                 ALU.subtract), wait=False)
            go(dve.scalar_tensor_tensor(out=quant[:, 1, d], in0=b[:, d, :], scalar=-1.0, in1=mu[:, d],
                                        op0=ALU.mult, op1=ALU.subtract), wait=False)
            go(dve.tensor_tensor(cut_up(quant[:, 2, d]), cut_up(a[:, d]), end.broadcast_to([HEADS, NC, CHUNK]),
                                 ALU.subtract), wait=False)
            go(dve.tensor_tensor(decay[:, d, :].unsqueeze(2), m, end, ALU.subtract))
        go(dve.tensor_scalar(mu, mu, -1.0, None, ALU.mult))
        dve.memset(zero[:, :], 0.0).then_inc(exps_ready, 1)
        dve.sem_inc(m_ready, 1)
        dve.wait_ge(turned, 1)
        go(dve.tensor_copy(cols[:, :, :, :, :].rearrange("p q d c h -> p (q d c h)"),
                           k.banks[4][0:CHUNK, 0:3 * 2 * NC * HEADS]), wait=False)
        go(dve.tensor_copy(keep[:, :, :, :].rearrange("p d c h -> p (d c) h"),
                           k.banks[5][:, 0:2 * NC * HEADS].rearrange("p (h n) -> p n h", h=HEADS)), wait=False)
        for part in range(2):
            with dve.Fori(0, WT) as i:
                go.enter(i, 6)
                dve.wait_ge(tile_out, i + (part * WT + 1 + per))
                z = zT[:, bass.ds(i + part * WT, 1), :].rearrange("p a t -> p (a t)")
                last = short_conv(dve, go, conv[:, :], z, lambda tap: k.vcol[
                    :, bass.ds(i + (V_MLCONV + (part * 3 + tap) * WT), 1)])
                go(last)
                go(dve.tensor_scalar(z, conv[:, :], 0.0625 if part else 1.0, None, ALU.mult))
                go.leave(WT)

    return Side(sync_early=sync_early, sync_states=sync_states, sync_last=sync_last,
                tensor_early=tensor_early, tensor_late=tensor_late,
                scalar_early=scalar_early, scalar_late=scalar_late, vector=vector)


def mlstm_scan(k, ctx, zT, oTM, rows, cols, keep, state, norm):
    nc, io, sem = k.nc, k.io, k.sem
    two = range(2)
    now = [k.sb(ctx, f"ml_qkv_now{d}", [P, 3 * WT, CHUNK]) for d in two]
    row_now = [k.sb(ctx, f"ml_rows_now{d}", [HEADS, 2, CHUNK]) for d in two]
    q_decayed = [k.sb(ctx, f"ml_q_decayed{d}", [P, 2 * HEADS, CHUNK]) for d in two]
    k_rows = [k.sb(ctx, f"ml_k_rows{d}", [CHUNK, W]) for d in two]
    v_rows = [k.sb(ctx, f"ml_v_rows{d}", [CHUNK, W]) for d in two]
    weight = [k.sb(ctx, f"ml_weight{d}", [CHUNK, HEADS, CHUNK]) for d in two]
    den = [k.sb(ctx, f"ml_den{d}", [CHUNK, 2, HEADS]) for d in two]
    hid = k.sb(ctx, "ml_hidden", [CHUNK, W])
    now_ready, weight_done, v_out = sem("ml_now_ready"), sem("ml_weight_done"), sem("ml_v_out")
    qk_mm, spread_mm, k_turned, v_turned = sem("ml_qk_mm"), sem("ml_spread_mm"), sem("ml_k_turned"), sem("ml_v_turned")
    q_ready, att_ready, k_ready = sem("ml_q_ready"), sem("ml_att_ready"), sem("ml_k_ready")
    o_mm, o_read, state_mm = sem("ml_o_mm"), sem("ml_o_read"), sem("ml_state_mm")
    state_ready, state_stored = sem("ml_state_ready"), sem("ml_state_stored")
    runs = ((GROUPS[1], 0, 0), (GROUPS[0], 2 * GROUPS[1][1], 2 * GROUPS[1][1] + 2))

    with nc.Block() as block:
        @block.scalar
        def _(act):
            for group, q0, s0 in runs:
                with act.Fori(0, group[1]) as i:
                    for d in two:
                        act.wait_ge(state_ready, i * 2 + (s0 + d + 1))
                        at = bass.ds(chunk_of(group, i, d) * CHUNK, CHUNK)
                        act.copy(now[d][:, :, :], zT[:, 0:3 * WT, at]).then_inc(now_ready, 1)
                        act.copy(row_now[d][:, :, :], rows[:, :, d, at]).then_inc(now_ready, 1)
                    for d in two:
                        c = chunk_of(group, i, d)
                        act.wait_ge(qk_mm, i * 2 + (q0 + d + 1))
                        for h in range(HEADS):
                            e = k.banks[0][0:CHUNK, (HEADS + h) * CHUNK:(HEADS + h + 1) * CHUNK]
                            act.activation(weight[d][:, h, :], e, ACT.Exp, bias=cols[:, 0, d, bass.ds(c, 1), h]
                                           ).then_inc(weight_done, 1)
                        for half in two:
                            act.wait_ge(v_turned, i * 4 + (2 * (q0 + d) + half + 1))
                            act.copy(v_rows[d][:, half * 512:(half + 1) * 512], k.banks[7 - 3 * half][0:CHUNK, :]
                                     ).then_inc(v_out, 1)

        @block.tensor
        def _(pe):
            ident = k.cst[:, C_ID:C_ID + P]
            for group, q0, s0 in runs:
                with pe.Fori(0, group[1]) as i:
                    for d in two:
                        q = i * 2 + (q0 + d)
                        pe.wait_ge(now_ready, q * 2 + 2)
                        pe.wait_ge(att_ready, q + 1)
                        for h in range(HEADS):
                            for j in two:
                                pe.matmul(k.banks[0][0:CHUNK, h * CHUNK:(h + 1) * CHUNK], now[d][:, WT + 2 * h + j, :],
                                          now[d][:, 2 * h + j, :], start=(j == 0), stop=(j == 1))
                        e = k.banks[0][0:CHUNK, HEADS * CHUNK:2 * HEADS * CHUNK]
                        mask = k.cst[0:CHUNK, C_NEG + d * CHUNK:C_NEG + (d + 1) * CHUNK]
                        pe.matmul(e.rearrange("p (h t) -> p h t", h=HEADS), k.cst[0:CHUNK, C_ID:C_ID + CHUNK],
                                  mask.unsqueeze(1).broadcast_to([CHUNK, HEADS, CHUNK]), start=True, stop=False)
                        for h in range(HEADS):
                            sel = C_SEL + h * P
                            mm = pe.matmul(e[:, h * CHUNK:(h + 1) * CHUNK], k.cst[0:HEADS, sel:sel + CHUNK],
                                           row_now[d][:, 0, :], start=False, stop=(h == HEADS - 1))
                        mm.then_inc(qk_mm, 1)
                        pe.wait_ge(state_ready, i * 2 + (s0 + 2))
                        pe.wait_ge(q_ready, q + 1)
                        pe.wait_ge(k_ready, q + 1)
                        pe.wait_ge(v_out, q * 2 + 1)
                        for h in range(HEADS):
                            mm = pe.matmul(k.banks[1][:, h * CHUNK:(h + 1) * CHUNK],
                                           k.cst[0:HEADS, C_SEL + h * P:C_SEL + (h + 1) * P], row_now[d][:, 1, :],
                                           start=True, stop=True)
                        mm.then_inc(spread_mm, 1)
                        for t in range(WT):
                            mm = pe.transpose(k.banks[5 + t // 4][0:CHUNK, t % 4 * P:(t % 4 + 1) * P],
                                              now[d][:, WT + t, :], ident)
                        mm.then_inc(k_turned, 1)
                        for half in two:
                            for t in range(4):
                                mm = pe.transpose(k.banks[7 - 3 * half][0:CHUNK, t * P:(t + 1) * P],
                                                  now[d][:, 2 * WT + 4 * half + t, :], ident)
                            mm.then_inc(v_turned, 1)
                    for d in two:
                        q = i * 2 + (q0 + d)
                        pe.wait_ge(att_ready, q + 2)
                        pe.wait_ge(q_ready, q + 2)
                        pe.wait_ge(v_out, i * 4 + (2 * q0 + 4) + 1)
                        pe.wait_ge(o_read, q + 1)
                        for h in range(HEADS):
                            out = k.banks[2 + h // 2][0:CHUNK, h % 2 * DV:(h % 2 + 1) * DV]
                            for j in two:
                                pe.matmul(out, q_decayed[d][:, 2 * h + j, :], state[:, d, 2 * h + j, :],
                                          start=(j == 0), stop=False)
                            pe.matmul(out, weight[d][:, h, :], v_rows[d][:, h * DV:(h + 1) * DV], start=False, stop=True)
                        pe.wait_ge(state_ready, i * 2 + (s0 + d + 2))
                        for h in range(HEADS):
                            out = k.banks[4][0:CHUNK, h:h + 1]
                            for j in two:
                                pe.matmul(out, q_decayed[d][:, 2 * h + j, :], norm[:, d, 2 * h + j:2 * h + j + 1],
                                          start=(j == 0), stop=False)
                            mm = pe.matmul(out, weight[d][:, h, :], k.cst[0:CHUNK, C_ONE:C_ONE + 1], start=False, stop=True)
                        mm.then_inc(o_mm, 1)
                        pe.wait_ge(k_ready, i * 2 + (q0 + 2) + 1)
                        for h in range(HEADS):
                            if h == HEADS - 1:
                                pe.wait_ge(o_read, q + 2)
                            for j in two:
                                mm = pe.matmul(k.banks[(5, 6, 7, 4)[h]][:, j * DV:(j + 1) * DV],
                                               k_rows[d][:, (2 * h + j) * P:(2 * h + j + 1) * P],
                                               v_rows[d][:, h * DV:(h + 1) * DV], start=True, stop=True)
                            if h % 2:
                                mm.then_inc(state_mm, 1)
                        for n in range(2 * HEADS):
                            mm = pe.matmul(k.banks[1][:, 256 + n:257 + n], k_rows[d][:, n * P:(n + 1) * P],
                                           k.cst[0:CHUNK, C_ONE:C_ONE + 1], start=True, stop=True)
                        mm.then_inc(state_mm, 1)

        @block.vector
        def _(dve):
            go = Steps(dve, sem("ml_scan_step"))
            go(dve.memset(oTM[0:CHUNK, :, :], 0.0))
            dve.sem_inc(att_ready, 1)
            dve.sem_inc(q_ready, 1)
            dve.sem_inc(k_ready, 1)
            dve.sem_inc(v_out, 1)
            dve.sem_inc(o_read, 1)
            dve.sem_inc(state_ready, 2)
            for group, q0, s0 in runs:
                if q0:
                    dve.wait_ge(state_ready, q0 + 2)
                    go(dve.memset(norm[:, :, :], 0.0))
                    dve.memset(state[:, :, :, :], 0.0).then_inc(state_ready, 2)
                    dve.wait_ge(state_ready, q0 + 4)
                with dve.Fori(0, group[1]) as i:
                    go.enter(i, 2 * (1 + 4 + 2 + 8 + 1))
                    for d in two:
                        q = i * 2 + (q0 + d)
                        c = chunk_of(group, i, d)
                        dve.wait_ge(spread_mm, q + 1)
                        spread = k.banks[1][:, 0:HEADS * CHUNK].rearrange("p (h t) -> p h t", h=HEADS)
                        dve.tensor_tensor(q_decayed[d][:, :, :].rearrange("p (h j) t -> p h j t", j=2),
                                          spread.unsqueeze(2).broadcast_to([P, HEADS, 2, CHUNK]),
                                          now[d][:, 0:WT, :].rearrange("p (h j) t -> p h j t", j=2),
                                          ALU.mult).then_inc(q_ready, 1)
                        dve.wait_ge(k_turned, q + 1)
                        for half in two:
                            wk = cols[:, 2, d, bass.ds(c, 1), 2 * half:2 * half + 2].rearrange("p a h -> p (a h)")
                            last = dve.tensor_tensor(
                                k_rows[d][:, half * 512:(half + 1) * 512].rearrange("p (h v) -> p h v", h=2),
                                k.banks[5 + half][0:CHUNK, :].rearrange("p (h v) -> p h v", h=2),
                                wk.unsqueeze(2).broadcast_to([CHUNK, 2, DV]), ALU.mult)
                            if half == 0:
                                go(last, wait=False)
                        last.then_inc(k_ready, 1)
                        dve.wait_ge(weight_done, q * 4 + 4)
                        dve.tensor_tensor(weight[d][:, :, :], k.banks[0][0:CHUNK, 0:HEADS * CHUNK].rearrange(
                            "p (h t) -> p h t", h=HEADS), weight[d][:, :, :], ALU.mult).then_inc(att_ready, 1)
                    for d in two:
                        q = i * 2 + (q0 + d)
                        c = chunk_of(group, i, d)
                        dve.wait_ge(o_mm, q + 1)
                        low, up = den[d][:, 0, :], den[d][:, 1, :]
                        em = cols[:, 1, d, bass.ds(c, 1), :].rearrange("p a h -> p (a h)")
                        go(dve.tensor_copy(low, k.banks[4][0:CHUNK, 0:HEADS]))
                        go(dve.scalar_tensor_tensor(out=up, in0=low, scalar=-1.0, in1=low, op0=ALU.mult, op1=ALU.max))
                        go(dve.tensor_tensor(up, up, em, ALU.max))
                        go(dve.reciprocal(low, up))
                        for half in two:
                            last = dve.tensor_tensor(
                                hid[:, half * 512:(half + 1) * 512].rearrange("p (h v) -> p h v", h=2),
                                k.banks[2 + half][0:CHUNK, :].rearrange("p (h v) -> p h v", h=2),
                                low[:, 2 * half:2 * half + 2].unsqueeze(2).broadcast_to([CHUNK, 2, DV]), ALU.mult)
                            if half == 0:
                                go(last, wait=False)
                        last.then_inc(o_read, 1)
                        dve.wait_ge(o_read, q + 2)
                        o = oTM[0:CHUNK, bass.ds(c, 1), :]
                        go(dve.tensor_tensor(o, o, hid[:, :].unsqueeze(1), ALU.add))
                        for h in range(HEADS):
                            if h % 2 == 0:
                                dve.wait_ge(state_mm, q * 3 + (h // 2 + 1))
                            for j in two:
                                part = dve.scalar_tensor_tensor(
                                    out=state[:, d, 2 * h + j, :], in0=state[:, d, 2 * h + j, :],
                                    scalar=keep[:, d, bass.ds(c, 1), h], in1=k.banks[(5, 6, 7, 4)[h]][:, j * DV:(j + 1) * DV],
                                    op0=ALU.mult, op1=ALU.add)
                                go(part, wait=False)
                        n8 = norm[:, d, :].rearrange("p (h j) -> p h j", j=2)
                        kp = keep[:, d, bass.ds(c, 1), :].rearrange("p a h -> p (a h)")
                        go(dve.tensor_tensor(n8, n8, kp.unsqueeze(2).broadcast_to([P, HEADS, 2]), ALU.mult))
                        dve.wait_ge(state_mm, q * 3 + 3)
                        dve.tensor_tensor(norm[:, d, :], k.banks[1][:, 256:264], norm[:, d, :], ALU.add
                                          ).then_inc(state_ready, 1)
                    go.leave(group[1])

        @block.sync
        def _(sp):
            sp.wait_ge(state_ready, 2 * NC + 4)
            for d in two:
                sp.dma_start(io["new_state_mlstm_C"][0, 0, d].rearrange("h (j p) v -> p (h j) v", p=P),
                             state[:, d, :, :]).then_inc(state_stored, 16)
                sp.dma_start(io["new_state_mlstm_n"][0, 0, d].rearrange("h (j p) -> p (h j)", p=P), norm[:, d, :],
                             allow_slow_non_contiguous=True).then_inc(state_stored, 16)
            sp.wait_ge(state_stored, 64)


def stage_merge(k, ctx):
    nc, io, sem = k.nc, k.io, k.sem
    SLOTS = 2
    wg = [k.sb(ctx, f"merge_gate_w{s}", [P, 3, KD, P]) for s in range(SLOTS)]
    wb = [k.sb(ctx, f"merge_branch_w{s}", [P, 3, WT, P]) for s in range(SLOTS)]
    sig = k.sb(ctx, "merge_sigmoid", [P, 3, TOK])
    tmp = k.sb(ctx, "merge_product", [P, TOK])
    gate_in = [[sem(f"merge_gate_w_in{s}_{b}") for b in range(3)] for s in range(SLOTS)]
    branch_in = [[sem(f"merge_branch_w_in{s}_{b}") for b in range(3)] for s in range(SLOTS)]
    g_mm, b_mm, sig_done, prod_done = sem("merge_gate_mm"), sem("merge_branch_mm"), sem("merge_sig_done"), sem("merge_prod_done")
    gate_w = io["w_in"][0][:, COL_GATE:].rearrange("(k p) (b n) -> p b k n", p=P, b=3)
    branch_w = io["w_branch"][0].rearrange("b (k p) n -> p b k n", p=P)

    with nc.Block() as block:
        @block.sync
        def _(sp):
            def load(s, at):
                for b in range(3):
                    sp.dma_start(wg[s][:, b], gate_w[:, b, :, at]).then_inc(gate_in[s][b], 16)
                    sp.dma_start(wb[s][:, b], branch_w[:, b, :, at]).then_inc(branch_in[s][b], 16)
            for s in range(SLOTS):
                load(s, slice(s * P, (s + 1) * P))
            with sp.Fori(1, KD // SLOTS) as i:
                for s in range(SLOTS):
                    sp.wait_ge(b_mm, i * (3 * SLOTS) + 3 * (s + 1 - SLOTS))
                    load(s, bass.ds(i * (SLOTS * P) + s * P, P))

        @block.tensor
        def _(pe):
            with pe.Fori(0, KD // SLOTS) as i:
                for s in range(SLOTS):
                    for b in range(3):
                        pe.wait_ge(gate_in[s][b], i * 16 + 16)
                        done = i * (3 * SLOTS) + (3 * s + b + 1)
                        pe.wait_ge(sig_done, done)
                        for kk in range(KD):
                            mm = pe.matmul(k.banks[b][:, 0:TOK], wg[s][:, b, kk, :], k.hT[:, kk, :],
                                           start=(kk == 0), stop=(kk == KD - 1))
                        mm.then_inc(g_mm, 1)
                        pe.wait_ge(prod_done, done)
                        pe.wait_ge(branch_in[s][b], i * 16 + 16)
                        for kk in range(WT):
                            mm = pe.matmul(k.banks[3 + b][:, 0:TOK], wb[s][:, b, kk, :], k.yT[b][:, kk, :],
                                           start=(kk == 0), stop=(kk == WT - 1))
                        mm.then_inc(b_mm, 1)

        @block.scalar
        def _(act):
            act.sem_inc(sig_done, 3)
            with act.Fori(0, KD // SLOTS) as i:
                for s in range(SLOTS):
                    for b in range(3):
                        done = i * (3 * SLOTS) + (3 * s + b + 1)
                        act.wait_ge(g_mm, done)
                        act.wait_ge(prod_done, done)
                        act.activation(sig[:, b, :], k.banks[b][:, 0:TOK], ACT.Sigmoid,
                                       bias=k.vcol[:, bass.ds(i * SLOTS + (V_GATE + b * KD + s), 1)]
                                       ).then_inc(sig_done, 1)

        @block.vector
        def _(dve):
            go = Steps(dve, sem("merge_step"))
            dve.sem_inc(prod_done, 3)
            with dve.Fori(0, KD // SLOTS) as i:
                go.enter(i, 2 * SLOTS)
                for s in range(SLOTS):
                    out = k.mergedT[:, bass.ds(i * SLOTS + s, 1), :]
                    for b in range(3):
                        done = i * (3 * SLOTS) + (3 * s + b + 1)
                        dve.wait_ge(b_mm, done)
                        dve.wait_ge(sig_done, done + 3)
                        to = out if b == 0 else tmp[:, :].unsqueeze(1)
                        dve.tensor_tensor(to, k.banks[3 + b][:, 0:TOK].unsqueeze(1), sig[:, b:b + 1, :], ALU.mult
                                          ).then_inc(prod_done, 1)
                        dve.wait_ge(prod_done, done + 3)
                        if b:
                            go(dve.tensor_tensor(out, out, tmp[:, :].unsqueeze(1), ALU.add))
                go.leave(KD // SLOTS)


def stage_out(k, ctx):
    nc, io, sem = k.nc, k.io, k.sem
    COLS = 512
    N = D // COLS
    ring = [k.sb(ctx, f"out_w{s}", [P, KD, COLS]) for s in range(2)]
    x = k.sb(ctx, "out_x", [P, TT, D])
    gt = k.sb(ctx, "out_gt", [P, 2, D])
    tmp = k.sb(ctx, "out_product", [P, COLS])
    CUT = KD // 4
    slot_in = [[sem(f"out_w_in{s}_{c}") for c in range(KD // CUT)] for s in range(2)]
    x_in, mm_done, added, stored = sem("out_x_in"), sem("out_mm"), sem("out_added"), sem("x1_stored")
    w = io["w_out"][0].rearrange("(k p) n -> p k n", p=P)
    with nc.Block() as block:
        @block.sync
        def _(sp):
            for n in range(N):
                if n >= 2:
                    sp.wait_ge(mm_done, TT * (n - 1))
                for c in range(KD // CUT):
                    at = slice(c * CUT, (c + 1) * CUT)
                    sp.dma_start(ring[n % 2][:, at, :], w[:, at, n * COLS:(n + 1) * COLS]
                                 ).then_inc(slot_in[n % 2][c], 16)
                if n == 0:
                    sp.dma_start(x[:, 0, :], io["x_prompt"][0]).then_inc(x_in, 16)
                    sp.dma_start(x[:, 1:3, :], io["x_sample"][0].rearrange("(t p) d -> p t d", p=P)).then_inc(x_in, 16)
                    for g in range(2):
                        sp.dma_start(gt[:, g, :], k.gt_dram[0, g:g + 1].broadcast_to([P, D])).then_inc(x_in, 16)
            sp.wait_ge(added, TT * N)
            sp.dma_start(k.x1_dram.rearrange("t p d -> p t d"), x[:, :, :]).then_inc(stored, 16)
            sp.wait_ge(stored, 16)

        @block.tensor
        def _(pe):
            for n in range(N):
                for t in range(TT):
                    u = TT * n + t
                    if u >= 8:
                        pe.wait_ge(added, u - 7)
                    for kk in range(KD):
                        if t == 0 and kk % CUT == 0:
                            pe.wait_ge(slot_in[n % 2][kk // CUT], 16 * (n // 2 + 1))
                        mm = pe.matmul(k.banks[u % 8][:, :], k.mergedT[:, kk, t * P:(t + 1) * P], ring[n % 2][:, kk, :],
                                       start=(kk == 0), stop=(kk == KD - 1))
                    mm.then_inc(mm_done, 1)

        @block.vector
        def _(dve):
            go = Steps(dve, sem("out_step"))
            dve.wait_ge(x_in, 64)
            for n in range(N):
                for t in range(TT):
                    u = TT * n + t
                    dve.wait_ge(mm_done, u + 1)
                    cols = slice(n * COLS, (n + 1) * COLS)
                    go(dve.tensor_tensor(tmp[:, :], k.banks[u % 8][:, :], gt[:, min(t, 1), cols], ALU.mult))
                    dve.tensor_tensor(x[:, t, cols], x[:, t, cols], tmp[:, :], ALU.add).then_inc(added, 1)
                    dve.wait_ge(added, u + 1)


def stage_queries(k, ctx):
    nc, io, sem = k.nc, k.io, k.sem
    SLOTS, COLS = 2, 256
    TURNS = D // COLS // SLOTS
    PER = SLOTS * COLS // P
    ring = [k.sb(ctx, f"wq{s}", [P, KD, COLS]) for s in range(SLOTS)]
    keys = k.sb(ctx, "keys", [NKEYS, 2 * PEER_H, P])
    keysT = k.sb(ctx, "keysT", [P, 2 * PEER_H, NKEYS])
    qT = [k.sb(ctx, f"queryT{s}", [P, TOK]) for s in range(2)]
    slot_in = [sem(f"wq_in{s}") for s in range(SLOTS)]
    norm = Norm(k, ctx, 2)
    keys_in, keys_turned, keys_out = sem("keys_in"), sem("keys_turned"), sem("keys_out")
    q_mm, q_out, s_mm, s_out = sem("query_mm"), sem("query_out"), sem("score_mm"), sem("score_out")
    h_turned, h_out = sem("h2_turned"), sem("h2_out")
    w = io["peer_wq"][0].rearrange("(k p) n -> p k n", p=P)
    with nc.Block() as block:
        @block.sync
        def _(sp):
            norm.load(sp)
            for t in range(2 * PEER_H):
                sp.dma_start(keys[:, t, :], io["peer_keys"][0, t // 2, t % 2]).then_inc(keys_in, 16)
            for s in range(SLOTS):
                sp.dma_start(ring[s][:, :, :], w[:, :, s * COLS:(s + 1) * COLS]).then_inc(slot_in[s], 16)
            with sp.Fori(1, TURNS) as i:
                for s in range(SLOTS):
                    sp.wait_ge(q_mm, i * PER + (2 * (s + 1) - PER))
                    sp.dma_start(ring[s][:, :, :], w[:, :, bass.ds(i * (SLOTS * COLS) + s * COLS, COLS)]
                                 ).then_inc(slot_in[s], 16)

        @block.tensor
        def _(pe):
            ident = k.cst[:, C_ID:C_ID + P]
            pe.wait_ge(keys_in, 16 * 2 * PEER_H)
            for n in range(4):
                for t in range(4):
                    mm = pe.transpose(k.banks[4 + n][:, t * P:(t + 1) * P], keys[:, 4 * n + t, :], ident)
                mm.then_inc(keys_turned, 1)
            pe.wait_ge(keys_out, 4)
            norm.tensor(pe)
            pe.wait_ge(norm.written, 2 * KD)
            for r in range(TT):
                for g in range(4):
                    n = r * 4 + g
                    if n >= 4:
                        pe.wait_ge(h_out, n - 3)
                    for t in range(4):
                        mm = pe.transpose(k.banks[4 + n % 4][:, t * P:(t + 1) * P],
                                          k.hT[:, 4 * g + t, r * P:(r + 1) * P], ident)
                    mm.then_inc(h_turned, 1)
            pe.wait_ge(h_out, 12)

            def scores(i, j):
                pe.wait_ge(q_out, i * PER + (j + 1))
                pe.wait_ge(s_out, i * PER + (j + 1))
                for r in range(TT):
                    mm = pe.matmul(k.banks[2 + j % 2][:, r * P:(r + 1) * P], qT[j % 2][:, r * P:(r + 1) * P],
                                   keysT[:, bass.ds(i * PER + j, 1), :].rearrange("p a n -> p (a n)"),
                                   start=True, stop=True)
                mm.then_inc(s_mm, 1)
            with pe.Fori(0, TURNS) as i:
                for j in range(PER):
                    s, half = j // 2, j % 2
                    if half == 0:
                        pe.wait_ge(slot_in[s], i * 16 + 16)
                    for kk in range(KD):
                        mm = pe.matmul(k.banks[j % 2][:, 0:TOK], ring[s][:, kk, half * P:(half + 1) * P],
                                       k.hT[:, kk, :], start=(kk == 0), stop=(kk == KD - 1))
                    mm.then_inc(q_mm, 1)
                    if j:
                        scores(i, j - 1)
                scores(i, PER - 1)

        @block.scalar
        def _(act):
            for n in range(4):
                act.wait_ge(keys_turned, n + 1)
                act.copy(keysT[:, 4 * n:4 * n + 4, :], k.banks[4 + n][:, :].rearrange("p (t n) -> p t n", t=4)
                         ).then_inc(keys_out, 1)
            norm.scalar(act)
            for n in range(12):
                act.wait_ge(h_turned, n + 1)
                rows = k.h2_prompt if n < 4 else k.h2_sample[:, n // 4 - 1]
                act.copy(rows[:, n % 4 * 512:(n % 4 + 1) * 512], k.banks[4 + n % 4][:, :]).then_inc(h_out, 1)
            with act.Fori(0, TURNS) as i:
                for j in range(PER):
                    act.wait_ge(q_mm, i * PER + (j + 1))
                    act.wait_ge(s_mm, i * PER + j)
                    act.copy(qT[j % 2][:, :], k.banks[j % 2][:, 0:TOK]).then_inc(q_out, 1)

        @block.vector
        def _(dve):
            sample = k.scores_sample[:, :, :].rearrange("p (r t) n -> p r t n", r=TT - 1)
            norm.vector_sums(dve)
            norm.vector_columns(dve, k.h2cols)
            dve.sem_inc(s_mm, 1)
            dve.sem_inc(s_out, 2)
            with dve.Fori(0, TURNS) as i:
                for j in range(PER):
                    dve.wait_ge(s_mm, i * PER + (j + 2))
                    bank = k.banks[2 + j % 2]
                    dve.tensor_copy(k.scores_prompt[:, bass.ds(i * PER + j, 1), :], bank[:, 0:P].unsqueeze(1))
                    dve.tensor_copy(sample[:, :, bass.ds(i * PER + j, 1), :],
                                    bank[:, P:TOK].rearrange("p (r a n) -> p r a n", r=TT - 1, a=1)
                                    ).then_inc(s_out, 1)


def top16(dve, go, waited, values, index, src, rest):
    dve.sem_inc(waited, 1)
    go(dve.max(values[:, 0:8], src))
    dve.sem_inc(waited, 1)
    go(dve.max_index(index[:, 0:8], values[:, 0:8], src), wait=False)
    go(dve.match_replace(rest, values[:, 0:8], src, NEG))
    dve.sem_inc(waited, 1)
    go(dve.max(values[:, 8:16], rest))
    dve.sem_inc(waited, 1)
    go(dve.max_index(index[:, 8:16], values[:, 8:16], rest))


class TopK:
    STEPS = 1 + 3 * 5 + 1 + 4 + 6 + 2

    def __init__(self, k, ctx):
        sb = lambda name, shape, dt=F32: k.sb(ctx, name, shape, dt)
        self.k = k
        self.now = sb("scores_now", [P, 2, NKEYS])
        self.rest = sb("scores_rest", [P, 256])
        self.val = sb("key_values", [P, 2, TOPK])
        self.ind = sb("key_index", [P, 2, TOPK], U32)
        self.indf = sb("key_index_f", [P, 2, TOPK])
        self.cand = sb("candidates", [P, TOPK, TOPK])
        self.best = sb("best", [P, TOPK])
        self.bi = sb("best_index", [P, TOPK], U32)
        self.part = sb("best_parts", [P, 2, TOPK], U32)
        self.partf = sb("best_parts_f", [P, 2, TOPK])
        self.eq = sb("one_hot", [P, TOPK, TOPK])
        self.sel = sb("selected", [P, 2, TOPK])
        self.neg = sb("neg_best", [P, 1])
        self.ex = sb("best_exp", [P, TOPK])
        self.tot = sb("best_sum", [P, 1])

    def begin(self, phase):
        sem = self.k.sem
        self.best_ready, self.exp_done = sem(f"best_ready_{phase}"), sem(f"best_exp_done_{phase}")
        self.index_ready, self.waited = sem(f"index_ready_{phase}"), sem(f"topk_waited_{phase}")

    def vector(self, dve, go, scores, head, turn, pairs=None):
        k, val, sel = self.k, self.val, self.sel
        go(dve.tensor_copy(self.now[:, :, :], scores))
        for s in range(2):
            top16(dve, go, self.waited, val[:, s, :], self.ind[:, s, :], self.now[:, s, :],
                  self.rest[:, s * P:(s + 1) * P])
        go(dve.tensor_tensor(self.cand[:, :, :], val[:, 0, :].unsqueeze(2).broadcast_to([P, TOPK, TOPK]),
                             val[:, 1, :].unsqueeze(1).broadcast_to([P, TOPK, TOPK]), ALU.add))
        top16(dve, go, self.waited, self.best, self.bi, self.cand[:, :, :].rearrange("p a b -> p (a b)"),
              self.rest[:, :])
        dve.tensor_scalar(self.neg[:, :], self.best[:, 0:1], -1.0, None, ALU.mult).then_inc(self.best_ready, 1)
        go(dve.tensor_copy(self.indf[:, :, :], self.ind[:, :, :]), wait=False)
        go(dve.tensor_scalar(self.part[:, 0, :], self.bi[:, :], 4, None, ALU.logical_shift_right), wait=False)
        go(dve.tensor_scalar(self.part[:, 1, :], self.bi[:, :], 15, None, ALU.bitwise_and))
        go(dve.tensor_copy(self.partf[:, :, :], self.part[:, :, :]))
        iota = k.cst[:, C_IOTA:C_IOTA + TOPK].unsqueeze(1).broadcast_to([P, TOPK, TOPK])
        for s in range(2):
            go(dve.tensor_tensor(self.eq[:, :, :], self.partf[:, s, :].unsqueeze(2).broadcast_to([P, TOPK, TOPK]),
                                 iota, ALU.is_equal))
            go(dve.tensor_tensor(self.eq[:, :, :], self.eq[:, :, :],
                                 self.indf[:, s, :].unsqueeze(1).broadcast_to([P, TOPK, TOPK]), ALU.mult))
            go(dve.tensor_reduce(sel[:, s, :], self.eq[:, :, :], AX_X, ALU.add))
        dve.scalar_tensor_tensor(out=k.index[:, bass.ds(head, 1), :], in0=sel[:, 0:1, :], scalar=float(NKEYS),
                                 in1=sel[:, 1:2, :], op0=ALU.mult, op1=ALU.add).then_inc(self.index_ready, 1)
        if pairs is not None:
            go(dve.tensor_copy(pairs, sel[:, :, :].unsqueeze(2)))
        dve.wait_ge(self.exp_done, turn + 1)
        go(dve.reciprocal(self.tot[:, :], self.tot[:, :]))
        go(dve.tensor_scalar(k.gate[:, bass.ds(head, 1), :], self.ex[:, :].unsqueeze(1), self.tot[:, 0:1], None,
                             ALU.mult))

    def scalar(self, act, turn):
        act.wait_ge(self.best_ready, turn + 1)
        act.activation(self.ex[:, :], self.best[:, :], ACT.Exp, bias=self.neg[:, 0:1], accum_out=self.tot[:, 0:1]
                       ).then_inc(self.exp_done, 1)


def stage_sample_dots(k, ctx, topk):
    nc, io, sem = k.nc, k.io, k.sem
    R, N = 8, (TT - 1) * PEER_H
    u = [k.sb(ctx, f"u_rows{s}", [P, D]) for s in range(R)]
    idx = [k.sb(ctx, f"index_now{s}", [P, TOPK], U32) for s in range(2)]
    dots = k.sb(ctx, "dots", [P, TOPK])
    u_in = [sem(f"u_in{s}") for s in range(R)]
    idx_copied, dot_done, gelu_done, slot_free = (
        sem("index_now_copied"), sem("dot_done"), sem("gelu_done"), sem("gather_slot_free"))
    weights_ready = sem("sample_weights_ready")
    u_tab = io["peer_u"][0]
    topk.begin("sample")

    with nc.Block() as block:
        @block.gpsimd
        def _(pool):
            with pool.Fori(0, N // 2) as i:
                for odd in range(2):
                    pool.wait_ge(topk.index_ready, i * 2 + (odd + 1))
                    pool.tensor_copy(idx[odd][:, :].unsqueeze(1), k.index[:, bass.ds(i * 2 + odd, 1), :]
                                     ).then_inc(idx_copied, 1)
                    pool.wait_ge(idx_copied, i * 2 + (odd + 1))
                    for n in range(TOPK):
                        pool.wait_ge(dot_done, i * (2 * TOPK) + (odd * TOPK + n + 1))
                        pool.sem_inc(slot_free, 1)
                        pool.indirect_dma_start(
                            out=u[n % R][:, :], out_offset=None, in_=u_tab,
                            in_offset=bass.IndirectOffsetOnAxis(ap=idx[odd][:, n:n + 1], axis=0)
                            ).then_inc(u_in[n % R], 16)

        @block.vector
        def _(dve):
            go = Steps(dve, sem("topk_step_sample"))
            dve.sem_inc(dot_done, R)
            dve.sem_inc(gelu_done, 1)

            def find(head):
                topk.vector(dve, go, k.scores_sample[:, bass.ds(head * 2, 2), :], head, head,
                            k.pairs[:, :, bass.ds(head, 1), :])

            def products(head, tile):
                dve.wait_ge(gelu_done, head + 1)
                for n in range(TOPK):
                    dve.wait_ge(u_in[n % R], head * 32 + 16 * (n // R + 1))
                    dve.scalar_tensor_tensor(out=u[n % R][:, :], in0=u[n % R][:, :], scalar=1.0,
                                             in1=k.h2_sample[:, tile, :], op0=ALU.mult, op1=ALU.mult,
                                             accum_out=dots[:, n:n + 1]).then_inc(dot_done, 1)

            find(0)
            for tile in range(TT - 1):
                n = PEER_H - (tile == TT - 2)
                with dve.Fori(0, n) as i:
                    go.enter(i, TopK.STEPS + 1)
                    find(i + (tile * PEER_H + 1))
                    products(i + tile * PEER_H, tile)
                    go.leave(n)
            topk.vector(dve, go, k.scores_prompt[:, 0:2, :], N, N)
            products(N - 1, TT - 2)
            dve.wait_ge(gelu_done, N + 1)
            dve.tensor_tensor(k.weight[:, :, :], k.weight[:, :, :], k.gate[:, 0:N, :], ALU.mult
                              ).then_inc(weights_ready, 1)

        @block.scalar
        def _(act):
            topk.scalar(act, 0)
            with act.Fori(0, N) as i:
                topk.scalar(act, i + 1)
                act.wait_ge(dot_done, i * TOPK + (TOPK + R))
                act.activation(k.weight[:, bass.ds(i, 1), :], dots[:, :].unsqueeze(1), ACT.Gelu_apprx_tanh
                               ).then_inc(gelu_done, 1)


def stage_experts(k, ctx, topk):
    nc, io, sem = k.nc, k.io, k.sem
    u, v = k.u_slots, k.v_slots
    RU, RV, RS = len(u), len(v), 8
    S_HEADS = (TT - 1) * PEER_H
    HALF, HCOLS = NKEYS // 2, D // 2
    G8, GROUPS8 = 8, SAMPLE // 8
    assert GROUPS8 == 2 * TOPK
    SPLIT = 4
    table = [k.sb(ctx, f"v_table{s}", [P, HCOLS]) for s in range(RS)]
    G = k.sb(ctx, "spread_weights", [P, HALF, SAMPLE])
    hot2 = [k.sb(ctx, f"one_hot_i2_{s}", [P, G8, NKEYS]) for s in range(2)]
    hot1 = [k.sb(ctx, f"one_hot_i1_{s}", [P, G8, HALF]) for s in range(2)]
    pairsT = k.sb(ctx, "pairsT", [P, 3, SAMPLE])
    out = k.sb(ctx, "sums_out", [P, 2, 512])
    idx = [k.sb(ctx, f"index_slot{s}", [P, TOPK], U32) for s in range(2)]
    dots = k.sb(ctx, "prompt_dots", [P, TOPK])
    wgt = k.sb(ctx, "prompt_weights", [P, TOPK])
    u_in, v_in = [sem(f"u_slot_in{s}") for s in range(RU)], [sem(f"v_slot_in{s}") for s in range(RV)]
    table_in = [sem(f"v_table_in{s}") for s in range(RS)]
    idx_copied, dot_done, gelu_done, w_ready, acc_done, slot_free = (
        sem("p_" + n) for n in ("index_copied", "dot_done", "gelu_done", "weights_ready", "acc_done", "slot_free"))
    zeroed, pairs_turned, pairs_out = sem("acc_zeroed"), sem("pairs_turned"), sem("pairs_out")
    hot1_ready, hot2_abs, hot2_ready = sem("one_hots_i1_ready"), sem("one_hots_i2_abs"), sem("one_hots_i2_ready")
    build_mm, g_out = sem("spread_mm"), sem("spread_out")
    table_mm, sums_read = sem("v_table_mm"), sem("sums_read")
    sums_stored = [sem(f"sums_stored{s}") for s in range(2)]
    u_tab, v_tab = io["peer_u"][0], io["peer_v"][0]
    v_cut = v_tab.rearrange("(a b) d -> b a d", b=NKEYS)
    topk.begin("prompt")

    with nc.Block() as block:
        @block.sync
        def _(sp):
            for quarter in range(4):
                half, cols = quarter // 2, quarter % 2 * HCOLS
                with sp.Fori(0, HALF // RS) as i:
                    for s in range(RS):
                        sp.wait_ge(table_mm, i * RS + (quarter * HALF + s + 1))
                        sp.dma_start(table[s][:, :].unsqueeze(1),
                                     v_cut[:, bass.ds(i * RS + (half * HALF + s), 1), cols:cols + HCOLS]
                                     ).then_inc(table_in[s], 16)
            sp.wait_ge(dot_done, RU + PEER_H * TOPK)
            for t in range(TT):
                sp.dma_start(u[t][:, :], k.x1_dram[t]).then_inc(k.final_in, 16)
            sp.dma_start(u[TT][:, :], io["final_g"].unsqueeze(0).broadcast_to([P, D])).then_inc(k.final_in, 16)
            sp.wait_ge(acc_done, RV + PEER_H * TOPK)
            for g in range(2):
                sp.dma_start(v[g][:, :], k.gt_dram[1, g:g + 1].broadcast_to([P, D])).then_inc(k.final_in, 16)

        @block.gpsimd
        def _(pool):
            with pool.Fori(0, PEER_H // 2) as i:
                for odd in range(2):
                    pool.wait_ge(topk.index_ready, i * 2 + (odd + 1))
                    pool.tensor_copy(idx[odd][:, :].unsqueeze(1), k.index[:, bass.ds(i * 2 + (S_HEADS + odd), 1), :]
                                     ).then_inc(idx_copied, 1)
                    pool.wait_ge(idx_copied, i * 2 + (odd + 1))
                    for tab, ring, arrived, used in ((u_tab, u, u_in, dot_done), (v_tab, v, v_in, acc_done)):
                        for n in range(TOPK):
                            pool.wait_ge(used, i * (2 * TOPK) + (odd * TOPK + n + 1))
                            pool.sem_inc(slot_free, 1)
                            pool.indirect_dma_start(
                                out=ring[n % len(ring)][:, :], out_offset=None, in_=tab,
                                in_offset=bass.IndirectOffsetOnAxis(ap=idx[odd][:, n:n + 1], axis=0)
                                ).then_inc(arrived[n % len(ring)], 16)

        @block.tensor
        def _(pe):
            for a, src in enumerate((k.pairs[:, 0], k.pairs[:, 1], k.weight)):
                for t in range(TT - 1):
                    n = 2 * a + t
                    last = pe.transpose(k.banks[4 + n // 4][:, n % 4 * P:(n % 4 + 1) * P],
                                        src[:, t * PEER_H:(t + 1) * PEER_H, :].rearrange("p h s -> p (h s)"),
                                        k.cst[:, C_ID:C_ID + P])
            last.then_inc(pairs_turned, 1)
            for half in range(2):
                if half:
                    pe.wait_ge(sums_read, 8)
                with pe.Fori(0, GROUPS8 // 2) as i:
                    for s in range(2):
                        pe.wait_ge(hot1_ready, i * 2 + (half * GROUPS8 + s + 1))
                        pe.wait_ge(hot2_ready, i * 2 + (half * GROUPS8 + s + 1))
                        pe.wait_ge(g_out, i * 2 + (half * GROUPS8 + s + 1))
                        for j in range(G8):
                            last = pe.matmul(k.banks[6 + s][:, j * HALF:(j + 1) * HALF], hot2[s][:, j, :],
                                             hot1[s][:, j, :], start=True, stop=True)
                        last.then_inc(build_mm, 1)
                pe.wait_ge(g_out, 2 + (half + 1) * GROUPS8)

                def multiply(quarter, i, last_turn):
                    for s in range(RS):
                        pe.wait_ge(table_in[s], i * 16 + 16 * (quarter * (HALF // RS) + 1))
                        weights = G[:, bass.ds(i * RS + s, 1), :].rearrange("p a t -> p (a t)")
                        for dt in range(HCOLS // P):
                            last = pe.matmul(
                                k.banks[4 * (quarter % 2) + dt // 2][:, dt % 2 * SAMPLE:(dt % 2 + 1) * SAMPLE],
                                table[s][:, dt * P:(dt + 1) * P], weights,
                                start=False, stop=(last_turn and s == RS - 1 and dt % 2 == 1))
                        last.then_inc(table_mm, 1)
                for quarter in (2 * half, 2 * half + 1):
                    for b in range(4):
                        pe.matmul(k.banks[4 * (quarter % 2) + b][:, :], k.cst[:, C_ID:C_ID + P],
                                  k.cst[:, C_ZERO:C_ZERO + 1].broadcast_to([P, 2 * SAMPLE]), start=True, stop=False)
                    with pe.Fori(0, HALF // RS - 1) as i:
                        multiply(quarter, i, False)
                    multiply(quarter, HALF // RS - 1, True)

        @block.vector
        def _(dve):
            go = Steps(dve, sem("topk_step_prompt"))
            for s, n in ((dot_done, RU), (acc_done, RV), (table_mm, RS), (build_mm, 2), (g_out, 2),
                         (topk.index_ready, 1)):
                dve.sem_inc(s, n)
            dve.memset(k.acc[:, :], 0.0).then_inc(zeroed, 1)
            dve.wait_ge(pairs_turned, 1)
            dve.tensor_copy(pairsT[:, 0:2, :], k.banks[4][:, :].rearrange("p (a t) -> p a t", a=2)
                            ).then_inc(pairs_out, 1)
            dve.tensor_copy(pairsT[:, 2, :], k.banks[5][:, 0:SAMPLE]).then_inc(pairs_out, 1)
            dve.wait_ge(pairs_out, 2)
            dve.wait_ge(zeroed, 1)

            def one_hots(g):
                half, s = g // GROUPS8, g % 2
                dve.wait_ge(build_mm, g + 1)
                at = slice(g % GROUPS8 * G8, (g % GROUPS8 + 1) * G8)
                spread = lambda a, n: pairsT[:, a, at].unsqueeze(2).broadcast_to([P, G8, n])
                iota = k.cst[:, C_IOTA + half * HALF:C_IOTA + (half + 1) * HALF].unsqueeze(1)
                go(dve.tensor_tensor(hot1[s][:, :, :], iota.broadcast_to([P, G8, HALF]), spread(0, HALF), ALU.is_equal))
                dve.tensor_tensor(hot1[s][:, :, :], hot1[s][:, :, :], spread(2, HALF), ALU.mult
                                  ).then_inc(hot1_ready, 1)

            def head(h, more, half=None):
                if more:
                    topk.vector(dve, go, k.scores_prompt[:, bass.ds(h * 2 + 2, 2), :], h + (S_HEADS + 1), h)
                for n in range(TOPK):
                    dve.wait_ge(u_in[n % RU], h * (16 * TOPK // RU) + 16 * (n // RU + 1))
                    dve.scalar_tensor_tensor(out=u[n % RU][:, :], in0=u[n % RU][:, :], scalar=1.0,
                                             in1=k.h2_prompt[:, :], op0=ALU.mult, op1=ALU.mult,
                                             accum_out=dots[:, n:n + 1]).then_inc(dot_done, 1)
                    if half is not None:
                        one_hots(half * GROUPS8 + n)
                dve.wait_ge(gelu_done, h + 1)
                dve.tensor_tensor(wgt[:, :].unsqueeze(1), wgt[:, :].unsqueeze(1),
                                  k.gate[:, bass.ds(h + S_HEADS, 1), :], ALU.mult).then_inc(w_ready, 1)
                dve.wait_ge(w_ready, h + 1)
                for n in range(TOPK):
                    dve.wait_ge(v_in[n % RV], h * (16 * TOPK // RV) + 16 * (n // RV + 1))
                    dve.wait_ge(acc_done, h * TOPK + (n + RV))
                    dve.scalar_tensor_tensor(out=k.acc[:, :], in0=v[n % RV][:, :], scalar=wgt[:, n:n + 1],
                                             in1=k.acc[:, :], op0=ALU.mult, op1=ALU.add).then_inc(acc_done, 1)
                    if half is not None:
                        one_hots(half * GROUPS8 + TOPK + n)

            def heads(first, end):
                with dve.Fori(0, end - first) as i:
                    go.enter(i, TopK.STEPS)
                    head(i + first, True)
                    go.leave(end - first)

            head(0, True, half=0)
            heads(1, SPLIT)
            head(SPLIT, True, half=1)
            heads(SPLIT + 1, PEER_H - 1)
            head(PEER_H - 1, False)

        @block.scalar
        def _(act):
            def one_hots_i2(g):
                s, t0 = g % 2, g % GROUPS8 * G8
                act.wait_ge(build_mm, g + 1)
                for j in range(G8):
                    act.activation(hot2[s][:, j, :], k.cst[:, C_IOTA:C_IOTA + NKEYS], ACT.Abs, scale=-1.0,
                                   bias=pairsT[:, 1, t0 + j:t0 + j + 1]).then_inc(hot2_abs, 1)
                act.wait_ge(hot2_abs, G8 * (g + 1))
                act.activation(hot2[s][:, :, :], hot2[s][:, :, :], ACT.Relu, scale=-1.0, bias=1.0
                               ).then_inc(hot2_ready, 1)

            def spread_out(groups):
                for g in groups:
                    act.wait_ge(build_mm, g + 3)
                    at = g % GROUPS8 * G8
                    act.copy(G[:, :, at:at + G8], k.banks[6 + g % 2][:, :].rearrange("p (t a) -> p a t", a=HALF)
                             ).then_inc(g_out, 1)
                    if g % GROUPS8 + 2 < GROUPS8:
                        one_hots_i2(g + 2)

            def head(h, more, half=None):
                if more:
                    topk.scalar(act, h)
                if half is not None:
                    act.wait_ge(pairs_out, 2)
                    one_hots_i2(half * GROUPS8)
                    one_hots_i2(half * GROUPS8 + 1)
                    spread_out(range(half * GROUPS8, half * GROUPS8 + TOPK - 1))
                act.wait_ge(dot_done, h * TOPK + (TOPK + RU))
                act.wait_ge(acc_done, h * TOPK + RV)
                act.activation(wgt[:, :], dots[:, :], ACT.Gelu_apprx_tanh).then_inc(gelu_done, 1)
                if half is not None:
                    spread_out(range(half * GROUPS8 + TOPK - 1, (half + 1) * GROUPS8))

            def heads(first, end):
                with act.Fori(0, end - first) as i:
                    head(i + first, True)

            def sums_out(half):
                for b in range(8):
                    n = 8 * half + b
                    act.wait_ge(table_mm, RS + (2 * half + b // 4 + 1) * HALF)
                    if n >= 2:
                        act.wait_ge(sums_stored[n % 2], 16 * (n // 2))
                    act.copy(out[:, n % 2, :], k.banks[b][:, :]).then_inc(sums_read, 1)
                    act.wait_ge(sums_read, n + 1)
                    act.dma_start(k.sums_dram[half, b], out[:, n % 2, :]).then_inc(sums_stored[n % 2], 16)

            head(0, True, half=0)
            heads(1, SPLIT)
            sums_out(0)
            head(SPLIT, True, half=1)
            heads(SPLIT + 1, PEER_H - 1)
            head(PEER_H - 1, False)
            sums_out(1)
            act.wait_ge(sums_stored[0], 16 * 8)
            act.wait_ge(sums_stored[1], 16 * 8)


def stage_final(k, ctx):
    nc, io, sem = k.nc, k.io, k.sem
    x, gain, gt = k.u_slots[0:TT], k.u_slots[TT], k.v_slots
    junk = k.sb(ctx, "final_squares", [P, D])
    ss = k.sb(ctx, "final_sums", [P, TT])
    parts = k.sb(ctx, "sample_sums", [P, 2, 8, 512])
    tmp = [k.sb(ctx, f"final_product{s}", [P, 512]) for s in range(2)]
    parts_in = [sem(f"final_parts_in{c}") for c in range(2)]
    joined, turned, added, squared, rms, root, done, stored = (
        sem("final_" + n) for n in ("joined", "turned", "added", "squared", "rms", "root",
                                    "done", "stored"))
    with nc.Block() as block:
        @block.sync
        def _(sp):
            sp.wait_ge(done, 1)
            sp.dma_start(io["y_prompt"][0], x[0][:, :]).then_inc(stored, 16)
            for t in range(1, TT):
                sp.wait_ge(done, t + 1)
                sp.dma_start(io["y_sample"][0, (t - 1) * P:t * P, :], x[t][:, :]).then_inc(stored, 16)
            sp.wait_ge(stored, 16 * TT)

        @block.vector
        def _(dve):
            go = Steps(dve, sem("final_step"))
            dve.wait_ge(k.final_in, 16 * (TT + 3))
            go(dve.tensor_tensor(k.acc[:, :], k.acc[:, :], gt[0][:, :], ALU.mult))
            dve.tensor_tensor(x[0][:, :], x[0][:, :], k.acc[:, :], ALU.add).then_inc(added, 4)
            for c in range(2):
                dve.wait_ge(parts_in[c], 32)
                dve.tensor_tensor(parts[:, 0, 4 * c:4 * c + 4], parts[:, 0, 4 * c:4 * c + 4],
                                  parts[:, 1, 4 * c:4 * c + 4], ALU.add).then_inc(joined, 1)
            for n in range(4 * (TT - 1)):
                t, c = 1 + n // 4, slice(n % 4 * 512, (n % 4 + 1) * 512)
                dve.wait_ge(turned, n + 1)
                if n >= 2:
                    dve.wait_ge(added, n + 3)
                go(dve.tensor_tensor(tmp[n % 2][:, :], k.banks[n % 4][:, :], gt[1][:, c], ALU.mult))
                dve.tensor_tensor(x[t][:, c], x[t][:, c], tmp[n % 2][:, :], ALU.add).then_inc(added, 1)
            dve.wait_ge(squared, TT)
            dve.tensor_scalar(ss[:, :], ss[:, :], 1.0 / D, EPS, ALU.mult, ALU.add).then_inc(rms, 1)
            dve.wait_ge(root, 1)
            go(dve.reciprocal(ss[:, :], ss[:, :]))
            for t in range(TT):
                dve.scalar_tensor_tensor(out=x[t][:, :], in0=x[t][:, :], scalar=ss[:, t:t + 1], in1=gain[:, :],
                                         op0=ALU.mult, op1=ALU.mult).then_inc(done, 1)

        @block.tensor
        def _(pe):
            for n in range(4 * (TT - 1)):
                t = n // 4
                pe.wait_ge(joined, n % 4 // 2 + 1)
                if n >= 4:
                    pe.wait_ge(added, n + 1)
                for j in range(4):
                    dt = 4 * (n % 4) + j
                    at = dt % 2 * SAMPLE + t * P
                    last = pe.transpose(k.banks[n % 4][:, j * P:(j + 1) * P], parts[:, 0, dt // 2, at:at + P],
                                        k.cst[:, C_ID:C_ID + P])
                last.then_inc(turned, 1)

        @block.scalar
        def _(act):
            for c in range(2):
                for half in range(2):
                    act.dma_start(parts[:, half, 4 * c:4 * c + 4],
                                  k.sums_dram[half, 4 * c:4 * c + 4].rearrange("b p n -> p b n")
                                  ).then_inc(parts_in[c], 16)
            for t in range(TT):
                act.wait_ge(added, 4 * (t + 1))
                act.activation(junk[:, :], x[t][:, :], ACT.Square, accum_out=ss[:, t:t + 1]).then_inc(squared, 1)
                act.wait_ge(squared, t + 1)
            act.wait_ge(rms, 1)
            act.activation(ss[:, :], ss[:, :], ACT.Sqrt).then_inc(root, 1)


_INS = ['x_prompt', 'x_sample', 'c', 'state_gla', 'state_mlstm_C', 'state_mlstm_n', 'state_mlstm_m', 'c_ctx',
        'mod_w', 'mod_b', 'norm1_g', 'norm2_g', 'final_g', 'w_in', 'b_in', 'hy_conv', 'hy_w1', 'hy_b1', 'hy_w2',
        'hy_b2', 'hy_w3', 'hy_freq', 'hy_bias', 'gla_a2_w', 'gla_a2_b', 'gla_norm_g', 'ml_conv', 'ml_gate_b',
        'ml_norm_g', 'w_branch', 'w_out', 'peer_wq', 'peer_keys', 'peer_u', 'peer_v']
_OUTS = {'y_prompt': (1, 128, 2048), 'y_sample': (1, 256, 2048), 'new_state_gla': (1, 1, 2, 4, 128, 256),
         'new_state_mlstm_C': (1, 1, 2, 4, 256, 256), 'new_state_mlstm_n': (1, 1, 2, 4, 256),
         'new_state_mlstm_m': (1, 1, 2, 4)}


def kernel(**inputs):
    import concourse.bacc as _bacc
    from concourse.bass_utils import run_bass_kernel_spmd as _run

    nc = _bacc.Bacc("TRN2", target_bir_lowering=False, num_devices=1)
    arrays, io = {}, {}
    for name, a in [(n, np.ascontiguousarray(inputs[n])) for n in _INS] + list(shape_constants().items()):
        arrays["in_" + name] = a
        io[name] = nc.dram_tensor("in_" + name, a.shape, mybir.dt.from_np(a.dtype), kind="ExternalInput").ap()
    for name, shape in _OUTS.items():
        io[name] = nc.dram_tensor("out_" + name, shape, F32, kind="ExternalOutput").ap()
    build(nc, io)
    r = _run(nc, [arrays], core_ids=[0])
    return tuple(r.results[0]["out_" + name] for name in _OUTS)
```
